# Optimizing a Trainium2 kernel written in Bass

```python
import math
import jax, jax.numpy as jnp
from jax import lax
import numpy as np

D_MODEL = 2048
BATCH = 1
SEQ = 256
DEPTH = 1

CHUNK = 64
Q_BLOCK = 128
D_MIX = D_MODEL
A_HEADS = 8
A_DK = 64
A_DV = 2 * A_DK
A_WIDTH = A_HEADS * A_DV
B_HEADS = 4
B_WIDTH = D_MIX - A_WIDTH
B_DV = B_WIDTH // B_HEADS
B_DK = B_DV // 2
GATE_RANK = 16
GATE_TAU = 16.0
N_BUCKETS = 32
MAX_DISTANCE = 256
N_GROUPS = 4
EXPERTS_PER_GROUP = 8
N_EXPERTS = N_GROUPS * EXPERTS_PER_GROUP
TOP_K = 2
D_EXPERT = D_MODEL // 4
MOE_BLOCK = 128
EPS = 1e-6
NEG_INF = -1e30
SZ_QA = A_HEADS * 2 * A_DK
SZ_KA = A_HEADS * 2 * A_DK
SZ_VA = A_WIDTH
SZ_QB = B_HEADS * B_DK
SZ_KB = B_HEADS * B_DK
SZ_VB = B_WIDTH
SZ_RB = B_WIDTH
SZ_ZB = GATE_RANK
D_IN = SZ_QA + SZ_KA + SZ_VA + SZ_QB + SZ_KB + SZ_VB + SZ_RB + SZ_ZB
IN_SPLITS = (SZ_QA,
             SZ_QA + SZ_KA,
             SZ_QA + SZ_KA + SZ_VA,
             SZ_QA + SZ_KA + SZ_VA + SZ_QB,
             SZ_QA + SZ_KA + SZ_VA + SZ_QB + SZ_KB,
             SZ_QA + SZ_KA + SZ_VA + SZ_QB + SZ_KB + SZ_VB,
             SZ_QA + SZ_KA + SZ_VA + SZ_QB + SZ_KB + SZ_VB + SZ_RB)

kernel_name = "hybrid_diffattn_gla_hmoe_block"

def rms_norm(x, g):
    xf = x.astype(jnp.float32)
    y = xf * lax.rsqrt(jnp.mean(xf * xf, axis=-1, keepdims=True) + EPS)
    return (y * g.astype(jnp.float32)).astype(x.dtype)

def t5_bucket(rel):
    nb = N_BUCKETS // 2
    max_exact = nb // 2
    base = jnp.where(rel > 0, nb, 0)
    n = jnp.abs(rel)
    nf = jnp.maximum(n, 1).astype(jnp.float32)
    large = max_exact + (jnp.log(nf / max_exact) / math.log(MAX_DISTANCE / max_exact)
                         * (nb - max_exact)).astype(jnp.int32)
    large = jnp.minimum(large, nb - 1)
    return base + jnp.where(n < max_exact, n, large)

def diff_attention(q, k, v, rel_bias, lam, sub_gain, lam_init):
    Bn, S = q.shape[0], q.shape[1]
    nblk = S // Q_BLOCK
    qb = (q * (A_DK ** -0.5)).reshape(Bn, nblk, Q_BLOCK, A_HEADS, 2, A_DK)
    qb = qb.transpose(1, 0, 3, 4, 2, 5)
    kt = k.transpose(0, 2, 3, 1, 4)
    vt = v.transpose(0, 2, 1, 3)
    kpos = jnp.arange(S)

    def block(args):
        blk, qblk = args
        qpos = blk * Q_BLOCK + jnp.arange(Q_BLOCK)
        rel = kpos[None, :] - qpos[:, None]
        bias = rel_bias[t5_bucket(rel)].transpose(2, 0, 1)
        allowed = (kpos[None, :] // CHUNK) <= (qpos[:, None] // CHUNK)
        s = jnp.einsum('bhmqd,bhmkd->bhmqk', qblk, kt).astype(jnp.float32)
        s = s + bias[None, :, None].astype(jnp.float32)
        s = jnp.where(allowed, s, NEG_INF)
        p = jax.nn.softmax(s, axis=-1)
        pd = p[:, :, 0] - lam * p[:, :, 1]
        return jnp.einsum('bhqk,bhkd->bhqd', pd.astype(v.dtype), vt)

    o = lax.map(block, (jnp.arange(nblk), qb))
    o = o.transpose(1, 0, 3, 2, 4).reshape(Bn, S, A_HEADS, A_DV)
    o = rms_norm(o, sub_gain) * (1.0 - lam_init)
    return o.reshape(Bn, S, A_WIDTH)

def gla(q, k, v, log_a):
    Bn, S = q.shape[0], q.shape[1]
    nc = S // CHUNK

    def to_chunks(t):
        return t.reshape(Bn, nc, CHUNK, B_HEADS, t.shape[-1]).transpose(1, 0, 3, 2, 4).astype(jnp.float32)

    qc = to_chunks(q * (B_DK ** -0.5))
    kc = to_chunks(k)
    vc = to_chunks(v)
    ac = to_chunks(log_a)

    def step(state, inp):
        qn, kn, vn, an = inp
        cum = jnp.cumsum(an, axis=2)
        total = cum[:, :, -1:]
        k_dec = kn * jnp.exp(total - cum)
        state = jnp.exp(total[:, :, 0])[..., None] * state + jnp.einsum('bhcd,bhce->bhde', k_dec, vn)
        return state, jnp.einsum('bhcd,bhde->bhce', qn, state)

    s0 = jnp.zeros((Bn, B_HEADS, B_DK, B_DV), jnp.float32)
    _, o = lax.scan(step, s0, (qc, kc, vc, ac))
    return o.transpose(1, 0, 3, 2, 4).reshape(Bn, S, B_HEADS, B_DV).astype(v.dtype)

def token_mixer(h, rel_bias, w_in, w_alpha, b_alpha, lam_q1, lam_k1, lam_q2, lam_k2,
                g_sub_a, g_norm_b, w_out, lam_init):
    Bn, S = h.shape[0], h.shape[1]
    proj = h @ w_in
    qa, ka, va, qb, kb, vb, rb, zb = jnp.split(proj, IN_SPLITS, axis=-1)
    lam = (jnp.exp(jnp.dot(lam_q1.astype(jnp.float32), lam_k1.astype(jnp.float32)))
           - jnp.exp(jnp.dot(lam_q2.astype(jnp.float32), lam_k2.astype(jnp.float32))) + lam_init)
    oa = diff_attention(qa.reshape(Bn, S, A_HEADS, 2, A_DK),
                        ka.reshape(Bn, S, A_HEADS, 2, A_DK),
                        va.reshape(Bn, S, A_HEADS, A_DV),
                        rel_bias, lam, g_sub_a, lam_init)
    log_a = jax.nn.log_sigmoid((zb @ w_alpha + b_alpha).astype(jnp.float32)) / GATE_TAU
    ob = gla(qb.reshape(Bn, S, B_HEADS, B_DK),
             kb.reshape(Bn, S, B_HEADS, B_DK),
             vb.reshape(Bn, S, B_HEADS, B_DV),
             log_a.reshape(Bn, S, B_HEADS, B_DK))
    ob = rms_norm(ob, g_norm_b).reshape(Bn, S, B_WIDTH) * jax.nn.silu(rb)
    return jnp.concatenate([oa, ob], axis=-1) @ w_out

def hier_moe(h, w_rg, b_rg, w_re, b_re, w1, w3, w2):
    Bn, S, D = h.shape
    g_prob = jax.nn.softmax((h @ w_rg + b_rg).astype(jnp.float32), axis=-1)
    g_val, g_idx = lax.top_k(g_prob, 1)
    e_logit = (h @ w_re + b_re).astype(jnp.float32).reshape(Bn, S, N_GROUPS, EXPERTS_PER_GROUP)
    sel = jax.nn.one_hot(g_idx[..., 0], N_GROUPS, dtype=jnp.float32)
    e_logit = jnp.einsum('bsg,bsge->bse', sel, e_logit)
    e_prob = jax.nn.softmax(e_logit, axis=-1)
    e_val, e_idx = lax.top_k(e_prob, TOP_K)
    e_val = e_val / jnp.sum(e_val, axis=-1, keepdims=True)
    weights = g_val * e_val
    expert_id = g_idx * EXPERTS_PER_GROUP + e_idx
    combine = jnp.sum(jax.nn.one_hot(expert_id, N_EXPERTS, dtype=jnp.float32) * weights[..., None], axis=2)

    nblk = S // MOE_BLOCK
    tb = h.reshape(Bn, nblk, MOE_BLOCK, D).transpose(1, 0, 2, 3).reshape(nblk, Bn * MOE_BLOCK, D)
    cb = combine.reshape(Bn, nblk, MOE_BLOCK, N_EXPERTS).transpose(1, 0, 2, 3).reshape(nblk, Bn * MOE_BLOCK, N_EXPERTS)

    def block(args):
        t, cw = args
        a = jnp.einsum('td,edf->tef', t, w1)
        b = jnp.einsum('td,edf->tef', t, w3)
        hid = jax.nn.silu(a) * b * cw[:, :, None].astype(t.dtype)
        return jnp.einsum('tef,efd->td', hid, w2)

    y = lax.map(block, (tb, cb))
    return y.reshape(nblk, Bn, MOE_BLOCK, D).transpose(1, 0, 2, 3).reshape(Bn, S, D)

def setup_inputs(seed: int = 0) -> dict:
    key = jax.random.key(seed)
    ks = jax.random.split(key, 26)
    f32 = jnp.float32
    nrm = lambda k, shape, s: jax.random.normal(k, shape, f32) * s
    gain = lambda k, shape: 1.0 + 0.05 * jax.random.normal(k, shape, f32)
    D, L = D_MODEL, DEPTH
    return {
        "x": nrm(ks[0], (BATCH, SEQ, D), 1.0),
        "c": nrm(ks[1], (BATCH, D), 1.0),
        "rel_bias": nrm(ks[2], (N_BUCKETS, A_HEADS), 0.5),
        "w_ada": nrm(ks[3], (L, D, 6 * D), 0.5 * D ** -0.5),
        "b_ada": nrm(ks[4], (L, 6 * D), 0.02),
        "g_pre_mix": gain(ks[5], (L, D)),
        "g_post_mix": gain(ks[6], (L, D)),
        "w_in": nrm(ks[7], (L, D, D_IN), D ** -0.5),
        "w_alpha": nrm(ks[8], (L, GATE_RANK, B_HEADS * B_DK), GATE_RANK ** -0.5),
        "b_alpha": nrm(ks[9], (L, B_HEADS * B_DK), 0.1),
        "lam_q1": nrm(ks[10], (L, A_DK), 0.1),
        "lam_k1": nrm(ks[11], (L, A_DK), 0.1),
        "lam_q2": nrm(ks[12], (L, A_DK), 0.1),
        "lam_k2": nrm(ks[13], (L, A_DK), 0.1),
        "g_sub_a": gain(ks[14], (L, A_DV)),
        "g_norm_b": gain(ks[15], (L, B_DV)),
        "w_out": nrm(ks[16], (L, D_MIX, D), D_MIX ** -0.5),
        "g_pre_ffn": gain(ks[17], (L, D)),
        "g_post_ffn": gain(ks[18], (L, D)),
        "w_router_g": nrm(ks[19], (L, D, N_GROUPS), D ** -0.5),
        "b_router_g": nrm(ks[20], (L, N_GROUPS), 0.01),
        "w_router_e": nrm(ks[21], (L, D, N_EXPERTS), D ** -0.5),
        "b_router_e": nrm(ks[22], (L, N_EXPERTS), 0.01),
        "w1": nrm(ks[23], (L, N_EXPERTS, D, D_EXPERT), D ** -0.5),
        "w3": nrm(ks[24], (L, N_EXPERTS, D, D_EXPERT), D ** -0.5),
        "w2": nrm(ks[25], (L, N_EXPERTS, D_EXPERT, D), D_EXPERT ** -0.5),
    }

def reference(x, c, rel_bias, w_ada, b_ada, g_pre_mix, g_post_mix, w_in, w_alpha, b_alpha,
              lam_q1, lam_k1, lam_q2, lam_k2, g_sub_a, g_norm_b, w_out, g_pre_ffn, g_post_ffn,
              w_router_g, b_router_g, w_router_e, b_router_e, w1, w3, w2):
    for i in range(DEPTH):
        lam_init = 0.8 - 0.6 * math.exp(-0.3 * i)
        ada = jax.nn.silu(c) @ w_ada[i] + b_ada[i]
        sh_m, sc_m, gt_m, sh_f, sc_f, gt_f = [a[:, None, :] for a in jnp.split(ada, 6, axis=-1)]
        h = rms_norm(x, g_pre_mix[i]) * (1 + sc_m) + sh_m
        y = token_mixer(h, rel_bias, w_in[i], w_alpha[i], b_alpha[i], lam_q1[i], lam_k1[i],
                        lam_q2[i], lam_k2[i], g_sub_a[i], g_norm_b[i], w_out[i], lam_init)
        x = x + gt_m * rms_norm(y, g_post_mix[i])
        h = rms_norm(x, g_pre_ffn[i]) * (1 + sc_f) + sh_f
        y = hier_moe(h, w_router_g[i], b_router_g[i], w_router_e[i], b_router_e[i], w1[i], w3[i], w2[i])
        x = x + gt_f * rms_norm(y, g_post_ffn[i])
    return x


_drawn_inputs = setup_inputs


def setup_inputs(seed=0):
    import zlib

    import numpy as np

    out = dict(_drawn_inputs(seed))
    spreads = {}
    factors = {'lam_q1': 4.51, 'g_post_ffn': 3.868, 'b_router_g': 8.0, 'b_router_e': 3.975}
    for name, (base, spread) in spreads.items():
        noise = np.random.default_rng([zlib.crc32(name.encode()), seed]).standard_normal(out[name].shape)
        drawn = base * np.exp(spread * noise) if base else spread * noise
        out[name] = __import__('jax').numpy.asarray(drawn.astype(out[name].dtype))
    for name, factor in factors.items():
        out[name] = (out[name] * factor).astype(out[name].dtype)
    return out
```

```python
import math
from contextlib import ExitStack

import numpy as np
import concourse.bass as bass
from concourse import mybir

D = 2048
S = 256
P = 128
TT = S // P
KD = D // P
CHUNK = 64
A_HEADS, A_DK, A_DV = 8, 64, 128
B_HEADS, B_DK, B_DV = 4, 128, 256
GATE_RANK, GATE_TAU = 16, 16.0
N_BUCKETS, MAX_DISTANCE = 32, 256
N_GROUPS, PER_GROUP = 4, 8
NE = N_GROUPS * PER_GROUP
F = D // 4
D_IN = 3 * 1024 + 2 * 512 + 2 * 1024 + GATE_RANK
EPS = 1e-6
LAM_INIT = 0.8 - 0.6 * math.exp(-0.3 * 0)
NEG = -1e30
ROWS = 32
MAX_TILES = NE + (2 * S - NE) // ROWS + 1
UNIT = 8192
REL = 2 * S - 1
SKEW = 384

C_ID, C_LT, C_SUF, C_ONE, C_IOTA, C_THR, C_TOK, C_NH, C_HALF, C_BKT = 0, 128, 256, 384, 512, 544, 552, 554, 558, 560
C_KEEP = C_BKT
C_ALL = C_BKT + 512

ORDER = [0, 2, 4, 1, 3, 5, 7, 6, 8, 9, 10, 11]
TRANSPOSED = {0, 1, 2, 3, 6}
ATT = 2 * A_HEADS
HEADS_READY = [6, 12]
MODS = [0, 1, 2, 3, 4, 5]


def head_block(i):
    g = i // 4
    return 4 * (g // 2) + i % 4, g % 2


def t5_bucket(rel):
    nb = N_BUCKETS // 2
    exact = nb // 2
    n = np.abs(rel)
    nf = np.maximum(n, 1).astype(np.float32)
    large = exact + (np.log(nf / exact) / math.log(MAX_DISTANCE / exact) * (nb - exact)).astype(np.int32)
    return np.where(rel > 0, nb, 0) + np.where(n < exact, n, np.minimum(large, nb - 1))


def shape_constants():
    c = np.zeros((P, C_ALL), np.float32)
    p = np.arange(P)
    c[:, C_ID:C_ID + P] = np.eye(P)
    c[:, C_LT:C_LT + P] = p[:, None] < p[None, :]
    c[:, C_SUF:C_SUF + P] = (p[:, None] > p[None, :]) & (p[:, None] // CHUNK == p[None, :] // CHUNK)
    c[:, C_ONE:C_ONE + P] = 1.0
    c[:, C_IOTA:C_IOTA + NE] = np.arange(NE)
    c[:, C_THR:C_THR + 8] = ROWS * np.arange(8)
    c[:, C_TOK:C_TOK + TT] = p[:, None] + P * np.arange(TT)
    c[:, C_NH:C_NH + 4] = -0.5
    c[:, C_HALF] = p < CHUNK
    c[:, C_HALF + 1] = p >= CHUNK
    rel = np.arange(REL) - (S - 1)
    c[0:N_BUCKETS, C_BKT:C_BKT + REL] = t5_bucket(rel)[None, :] == np.arange(N_BUCKETS)[:, None]
    return c


def schedule():
    out = []
    for m in (0, 1):
        out += [("ada", m, q) for q in range(4)] + [("mod", m)]
    out += [("modulate",), ("alpha",)]
    ada = [(m, q) for m in (2, 3, 4) for q in range(4)]
    slot = 0
    for i in range(12):
        out += [("ada",) + ada[i]]
        for half in range(2):
            out.append(("proj", i, half))
            if i >= 3:
                out.append(("att", slot))
                slot += 1
        if i == 6:
            out.append(("kdec",))
        if i % 4 == 3:
            out.append(("mod", ada[i][0]))
    while slot < ATT + 3:
        out.append(("att", slot))
        slot += 1
    out += [("gla", n) for n in range(4)] + [("glanorm", 0), ("glanorm", 1)]
    for u in range(4):
        out += [("wout", u), ("ada", 5, u)]
    out.append(("mod", 5))
    return out


def build(nc, a, out):
    f32, i32, u32 = mybir.dt.float32, mybir.dt.int32, mybir.dt.uint32
    ALU, ACT, AX = mybir.AluOpType, mybir.ActivationFunctionType, mybir.AxisListType
    SCHED = schedule()
    STREAM = [s for s in SCHED if s[0] in ("ada", "wout") or (s[0] == "proj" and s[2] == 0)]
    SLOT = {s[:3]: (n % 3, n // 3) for n, s in enumerate(STREAM)}

    ctx = ExitStack()
    with ctx:
        def sb(name, shape, dt=f32):
            return ctx.enter_context(nc.sbuf_tensor(name, shape, dt))

        def sem(name):
            return ctx.enter_context(nc.semaphore(name))

        def dram(name, shape, dt=f32):
            return nc.dram_tensor(name, shape, dt, kind="Internal")

        stream = sb("stream", [P, 5, UNIT])
        resid = sb("resid", [P, TT, D])
        acc = sb("acc", [P, D])
        wk = sb("wk", [P, 4096])
        cst = sb("cst", [P, C_KEEP])
        wr = sb("wr", [P, KD, N_GROUPS + NE])
        br = sb("br", [P, N_GROUPS + NE])
        cc = sb("cc", [P, 3, KD])
        gains = sb("gains", [P, 4, KD])
        bada = sb("bada", [P, 6, KD])
        mod = sb("mod", [P, 6, KD])
        gsub = sb("gsub", [P, 1])
        gnb = sb("gnb", [P, 2])
        lamv = sb("lamv", [P, 8])
        st = sb("st", [P, 96])
        cums = sb("cums", [1, NE + 1], i32)
        rel = sb("rel", [P, TT, 2])
        gates = sb("gates", [P, TT, 2])
        slots = sb("slots", [P, 2 * TT], u32)

        ident = cst[:, C_ID:C_ID + P]
        ones = cst[:, C_ONE:C_ONE + P]

        def view(t, lo, n, c):
            return t[:, lo:lo + n * c].rearrange("p (n c) -> p n c", n=n)
        s3, s4 = stream[:, 3, :], stream[:, 4, :]
        va, vb, rb = view(s3, 0, TT, 1024), view(s3, 2048, TT, 1024), view(s3, 4096, TT, 1024)
        kb, qbT = view(s3, 6144, TT, 512), view(s3, 7168, B_HEADS, S)
        y, h2T = view(s3, 0, TT, D), view(s3, 4096, KD, S)
        hT, qaT, kaT = view(s4, 0, KD, S), view(s4, 4096, A_HEADS, S), view(s4, 6144, A_HEADS, S)
        oTa, oTb = qaT, view(s4, 0, 8, S)
        junk1 = s4[:, 4096:4096 + D]
        gl = resid[:, :, :].rearrange("p t d -> p (t d)")
        kdec, state = view(gl, 0, TT, 512), view(gl, 1024, B_HEADS, B_DV)
        la, tmp = view(gl, 2048, TT, 512), gl[:, 3072:4096]
        bias = view(wk, 0, A_HEADS, S)
        sc, pr = view(wk, 2048, 2, S), view(wk, 2560, 2, S)
        pd, pdT, on = wk[:, 3072:3328], wk[:, 3328:3584], view(wk, 3584, 4, A_DV)
        walpha, balpha, bkt = wk[0:GATE_RANK, 2048:2560], wk[:, 2560:3072], wk[0:N_BUCKETS, 3072:3584]
        zbT = wk[0:GATE_RANK, 3072:3328]
        wzb = view(s3, 7168, KD, GATE_RANK)
        relb, relrow, lamw = wk[0:N_BUCKETS, 3584:3592], wk[0:A_HEADS, 3600:3984], wk[:, 0:256]
        g1b = wk[:, 0:D]
        xe = view(wk, 2048, KD, ROWS)
        ab, eh, hid, ye = wk[:, 2560:2816], view(wk, 2816, 2, 64), view(wk, 2944, 2, 64), wk[:, 3072:3584]
        xp = wk[:, 3584:4096]
        wrf = wr[:, :, :].rearrange("p k n -> p (k n)")
        hit, pick = view(wrf, 0, 2 * TT, ROWS), view(wrf, 256, TT, ROWS)
        x1r, g2b = view(stream[:, 2, :], 0, TT, D), stream[:, 2, 2 * D:3 * D]
        normed = resid[:, :, :].rearrange("p t (k q) -> p t k q", k=KD)
        RSHAPES = dict(L=(TT, 36), g8=(TT, 8), gm=(TT, 8), gi=(TT, 8), ng=(TT, 1), gf=(TT, 1), sel=(TT, 4), eg=(TT, 4, 8), es=(TT, 8),
                       em=(TT, 8), ei=(TT, 8), d2=(TT, 1), ef=(TT, 2), ex=(TT, 2), oh=(TT, 2, NE), M=(TT, NE), w=(TT, 2), e2=(TT, 1),
                       gs=(TT, 1), ge=(TT, 4), cnt=(NE,), cmp=(NE, 8), nt=(NE,), zero=(NE,), cum=(NE,), base=(NE,), pos=(TT, NE))

        def R(name):
            lo = sum(int(np.prod(v)) for k, v in RSHAPES.items() if list(RSHAPES).index(k) < list(RSHAPES).index(name))
            shape = RSHAPES[name]
            v = wk[:, D + lo:D + lo + int(np.prod(shape))]
            if name in ("gi", "ei"):
                v = v.bitcast(u32)
            if len(shape) == 2:
                v = v.rearrange("p (a b) -> p a b", a=shape[0])
            if len(shape) == 3:
                v = v.rearrange("p (a b c) -> p a b c", a=shape[0], b=shape[1])
            return v

        def fin_rows(j):
            return stream[:, 0, D * j:D * j + D]

        ps = ctx.enter_context(nc.psum_tensor("ps", [P, 8, 512], f32))

        def bank(b, *dims):
            if not dims:
                return ps[:, b, :]
            return ps[:, b, 0:dims[0] * dims[1]].rearrange("p (n c) -> p n c", n=dims[0])

        skew = dram("skew", [A_HEADS, P, SKEW])
        gdram = dram("gdram", [2, P, KD])
        x1d = dram("x1d", [P, TT, D])
        ys = dram("ys", [MAX_TILES * ROWS, D])

        c_in, const_in, x_in, par_in, late_in = sem("c_in"), sem("const_in"), sem("x_in"), sem("par_in"), sem("late_in")
        bias_in, skew_out = sem("bias_in"), sem("skew_out")
        unit_in = [sem(f"unit_in{i}") for i in range(3)]
        ada_done = sem("ada_done")
        act_c, dve_c, pool_c = sem("act_chain"), sem("dve_chain"), sem("pool_chain")
        relrow_ps, relrow_sb, masked = sem("relrow_ps"), sem("relrow_sb"), sem("masked")
        c_exp = sem("c_exp")
        xsq, xr, xn = sem("xsq"), sem("xr"), sem("xn")
        xT_ps, xT_sb = sem("xT_ps"), sem("xT_sb")
        mod_ps, mod_sb = sem("mod_ps"), sem("mod_sb")
        hT_ready = sem("hT_ready")
        zb_ps, zb_sb, z_ps, z_abs, z_ln, la_sb = sem("zb_ps"), sem("zb_sb"), sem("z_ps"), sem("z_abs"), sem("z_ln"), sem("la_sb")
        suf_ps, suf_exp, kdec_sb = sem("suf_ps"), sem("suf_exp"), sem("kdec_sb")
        proj_ps, proj_sb = sem("proj_ps"), sem("proj_sb")
        s_ps, s_sb, p_max, p_exp, pd_sb = sem("s_ps"), sem("s_sb"), sem("p_max"), sem("p_exp"), sem("pd_sb")
        pdT_ps, pdT_sb, o_ps, o_sq, o_rs, o_sb = sem("pdT_ps"), sem("pdT_sb"), sem("o_ps"), sem("o_sq"), sem("o_rs"), sem("o_sb")
        oT_ps, oT_sb = sem("oT_ps"), sem("oT_sb")
        lam_sum, lam_exp = sem("lam_sum"), sem("lam_exp")
        kv_ps, state_sb, gla_ps = sem("kv_ps"), sem("state_sb"), sem("gla_ps")
        rb_exp, rb_sb, gla_sq, gla_rs, gla_sb = sem("rb_exp"), sem("rb_sb"), sem("gla_sq"), sem("gla_rs"), sem("gla_sb")
        glaT_ps, glaT_sb = sem("glaT_ps"), sem("glaT_sb")
        g_sb, g1_out, g2_out, g1_in, g2_in, xre_in = sem("g_sb"), sem("g1_out"), sem("g2_out"), sem("g1_in"), sem("g2_in"), sem("xre_in")
        y_tot, y_sum, y_rs, x1_sb, x1_sq, x1_rs, h2_sb, x1_out = sem("y_tot"), sem("y_sum"), sem("y_rs"), sem("x1_sb"), sem("x1_sq"), sem("x1_rs"), sem("h2_sb"), sem("x1_out")
        h2T_ps, h2T_dve, h2T_act = sem("h2T_ps"), sem("h2T_dve"), sem("h2T_act")
        pick_sb, pick_c, rows_ps, rows_sb, ys_zero, ye_out, h2_kept = (
            sem("pick_sb"), sem("pick_c"), sem("rows_ps"), sem("rows_sb"), sem("ys_zero"), sem("ye_out"), sem("h2_kept"))
        log_ps, g_max, r_exp1, e_max, r_exp2, m_sb, rank_ps, route_sb = (
            sem("log_ps"), sem("g_max"), sem("r_exp1"), sem("e_max"), sem("r_exp2"), sem("m_sb"), sem("rank_ps"),
            sem("route_sb"))
        w1_in, w3_in, w2_in = [sem("w1_in0"), sem("w1_in1")], [sem("w3_in0"), sem("w3_in1")], sem("w2_in")
        xe_ps, xe_t, xe_sb, ab_ps, ab_sb, h_ps, h_exp, h_t, hid_sb, ye_ps, ye_sb = (
            sem("xe_ps"), sem("xe_t"), sem("xe_sb"), sem("ab_ps"), sem("ab_sb"), sem("h_ps"), sem("h_exp"), sem("h_t"),
            sem("hid_sb"), sem("ye_ps"), sem("ye_sb"))
        fin_rows_in, fin_sum, fin_in, fin_sq, fin_rs, fin_sb, fin_out = (
            [sem("fin_rows_in0"), sem("fin_rows_in1")], sem("fin_sum"), sem("fin_in"), sem("fin_sq"), sem("fin_rs"), sem("fin_sb"), sem("fin_out"))

        w_ada = a["w_ada"].rearrange("l (p k) (m n) -> (l p) k m n", p=P, m=6)
        w_in = a["w_in"].rearrange("l (p k) n -> (l p) k n", p=P)
        w_out = a["w_out"].rearrange("l (k p) n -> (l p) k n", p=P)
        w1 = a["w1"].rearrange("l e (p k) f -> (l e) p (k f)", p=P)
        w3 = a["w3"].rearrange("l e (p k) f -> (l e) p (k f)", p=P)
        w2 = a["w2"].rearrange("l e (k p) n -> (l e) p k n", p=P)
        x_d = a["x"].rearrange("b (t p) d -> (b p) t d", p=P)
        out_d = out.rearrange("b (t p) d -> (b p) t d", p=P)

        def row_bcast(ap, n):
            return bass.AP(tensor=ap.tensor, offset=ap.offset, ap=[[0, P], [1, n]])

        def DECAY(n, h):
            return 32 + 8 * (n // 2) + 2 * h + n % 2

        def vec(ap):
            return ap.rearrange("l (p k) -> (l p) k", p=P)

        params = [
            (relb, a["rel_bias"][:, :]),
            (lamw[:, 0:64], row_bcast(a["lam_q1"], 64)), (lamw[:, 64:128], row_bcast(a["lam_k1"], 64)),
            (lamw[:, 128:192], row_bcast(a["lam_q2"], 64)), (lamw[:, 192:256], row_bcast(a["lam_k2"], 64)),
            (gsub[:, :], a["g_sub_a"].rearrange("l (p o) -> (l p) o", o=1)),
            (bada[:, :, :], a["b_ada"].rearrange("l (m p k) -> (l p) m k", m=6, p=P)),
            (gains[:, 0, :], vec(a["g_pre_mix"])), (gains[:, 1, :], vec(a["g_post_mix"])),
            (gains[:, 2, :], vec(a["g_pre_ffn"])), (gains[:, 3, :], vec(a["g_post_ffn"])),
            (wzb[:, :, :], w_in[:, :, D_IN - GATE_RANK:D_IN]),
            (gnb[:, 0:1], a["g_norm_b"][:, 0:P].rearrange("l (p o) -> (l p) o", o=1)),
            (gnb[:, 1:2], a["g_norm_b"][:, P:2 * P].rearrange("l (p o) -> (l p) o", o=1)),
            (wr[:, :, 0:N_GROUPS], a["w_router_g"].rearrange("l (p k) n -> (l p) k n", p=P)),
            (wr[:, :, N_GROUPS:N_GROUPS + NE], a["w_router_e"].rearrange("l (p k) n -> (l p) k n", p=P)),
            (br[:, 0:N_GROUPS], row_bcast(a["b_router_g"], N_GROUPS)), (br[:, N_GROUPS:N_GROUPS + NE], row_bcast(a["b_router_e"], NE)),
        ]

        W1 = [stream[:, 0, :], stream[:, 1, :]]
        W3 = [stream[:, 2, :], stream[:, 3, :]]
        W2 = stream[:, 4, :]

        def w_unit(e, t):
            return t[bass.ds(e, 1)].rearrange("e p n -> (e p) n")

        block = ctx.enter_context(nc.Block())

        @block.sync
        def _(sp):
            def wait_used(item):
                if item[0] == "ada":
                    sp.wait_ge(ada_done, 4 * MODS.index(item[1]) + item[2] + 1)
                elif item[0] == "proj":
                    sp.wait_ge(proj_ps, 2 * item[1] + 2)
                else:
                    sp.wait_ge(proj_ps, 24 + 2 * item[1] + 2)

            for n, item in enumerate(STREAM):
                s = n % 3
                if n >= 3:
                    wait_used(STREAM[n - 3])
                dst = stream[:, s, :]
                if item[0] == "ada":
                    _, m, q = item
                    sp.dma_start(dst.rearrange("p (k n) -> p k n", k=4), w_ada[:, 4 * q:4 * q + 4, m, :]).then_inc(unit_in[s], 16)
                elif item[0] == "proj":
                    c = ORDER[item[1]]
                    sp.dma_start(dst.rearrange("p (k n) -> p k n", k=KD), w_in[:, :, 512 * c:512 * c + 512]).then_inc(unit_in[s], 16)
                else:
                    u = item[1]
                    sp.dma_start(dst.rearrange("p (k n) -> p k n", k=KD), w_out[:, :, 512 * u:512 * u + 512]).then_inc(unit_in[s], 16)
            for n in range(len(STREAM) - 3, len(STREAM)):
                wait_used(STREAM[n])
                if n % 3 == 0:
                    sp.dma_start(W1[0], w1[0]).then_inc(w1_in[0], 16)
                elif n % 3 == 1:
                    sp.dma_start(W1[1], w1[1]).then_inc(w1_in[1], 16)
                else:
                    sp.dma_start(W3[0], w3[0]).then_inc(w3_in[0], 16)
            sp.wait_ge(proj_ps, 24 + 8)
            sp.dma_start(W2.rearrange("p (k n) -> p k n", k=4), w2[0]).then_inc(w2_in, 16)
            sp.wait_ge(log_ps, 1)
            sp.wait_ge(h2_kept, TT)
            sp.dma_start(W3[1], w3[1]).then_inc(w3_in[1], 16)
            sp.wait_ge(route_sb, 1)
            done = sp.value_load(cums[0:1, 1:2], min_val=1, max_val=MAX_TILES)
            sp.wait_ge(ye_ps, done)
            sp.dma_start(W2.rearrange("p (k n) -> p k n", k=4), w2[1]).then_inc(w2_in, 16)
            with sp.Fori(1, NE // 2) as i:
                for b in range(2):
                    e = 2 * i + b
                    done = sp.value_load(cums[0:1, bass.ds(e - 1, 1)], min_val=1, max_val=MAX_TILES)
                    sp.wait_ge(ye_ps, done)
                    sp.dma_start(W1[b], w_unit(e, w1)).then_inc(w1_in[b], 16)
                    sp.dma_start(W3[b], w_unit(e, w3)).then_inc(w3_in[b], 16)
                    done = sp.value_load(cums[0:1, bass.ds(e, 1)], min_val=1, max_val=MAX_TILES)
                    sp.wait_ge(ye_ps, done)
                    sp.dma_start(W2.rearrange("p (k n) -> p k n", k=4),
                                 w2[bass.ds(e, 1)].rearrange("e p k n -> (e p) k n")).then_inc(w2_in, 16)
            done = sp.value_load(cums[0:1, NE - 1:NE], min_val=1, max_val=MAX_TILES)
            sp.wait_ge(ye_ps, done)
            sp.dma_start(x1r, x1d[:, :, :]).then_inc(fin_in, 16)
            sp.dma_start(g2b, row_bcast(gdram[1, :, :], D)).then_inc(fin_in, 16)

        @block.tensor
        def _(pe):
            pe.wait_ge(const_in, 32)
            pe.wait_ge(par_in, 16 * len(params))
            nc.tensor.matmul(bank(4)[0:A_HEADS, 0:384], relb, bkt[:, 0:384], start=True, stop=True).then_inc(relrow_ps, 1)
            for t in range(TT):
                pe.wait_ge(xn, t + 1)
                for j in range(4):
                    if t:
                        pe.wait_ge(xT_sb, j + 1)
                    for k in range(4):
                        last = nc.tensor.transpose(bank(j, 4, P)[:, k, :], resid[:, t, 4 * j + k::KD], ident)
                    last.then_inc(xT_ps, 1)

            fill = 0
            for item in SCHED:
                kind = item[0]
                if kind == "mod":
                    m = item[1]
                    pe.wait_ge(ada_done, 4 * (MODS.index(m) + 1))
                    for k in range(KD):
                        last = nc.tensor.matmul(bank(6)[:, 16 * m + k:16 * m + k + 1], acc[:, k::KD], ones[:, 0:1], start=True, stop=True)
                    last.then_inc(mod_ps, 1)
                elif kind == "alpha":
                    pe.wait_ge(hT_ready, 1)
                    for k in range(KD):
                        last = nc.tensor.matmul(bank(5)[0:GATE_RANK, 0:S], wzb[:, k, :], hT[:, k, :], start=(k == 0), stop=(k == KD - 1))
                    last.then_inc(zb_ps, 1)
                    pe.wait_ge(late_in, 32)
                    pe.wait_ge(zb_sb, 1)
                    for t in range(TT):
                        nc.tensor.matmul(bank(2 + t), zbT[:, P * t:P * t + P], walpha, start=True, stop=True).then_inc(z_ps, 1)
                    for t in range(TT):
                        pe.wait_ge(la_sb, t + 1)
                        nc.tensor.matmul(bank(4 + t), cst[:, C_SUF:C_SUF + P], la[:, t, :], start=True, stop=True).then_inc(suf_ps, 1)
                    for t in range(TT):
                        for h in range(B_HEADS):
                            last = nc.tensor.matmul(bank(7)[:, 8 * t + 2 * h:8 * t + 2 * h + 2], la[:, t, P * h:P * h + P],
                                                    cst[:, C_HALF:C_HALF + 2], start=True, stop=True)
                    last.then_inc(suf_ps, 1)
                elif kind == "proj":
                    _, i, half = item
                    c = ORDER[i]
                    s, n = SLOT[("proj", i, 0)]
                    w = stream[:, s, :].rearrange("p (k n) -> p k n", k=KD)
                    if half == 0:
                        pe.wait_ge(unit_in[s], 16 * (n + 1))
                    if fill >= 2:
                        pe.wait_ge(proj_sb, fill - 1)
                    dst = bank(fill % 2, 2, S)
                    if c in TRANSPOSED:
                        for j in range(2):
                            for k in range(KD):
                                lo = 256 * half + P * j
                                last = nc.tensor.matmul(dst[:, j, :], w[:, k, lo:lo + P], hT[:, k, :], start=(k == 0), stop=(k == KD - 1))
                    else:
                        for k in range(KD):
                            last = nc.tensor.matmul(bank(fill % 2), hT[:, k, P * half:P * half + P], w[:, k, :], start=(k == 0), stop=(k == KD - 1))
                    last.then_inc(proj_ps, 1)
                    fill += 1
                elif kind == "att":
                    i = item[1]
                    if i < ATT:
                        h, b = head_block(i)
                        nk = P * (b + 1)
                        if i == 0:
                            pe.wait_ge(suf_exp, 3)
                        else:
                            pe.wait_ge(s_sb, i)
                        pe.wait_ge(proj_sb, HEADS_READY[h // 4])
                        for m in range(2):
                            r = slice(A_DK * m, A_DK * m + A_DK)
                            last = nc.tensor.matmul(ps[:, 2 + m, 0:nk], qaT[r, h, P * b:P * b + P], kaT[r, h, 0:nk], start=True, stop=True)
                        last.then_inc(s_ps, 1)
                    if 2 <= i < ATT + 2:
                        j = i - 2
                        h, b = head_block(j)
                        pe.wait_ge(pdT_sb, j + 1)
                        if j >= 4 and j % 4 == 0:
                            pe.wait_ge(o_sb, j // 4)
                        for kt in range(b + 1):
                            last = nc.tensor.matmul(bank(4, 4, A_DV)[:, j % 4, :], pdT[:, P * kt:P * kt + P], va[:, kt, A_DV * h:A_DV * h + A_DV],
                                                    start=(kt == 0), stop=(kt == b))
                        last.then_inc(o_ps, 1)
                    if 1 <= i < ATT + 1:
                        j = i - 1
                        _, b = head_block(j)
                        pe.wait_ge(pd_sb, j + 1)
                        for kt in range(b + 1):
                            last = nc.tensor.transpose(bank(7)[:, P * kt:P * kt + P], pd[:, P * kt:P * kt + P], ident)
                        last.then_inc(pdT_ps, 1)
                    if i % 4 == 2 and i >= 6:
                        g = (i - 6) // 4
                        pe.wait_ge(o_sb, g + 1)
                        for j in range(4):
                            last = nc.tensor.transpose(bank(5, 4, P)[:, j, :], on[:, j, :], ident)
                        last.then_inc(oT_ps, 1)
                elif kind == "gla":
                    n = item[1]
                    t, lo = n // 2, CHUNK * (n % 2)
                    if n == 0:
                        pe.wait_ge(kdec_sb, 1)
                        pe.wait_ge(mod_sb, MODS.index(4) + 1)
                        pe.wait_ge(oT_sb, 4)
                        pe.wait_ge(proj_sb, 24)
                    for h in range(B_HEADS):
                        last = nc.tensor.matmul(bank(6 + h // 2, 2, B_DV)[:, h % 2, :], kdec[lo:lo + CHUNK, t, P * h:P * h + P],
                                                vb[lo:lo + CHUNK, t, B_DV * h:B_DV * h + B_DV], start=True, stop=True)
                    last.then_inc(kv_ps, 1)
                    pe.wait_ge(state_sb, n + 1)
                    for h in range(B_HEADS):
                        last = nc.tensor.matmul(bank(2 + 2 * t + h // 2, 2, B_DV)[lo:lo + CHUNK, h % 2, :], qbT[:, h, CHUNK * n:CHUNK * n + CHUNK],
                                                state[:, h, :], start=True, stop=True)
                    last.then_inc(gla_ps, 1)
                elif kind == "glanorm":
                    t = item[1]
                    pe.wait_ge(gla_sb, t + 1)
                    for j in range(2):
                        if t:
                            pe.wait_ge(glaT_sb, j + 1)
                        for k in range(4):
                            last = nc.tensor.transpose(bank(6 + j, 4, P)[:, k, :], rb[:, t, P * (4 * j + k):P * (4 * j + k) + P], ident)
                        last.then_inc(glaT_ps, 1)
                elif kind == "wout":
                    u = item[1]
                    s, n = SLOT[("wout", u)]
                    w = stream[:, s, :].rearrange("p (k n) -> p k n", k=KD)
                    pe.wait_ge(unit_in[s], 16 * (n + 1))
                    if u == 0:
                        pe.wait_ge(glaT_sb, 4)
                    for t in range(TT):
                        pe.wait_ge(proj_sb, fill - 1)
                        for k in range(KD):
                            lhs = (oTa if k < 8 else oTb)[:, k % 8, P * t:P * t + P]
                            last = nc.tensor.matmul(bank(fill % 2), lhs, w[:, k, :], start=(k == 0), stop=(k == KD - 1))
                        last.then_inc(proj_ps, 1)
                        fill += 1

            for t in range(TT):
                pe.wait_ge(h2_sb, t + 1)
                for j in range(4):
                    if t:
                        pe.wait_ge(h2T_act if j % 2 else h2T_dve, j // 2 + 1)
                    for k in range(4):
                        last = nc.tensor.transpose(bank(2 + j, 4, P)[:, k, :], y[:, t, 4 * j + k::KD], ident)
                    last.then_inc(h2T_ps, 1)
            pe.wait_ge(h2T_dve, 4)
            pe.wait_ge(h2T_act, 4)
            for t in range(TT):
                for k in range(KD):
                    last = nc.tensor.matmul(bank(0, TT, 36)[:, t, :], h2T[:, k, P * t:P * t + P], wr[:, k, :], start=(k == 0), stop=(k == KD - 1))
            last.then_inc(log_ps, 1)
            pe.wait_ge(m_sb, 1)
            rk = bank(1, 4, NE)
            lt = cst[:, C_LT:C_LT + P]
            nc.tensor.matmul(rk[:, 0, :], lt, R("M")[:, 0, :], start=True, stop=True)
            nc.tensor.matmul(rk[:, 1, :], ones, R("M")[:, 0, :], start=True, stop=False)
            nc.tensor.matmul(rk[:, 1, :], lt, R("M")[:, 1, :], start=False, stop=True)
            nc.tensor.matmul(rk[:, 2, :], ones, R("M")[:, 0, :], start=True, stop=False)
            nc.tensor.matmul(rk[:, 2, :], ones, R("M")[:, 1, :], start=False, stop=True).then_inc(rank_ps, 1)

            def pick_rows():
                for t2 in range(TT):
                    for g in range(4):
                        last = nc.tensor.matmul(bank(0)[32 * g:32 * g + 32, :], pick[:, t2, :], normed[:, t2, 4 * g:4 * g + 4, :], start=(t2 == 0), stop=(t2 == TT - 1))
                last.then_inc(rows_ps, 1)

            def turn_rows():
                for j in range(4):
                    last = nc.tensor.transpose(bank(4, 4, P)[:, j, :], xp[:, P * j:P * j + P], ident)
                last.then_inc(xe_ps, 1)

            pe.wait_ge(h2_kept, TT)
            pe.wait_ge(pick_sb, 1)
            pick_rows()
            pe.wait_ge(rows_sb, 1)
            turn_rows()
            pe.wait_ge(route_sb, 1)
            with pe.Fori(0, NE // 2) as i:
                for b in range(2):
                    lo = pe.value_load(cums[0:1, bass.ds(2 * i + b, 1)], min_val=0, max_val=MAX_TILES)
                    hi = pe.value_load(cums[0:1, bass.ds(2 * i + b + 1, 1)], min_val=1, max_val=MAX_TILES)
                    pe.wait_ge(w1_in[b], 16 * i + 16)
                    pe.wait_ge(w3_in[b], 16 * i + 16)
                    pe.nop(nofuse=True)
                    a13 = [W1[b].rearrange("p (k f) -> p k f", k=KD), W3[b].rearrange("p (k f) -> p k f", k=KD)]
                    w2v = W2.rearrange("p (k n) -> p k n", k=4)
                    with pe.Fori(lo, hi) as t:
                        pe.wait_ge(xe_sb, t + 1)
                        for k in range(KD):
                            for g in range(4):
                                last = nc.tensor.matmul(bank(1)[32 * g:32 * g + 32, 0:256], xe[:, k, :], a13[g // 2][:, k, 256 * (g % 2):256 * (g % 2) + 256],
                                                        start=(k == 0), stop=(k == KD - 1))
                        last.then_inc(ab_ps, 1)
                        pe.wait_ge(pick_sb, t + 2)
                        pick_rows()
                        pe.wait_ge(ab_sb, t + 1)
                        for c in range(2):
                            last = nc.tensor.transpose(bank(2, 2, P)[:, c, :], ab[:, P * c:P * c + P], ident)
                        last.then_inc(h_ps, 1)
                        pe.wait_ge(rows_sb, t + 2)
                        turn_rows()
                        pe.wait_ge(ye_sb, t + 1)
                        pe.wait_ge(hid_sb, t + 1)
                        pe.wait_ge(w2_in, 32 * i + 16 * b + 16)
                        for k in range(4):
                            for g in range(4):
                                last = nc.tensor.matmul(bank(3)[32 * g:32 * g + 32, :], hid[:, k % 2, 32 * (k // 2):32 * (k // 2) + 32], w2v[:, k, 512 * g:512 * g + 512],
                                                        start=(k == 0), stop=(k == 3))
                        last.then_inc(ye_ps, 1)

        @block.vector
        def _(dve):
            n_c = [0]

            def step(ins):
                ins.then_inc(dve_c, 1)
                n_c[0] += 1

            def settle():
                dve.wait_ge(dve_c, n_c[0])

            def link(ins):
                step(ins)
                settle()

            V = nc.vector
            dve.wait_ge(c_exp, 1)
            link(V.tensor_scalar_add(cc[:, 2, :], cc[:, 1, :], 1.0))
            link(V.reciprocal(cc[:, 2, :], cc[:, 2, :]))
            link(V.tensor_tensor(cc[:, 2, :], cc[:, 2, :], cc[:, 0, :], ALU.mult))

            def prepare():
                dve.wait_ge(par_in, 16 * len(params))
                lw = lamw.rearrange("p (n c) -> p n c", n=4)
                link(V.tensor_tensor(lw[:, 0:4:2, :], lw[:, 0:4:2, :], lw[:, 1:4:2, :], ALU.mult))
                V.tensor_reduce(lamv[:, 0:2], lw[:, 0:4:2, :], axis=AX.X, op=ALU.add).then_inc(lam_sum, 1)
                dve.wait_ge(lam_exp, 1)
                link(V.tensor_tensor(lamv[:, 4:5], lamv[:, 3:4], lamv[:, 2:3], ALU.subtract))
                link(V.tensor_scalar_add(lamv[:, 5:6], lamv[:, 4:5], -LAM_INIT))
                link(V.tensor_scalar(gsub[:, :], gsub[:, :], 1.0 - LAM_INIT, None, ALU.mult))
                dve.wait_ge(relrow_ps, 1)
                V.tensor_copy(relrow, bank(4)[0:A_HEADS, 0:384]).then_inc(relrow_sb, 1)
                for t in range(TT):
                    dve.wait_ge(xr, t + 1)
                    V.tensor_scalar(resid[:, t, :], resid[:, t, :], st[:, 2 + t:3 + t], None, ALU.mult).then_inc(xn, 1)

            def accumulate(m, q):
                s, n = SLOT[("ada", m, q)]
                w = stream[:, s, :].rearrange("p (k n) -> p k n", k=4)
                dve.wait_ge(unit_in[s], 16 * (n + 1))
                if q == 0 and MODS.index(m):
                    dve.wait_ge(mod_ps, MODS.index(m))
                for k in range(4):
                    col = cc[:, 2, 4 * q + k:4 * q + k + 1]
                    if 4 * q + k == 0:
                        ins = V.tensor_scalar(acc[:, :], w[:, k, :], col, None, ALU.mult)
                    else:
                        ins = V.scalar_tensor_tensor(out=acc[:, :], in0=w[:, k, :], scalar=col, in1=acc[:, :], op0=ALU.mult, op1=ALU.add)
                    if k < 3:
                        link(ins)
                ins.then_inc(ada_done, 1)
                dve.wait_ge(ada_done, 4 * MODS.index(m) + q + 1)

            for item in SCHED:
                kind = item[0]
                if kind == "ada":
                    accumulate(item[1], item[2])
                elif kind == "mod":
                    m = item[1]
                    j = MODS.index(m)
                    if j == 0:
                        prepare()
                    dve.wait_ge(mod_ps, j + 1)
                    V.tensor_tensor(mod[:, m, :], bank(6)[:, 16 * m:16 * m + 16], bada[:, m, :], ALU.add).then_inc(mod_sb, 1)
                    dve.wait_ge(mod_sb, j + 1)
                    if m == 1 or m == 4:
                        link(V.scalar_tensor_tensor(out=mod[:, m, :], in0=mod[:, m, :], scalar=1.0, in1=gains[:, 0 if m == 1 else 2, :], op0=ALU.add, op1=ALU.mult))
                    if m == 2 or m == 5:
                        V.tensor_tensor(mod[:, m, :], mod[:, m, :], gains[:, 1 if m == 2 else 3, :], ALU.mult).then_inc(g_sb, 1)
                elif kind == "modulate":
                    dve.wait_ge(xT_sb, 8)
                    for k in range(KD):
                        ins = V.tensor_scalar(hT[:, k, :], hT[:, k, :], mod[:, 1, k:k + 1], mod[:, 0, k:k + 1], ALU.mult, ALU.add)
                    ins.then_inc(hT_ready, 1)
                elif kind == "alpha":
                    dve.wait_ge(late_in, 32)
                    for t in range(TT):
                        dve.wait_ge(z_ps, t + 1)
                        link(V.tensor_tensor(la[:, t, :], bank(2 + t), balpha, ALU.add))
                        V.scalar_tensor_tensor(out=tmp[:, 512 * t:512 * t + 512], in0=la[:, t, :], scalar=-1.0, in1=la[:, t, :],
                                               op0=ALU.mult, op1=ALU.max).then_inc(z_abs, 1)
                    for t in range(TT):
                        dve.wait_ge(z_ln, t + 1)
                        V.scalar_tensor_tensor(out=la[:, t, :], in0=la[:, t, :], scalar=0.0, in1=tmp[:, 512 * t:512 * t + 512],
                                               op0=ALU.min, op1=ALU.subtract).then_inc(la_sb, 1)
                elif kind == "kdec":
                    dve.wait_ge(suf_exp, 3)
                    dve.wait_ge(proj_sb, 14)
                    for t in range(TT):
                        ins = V.tensor_tensor(kdec[:, t, :], kdec[:, t, :], kb[:, t, :], ALU.mult)
                    ins.then_inc(kdec_sb, 1)
                elif kind == "att":
                    i = item[1]
                    if i < ATT:
                        h, b = head_block(i)
                        nk = P * (b + 1)
                        if i == 0:
                            dve.wait_ge(masked, 1)
                        dve.wait_ge(s_ps, i + 1)
                        V.scalar_tensor_tensor(out=sc[:, :, 0:nk], in0=ps[:, 2:4, 0:nk], scalar=A_DK ** -0.5,
                                               in1=bias[:, h:h + 1, S - nk:S].to_broadcast((P, 2, nk)), op0=ALU.mult, op1=ALU.add).then_inc(s_sb, 1)
                        dve.wait_ge(s_sb, i + 1)
                        V.tensor_reduce(st[:, 8:10], sc[:, :, 0:nk], axis=AX.X, op=ALU.max, negate=True).then_inc(p_max, 1)
                        dve.wait_ge(p_exp, i + 1)
                        if i:
                            dve.wait_ge(pdT_ps, i)
                        link(V.reciprocal(st[:, 12:14], st[:, 10:12]))
                        link(V.tensor_tensor(st[:, 14:15], st[:, 13:14], lamv[:, 5:6], ALU.mult))
                        link(V.tensor_scalar(pr[:, 0, 0:nk], pr[:, 0, 0:nk], st[:, 12:13], None, ALU.mult))
                        V.scalar_tensor_tensor(out=pd[:, 0:nk], in0=pr[:, 1, 0:nk], scalar=st[:, 14:15], in1=pr[:, 0, 0:nk],
                                               op0=ALU.mult, op1=ALU.add).then_inc(pd_sb, 1)
                    if i % 4 == 1 and i >= 5:
                        g = (i - 5) // 4
                        dve.wait_ge(o_rs, g + 1)
                        if g:
                            dve.wait_ge(oT_ps, g)
                        V.tensor_tensor(on, bank(4, 4, A_DV), st[:, 20:24].unsqueeze(2).to_broadcast((P, 4, A_DV)), ALU.mult).then_inc(o_sb, 1)
                    if i % 4 == 2 and i >= 6:
                        g = (i - 6) // 4
                        dve.wait_ge(oT_ps, g + 1)
                        V.tensor_scalar(oTa[:, 4 * (g // 2):4 * (g // 2) + 4, P * (g % 2):P * (g % 2) + P], bank(5, 4, P), gsub[:, 0:1], None,
                                        ALU.mult).then_inc(oT_sb, 1)
                elif kind == "gla":
                    n = item[1]
                    if n == 0:
                        for t in range(TT):
                            dve.wait_ge(rb_exp, t + 1)
                            link(V.tensor_scalar_add(tmp, tmp, 1.0))
                            link(V.reciprocal(tmp, tmp))
                            V.tensor_tensor(rb[:, t, :], rb[:, t, :], tmp, ALU.mult).then_inc(rb_sb, 1)
                    dve.wait_ge(kv_ps, n + 1)
                    for h in range(B_HEADS):
                        kv = bank(6 + h // 2, 2, B_DV)[:, h % 2, :]
                        if n == 0:
                            ins = V.tensor_copy(state[:, h, :], kv)
                        else:
                            ins = V.scalar_tensor_tensor(out=state[:, h, :], in0=state[:, h, :], scalar=st[:, DECAY(n, h):DECAY(n, h) + 1], in1=kv,
                                                         op0=ALU.mult, op1=ALU.add)
                    ins.then_inc(state_sb, 1)
                    dve.wait_ge(state_sb, n + 1)
                elif kind == "glanorm":
                    t = item[1]
                    dve.wait_ge(gla_rs, t + 1)
                    dve.wait_ge(rb_sb, 2)
                    for h in range(B_HEADS):
                        r = rb[:, t, B_DV * h:B_DV * h + B_DV]
                        ins = V.scalar_tensor_tensor(out=r, in0=bank(2 + 2 * t + h // 2, 2, B_DV)[:, h % 2, :], scalar=st[:, 28 + h:29 + h], in1=r,
                                                     op0=ALU.mult, op1=ALU.mult)
                    ins.then_inc(gla_sb, 1)

            dve.wait_ge(y_sum, 8)
            V.tensor_reduce(st[:, 56:58], st[:, 48:56].rearrange("p (t u) -> p t u", t=TT), axis=AX.X, op=ALU.add).then_inc(y_tot, 1)
            dve.wait_ge(g1_in, 16)
            dve.wait_ge(xre_in, 16)
            dve.wait_ge(y_rs, 1)
            dve.wait_ge(proj_sb, 24 + 8)
            for t in range(TT):
                link(V.scalar_tensor_tensor(out=y[:, t, :], in0=y[:, t, :], scalar=st[:, 58 + t:59 + t], in1=g1b, op0=ALU.mult, op1=ALU.mult))
                V.tensor_tensor(resid[:, t, :], resid[:, t, :], y[:, t, :], ALU.add).then_inc(x1_sb, 1)
            for t in range(TT):
                dve.wait_ge(x1_rs, t + 1)
                V.tensor_scalar(y[:, t, :], resid[:, t, :], st[:, 62 + t:63 + t], None, ALU.mult).then_inc(h2_sb, 1)
            for t in range(TT):
                for j in (0, 2):
                    dve.wait_ge(h2T_ps, 4 * t + j + 1)
                    for k in range(4):
                        ins = V.tensor_scalar(h2T[:, 4 * j + k, P * t:P * t + P], bank(2 + j, 4, P)[:, k, :], mod[:, 4, 4 * j + k:4 * j + k + 1],
                                              mod[:, 3, 4 * j + k:4 * j + k + 1], ALU.mult, ALU.add)
                    ins.then_inc(h2T_dve, 1)

            dve.wait_ge(log_ps, 1)
            L, g8 = R("L"), R("g8")
            link(V.memset(g8, -3.0e38))
            link(V.tensor_tensor(L, bank(0, TT, 36), br[:, :].unsqueeze(1).to_broadcast((P, TT, 36)), ALU.add))
            link(V.tensor_copy(g8[:, :, 0:4], L[:, :, 0:4]))
            for t in range(TT):
                link(V.max(R("gm")[:, t, :], g8[:, t, :]))
                link(V.max_index(R("gi")[:, t, :], R("gm")[:, t, :], g8[:, t, :]))
            V.tensor_scalar(R("ng"), R("gm")[:, :, 0:1], -1.0, None, ALU.mult).then_inc(g_max, 1)
            link(V.tensor_copy(R("gf"), R("gi")[:, :, 0:1]))
            for t in range(TT):
                link(V.tensor_scalar(R("sel")[:, t, :], cst[:, C_IOTA:C_IOTA + 4], R("gf")[:, t, :], None, ALU.is_equal))
                link(V.tensor_tensor(R("eg")[:, t], L[:, t, 4:36].rearrange("p (g e) -> p g e", g=4),
                                     R("sel")[:, t, :].unsqueeze(2).to_broadcast((P, 4, 8)), ALU.mult))
                link(V.tensor_reduce(R("es")[:, t, :], R("eg")[:, t].rearrange("p g e -> p e g"), axis=AX.X, op=ALU.add))
                link(V.max(R("em")[:, t, :], R("es")[:, t, :]))
                link(V.max_index(R("ei")[:, t, :], R("em")[:, t, :], R("es")[:, t, :]))
            V.tensor_tensor(R("d2"), R("em")[:, :, 1:2], R("em")[:, :, 0:1], ALU.subtract).then_inc(e_max, 1)
            link(V.tensor_copy(R("ef"), R("ei")[:, :, 0:2]))
            for t in range(TT):
                link(V.scalar_tensor_tensor(out=R("ex")[:, t, :], in0=R("gf")[:, t, :].to_broadcast((P, 2)), scalar=float(PER_GROUP), in1=R("ef")[:, t, :],
                                            op0=ALU.mult, op1=ALU.add))
                for j in range(2):
                    link(V.tensor_scalar(R("oh")[:, t, j, :], cst[:, C_IOTA:C_IOTA + NE], R("ex")[:, t, j:j + 1], None, ALU.is_equal))
                ins = V.tensor_tensor(R("M")[:, t, :], R("oh")[:, t, 0, :], R("oh")[:, t, 1, :], ALU.add)
                if t == TT - 1:
                    ins.then_inc(m_sb, 1)
                    dve.wait_ge(m_sb, 1)
            dve.wait_ge(r_exp2, 1)
            link(V.tensor_scalar_add(R("w")[:, :, 0:1], R("e2"), 1.0))
            link(V.tensor_tensor(R("w")[:, :, 0:1], R("w")[:, :, 0:1], R("gs"), ALU.mult))
            link(V.reciprocal(R("w")[:, :, 0:1], R("w")[:, :, 0:1]))
            link(V.tensor_tensor(R("w")[:, :, 1:2], R("w")[:, :, 0:1], R("e2"), ALU.mult))
            dve.wait_ge(rank_ps, 1)
            rk = bank(1, 4, NE)
            link(V.tensor_copy(R("cnt"), rk[:, 2, :]))
            link(V.tensor_tensor(R("cmp"), R("cnt").unsqueeze(2).to_broadcast((P, NE, 8)),
                                 cst[:, C_THR:C_THR + 8].unsqueeze(1).to_broadcast((P, NE, 8)), ALU.is_gt))
            link(V.tensor_reduce(R("nt"), R("cmp"), axis=AX.X, op=ALU.add))
            link(V.tensor_scalar(R("nt"), R("nt"), 1.0, None, ALU.max))
            link(V.memset(R("zero"), 0.0))
            link(V.tensor_tensor_scan(R("cum"), R("nt"), R("zero"), 0.0, ALU.add, ALU.add))
            link(V.memset(cums[0:1, 0:1], 0))
            link(V.tensor_copy(cums[0:1, 1:NE + 1], R("cum")[0:1, :]))
            link(V.tensor_tensor(R("base"), R("cum"), R("nt"), ALU.subtract))
            for t in range(TT):
                link(V.scalar_tensor_tensor(out=R("pos")[:, t, :], in0=R("base"), scalar=float(ROWS), in1=rk[:, t, :], op0=ALU.mult, op1=ALU.add))
                for j in range(2):
                    link(V.tensor_tensor(R("oh")[:, t, j, :], R("oh")[:, t, j, :], R("pos")[:, t, :], ALU.mult))
            link(V.tensor_reduce(rel[:, :, :], R("oh"), axis=AX.X, op=ALU.add))
            link(V.tensor_copy(slots[:, :], rel[:, :, :].rearrange("p t j -> p (t j)")))
            V.tensor_copy(gates[:, :, :], R("w")).then_inc(route_sb, 1)
            dve.wait_ge(route_sb, 1)

            total = dve.value_load(cums[0:1, NE:NE + 1], min_val=NE, max_val=MAX_TILES)
            iota = cst[:, C_IOTA:C_IOTA + ROWS].unsqueeze(1).to_broadcast((P, 2 * TT, ROWS))
            rel4 = rel[:, :, :].rearrange("p t j -> p (t j)").unsqueeze(2).to_broadcast((P, 2 * TT, ROWS))

            def picks():
                return V.tensor_tensor(hit, iota, rel4, ALU.is_equal)

            def both():
                return V.tensor_tensor(pick, hit[:, 0::2, :], hit[:, 1::2, :], ALU.add)

            def by_column(m):
                return mod[:, m, :].rearrange("p (g j) -> p j g", g=4).unsqueeze(3).to_broadcast((P, 4, 4, ROWS))

            xe4 = xe.rearrange("p (g j) r -> p j g r", g=4)
            xe_ps4 = bank(4, 4, P).rearrange("p j (g r) -> p j g r", g=4)

            link(picks())
            both().then_inc(pick_sb, 1)
            dve.wait_ge(rows_ps, 1)
            V.tensor_copy(xp, bank(0)).then_inc(rows_sb, 1)
            dve.wait_ge(xe_ps, 1)
            V.tensor_tensor(xe4, xe_ps4, by_column(4), ALU.mult).then_inc(xe_t, 1)
            dve.wait_ge(xe_t, 1)
            V.tensor_tensor(xe4, xe4, by_column(3), ALU.add).then_inc(xe_sb, 1)
            with dve.Fori(0, total) as t:
                V.tensor_scalar_add(rel[:, :, :], rel[:, :, :], -float(ROWS)).then_inc(pick_c, 1)
                dve.wait_ge(pick_c, 2 * t + 1)
                picks().then_inc(pick_c, 1)
                dve.wait_ge(pick_c, 2 * t + 2)
                both().then_inc(pick_sb, 1)
                dve.wait_ge(rows_ps, t + 2)
                V.tensor_copy(xp, bank(0)).then_inc(rows_sb, 1)
                dve.wait_ge(h_exp, t + 1)
                hp = bank(2, 2, P)
                V.tensor_scalar_add(eh, eh, 1.0).then_inc(h_t, 1)
                dve.wait_ge(h_t, 3 * t + 1)
                V.reciprocal(eh, eh).then_inc(h_t, 1)
                dve.wait_ge(h_t, 3 * t + 2)
                V.tensor_tensor(eh, hp[:, :, 0:64], eh, ALU.mult).then_inc(h_t, 1)
                dve.wait_ge(h_t, 3 * t + 3)
                V.tensor_tensor(hid, hp[:, :, 64:128], eh, ALU.mult).then_inc(hid_sb, 1)
                dve.wait_ge(xe_ps, t + 2)
                V.tensor_tensor(xe4, xe_ps4, by_column(4), ALU.mult).then_inc(xe_t, 1)
                dve.wait_ge(xe_t, t + 2)
                V.tensor_tensor(xe4, xe4, by_column(3), ALU.add).then_inc(xe_sb, 1)

            for t in range(TT):
                dve.wait_ge(fin_rows_in[t], 32)
                ga, gb = fin_rows(2 * t), fin_rows(2 * t + 1)
                link(V.tensor_scalar(ga, ga, gates[:, t, 0:1], None, ALU.mult))
                V.scalar_tensor_tensor(out=ga, in0=gb, scalar=gates[:, t, 1:2], in1=ga, op0=ALU.mult, op1=ALU.add).then_inc(fin_sum, 1)
            dve.wait_ge(fin_in, 32)
            for t in range(TT):
                dve.wait_ge(fin_rs, t + 1)
                link(V.scalar_tensor_tensor(out=fin_rows(2 * t), in0=fin_rows(2 * t), scalar=st[:, 70 + t:71 + t], in1=g2b, op0=ALU.mult, op1=ALU.mult))
                V.tensor_tensor(x1r[:, t, :], x1r[:, t, :], fin_rows(2 * t), ALU.add).then_inc(fin_sb, 1)

        @block.scalar
        def _(act):
            n_c = [0]

            def link(ins):
                ins.then_inc(act_c, 1)
                n_c[0] += 1
                act.wait_ge(act_c, n_c[0])

            A = nc.scalar.activation
            act.dma_start(cc[:, 0, :], vec(a["c"])).then_inc(c_in, 16)
            act.dma_start(cst[:, :], a["cst"][:, 0:C_KEEP]).then_inc(const_in, 16)
            act.dma_start(bkt, a["cst"][0:N_BUCKETS, C_BKT:C_ALL]).then_inc(const_in, 16)
            for t in range(TT):
                act.dma_start(resid[:, t, :], x_d[:, t, :]).then_inc(x_in, 16)
            act.wait_ge(c_in, 16)
            A(cc[:, 1, :], cc[:, 0, :], ACT.Exp, scale=-1.0).then_inc(c_exp, 1)
            act.wait_ge(x_in, 32)
            for t in range(TT):
                A(junk1, resid[:, t, :], ACT.Square, accum_out=st[:, t:t + 1]).then_inc(xsq, 1)
                act.wait_ge(xsq, t + 1)
            act.wait_ge(lam_sum, 1)
            A(lamv[:, 2:4], lamv[:, 0:2], ACT.Exp).then_inc(lam_exp, 1)
            act.wait_ge(relrow_sb, 1)
            rr = bass.AP(tensor=relrow.tensor, offset=relrow.offset, ap=[relrow.ap[0], [0, P], [1, SKEW]])
            act.dma_start(skew[:, :, :], rr).then_inc(skew_out, 16)
            for t in range(TT):
                for j in range(4):
                    act.wait_ge(xT_ps, 4 * t + j + 1)
                    A(hT[:, 4 * j:4 * j + 4, P * t:P * t + P], bank(j, 4, P), ACT.Copy).then_inc(xT_sb, 1)
            act.wait_ge(skew_out, 16)
            act.dma_start(bias, bass.AP(tensor=skew[:, :, :].tensor, offset=P - 1, ap=[[SKEW - 1, P], [P * SKEW, A_HEADS], [1, S]])).then_inc(bias_in, 16)
            act.dma_start(walpha, a["w_alpha"][0]).then_inc(late_in, 16)
            act.dma_start(balpha, row_bcast(a["b_alpha"], 512)).then_inc(late_in, 16)

            fill = 0
            for item in SCHED:
                kind = item[0]
                if kind == "alpha":
                    act.wait_ge(zb_ps, 1)
                    A(zbT[:, :], bank(5)[0:GATE_RANK, 0:S], ACT.Copy).then_inc(zb_sb, 1)
                    for t in range(TT):
                        act.wait_ge(z_abs, t + 1)
                        link(A(tmp[:, 512 * t:512 * t + 512], tmp[:, 512 * t:512 * t + 512], ACT.Exp, scale=-1.0))
                        A(tmp[:, 512 * t:512 * t + 512], tmp[:, 512 * t:512 * t + 512], ACT.Ln, bias=ones[:, 0:1]).then_inc(z_ln, 1)
                    for t in range(TT):
                        act.wait_ge(suf_ps, t + 1)
                        A(kdec[:, t, :], bank(4 + t), ACT.Exp, scale=1.0 / GATE_TAU).then_inc(suf_exp, 1)
                    act.wait_ge(suf_ps, 3)
                    A(st[:, 32:48], bank(7)[:, 0:16], ACT.Exp, scale=1.0 / GATE_TAU).then_inc(suf_exp, 1)
                elif kind == "proj":
                    _, i, half = item
                    c = ORDER[i]
                    act.wait_ge(proj_ps, fill + 1)
                    src = bank(fill % 2)
                    if c in TRANSPOSED:
                        dst = {0: (qaT, 0), 1: (qaT, 4), 2: (kaT, 0), 3: (kaT, 4), 6: (qbT, 0)}[c]
                        dst = dst[0][:, dst[1] + 2 * half:dst[1] + 2 * half + 2, :]
                        src = bank(fill % 2, 2, S)
                        scale = B_DK ** -0.5 if c == 6 else 1.0
                    else:
                        dst = {4: (va, 0), 5: (va, 512), 7: (kb, 0), 8: (vb, 0), 9: (vb, 512), 10: (rb, 0), 11: (rb, 512)}[c]
                        dst = dst[0][:, half, dst[1]:dst[1] + 512]
                        scale = 1.0
                    A(dst, src, ACT.Copy, scale=scale).then_inc(proj_sb, 1)
                    fill += 1
                elif kind == "att":
                    i = item[1]
                    if 1 <= i < ATT + 1:
                        j = i - 1
                        _, b = head_block(j)
                        act.wait_ge(pdT_ps, j + 1)
                        A(pdT[:, 0:P * (b + 1)], bank(7)[:, 0:P * (b + 1)], ACT.Copy).then_inc(pdT_sb, 1)
                    if i < ATT:
                        _, b = head_block(i)
                        nk = P * (b + 1)
                        act.wait_ge(p_max, i + 1)
                        if i:
                            act.wait_ge(pd_sb, i)
                        for m in range(2):
                            ins = A(pr[:, m, 0:nk], sc[:, m, 0:nk], ACT.Exp, bias=st[:, 8 + m:9 + m], accum_out=st[:, 10 + m:11 + m])
                        ins.then_inc(p_exp, 1)
                    if i % 4 == 1 and i >= 5:
                        g = (i - 5) // 4
                        act.wait_ge(o_ps, 4 * g + 4)
                        for j in range(4):
                            ins = A(tmp[:, 0:A_DV], bank(4, 4, A_DV)[:, j, :], ACT.Square, accum_out=st[:, 16 + j:17 + j])
                            if j < 3:
                                link(ins)
                        ins.then_inc(o_sq, 1)
                        act.wait_ge(o_sq, g + 1)
                elif kind == "gla":
                    n = item[1]
                    if n == 0:
                        act.wait_ge(proj_sb, 24)
                        for t in range(TT):
                            if t:
                                act.wait_ge(rb_sb, t)
                            A(tmp, rb[:, t, :], ACT.Exp, scale=-1.0).then_inc(rb_exp, 1)
                elif kind == "glanorm":
                    t = item[1]
                    act.wait_ge(gla_ps, 2 * t + 2)
                    act.wait_ge(rb_sb, 2)
                    if t:
                        act.wait_ge(gla_sb, t)
                    for h in range(B_HEADS):
                        ins = A(tmp[:, 0:B_DV], bank(2 + 2 * t + h // 2, 2, B_DV)[:, h % 2, :], ACT.Square, accum_out=st[:, 24 + h:25 + h])
                        if h < B_HEADS - 1:
                            link(ins)
                    ins.then_inc(gla_sq, 1)
                    act.wait_ge(gla_sq, t + 1)
                    for j in range(2):
                        act.wait_ge(glaT_ps, 2 * t + j + 1)
                        for r in range(2):
                            ins = A(oTb[:, 4 * j + r:4 * j + 4:2, P * t:P * t + P], bank(6 + j, 4, P)[:, r::2, :], ACT.Copy, scale=gnb[:, r:r + 1])
                        ins.then_inc(glaT_sb, 1)
                elif kind == "wout":
                    u = item[1]
                    for t in range(TT):
                        act.wait_ge(proj_ps, fill + 1)
                        A(y[:, t, 512 * u:512 * u + 512], bank(fill % 2), ACT.Square, accum_out=st[:, 48 + 4 * t + u:49 + 4 * t + u]).then_inc(y_sum, 1)
                        act.wait_ge(y_sum, 2 * u + t + 1)
                        A(y[:, t, 512 * u:512 * u + 512], bank(fill % 2), ACT.Copy).then_inc(proj_sb, 1)
                        fill += 1
                    if u == 0:
                        act.dma_start(resid[:, :, :], x_d).then_inc(xre_in, 16)
                        act.wait_ge(g1_out, 16)
                        act.dma_start(g1b, row_bcast(gdram[0, :, :], D)).then_inc(g1_in, 16)

            for t in range(TT):
                act.wait_ge(x1_sb, t + 1)
                A(h2T[:, 0:8, :], resid[:, t, :].rearrange("p (k n) -> p k n", k=8), ACT.Square, accum_out=st[:, 60 + t:61 + t]).then_inc(x1_sq, 1)
                act.wait_ge(x1_sq, t + 1)
            act.dma_start(x1d[:, :, :], resid[:, :, :]).then_inc(x1_out, 16)
            for t in range(TT):
                for j in (1, 3):
                    act.wait_ge(h2T_ps, 4 * t + j + 1)
                    for k in range(4):
                        ins = A(h2T[:, 4 * j + k, P * t:P * t + P], bank(2 + j, 4, P)[:, k, :], ACT.Identity,
                                scale=mod[:, 4, 4 * j + k:4 * j + k + 1], bias=mod[:, 3, 4 * j + k:4 * j + k + 1])
                    ins.then_inc(h2T_act, 1)
            act.wait_ge(x1_out, 16)
            act.wait_ge(h2_sb, TT)
            for t in range(TT):
                A(normed[:, t], y[:, t, :].rearrange("p (q k) -> p k q", k=KD), ACT.Copy).then_inc(h2_kept, 1)
            act.wait_ge(g_max, 1)
            for t in range(TT):
                link(A(R("ge")[:, t, :], R("L")[:, t, 0:4], ACT.Exp, bias=R("ng")[:, t, :], accum_out=R("gs")[:, t, :]))
            act.wait_ge(e_max, 1)
            A(R("e2"), R("d2"), ACT.Exp).then_inc(r_exp2, 1)

            act.wait_ge(route_sb, 1)
            act.wait_ge(ys_zero, 16)
            total = act.value_load(cums[0:1, NE:NE + 1], min_val=NE, max_val=MAX_TILES)

            def tile(t, first):
                act.wait_ge(ab_ps, t + 1)
                A(ab, bank(1)[:, 0:256], ACT.Copy).then_inc(ab_sb, 1)
                act.wait_ge(h_ps, t + 1)
                A(eh, bank(2, 2, P)[:, :, 0:64], ACT.Exp, scale=-1.0).then_inc(h_exp, 1)
                act.wait_ge(ye_ps, t + 1)
                if not first:
                    act.wait_ge(ye_out, 64 * t)
                A(ye, bank(3), ACT.Copy).then_inc(ye_sb, 1)
                act.wait_ge(ye_sb, t + 2)
                for g in range(4):
                    act.dma_start(ys[bass.ds(t * ROWS, ROWS), 512 * g:512 * g + 512], ye[32 * g:32 * g + 32, :]).then_inc(ye_out, 16)

            tile(0, True)
            with act.Fori(1, total) as t:
                tile(t, False)
            for t in range(TT):
                act.wait_ge(fin_sum, t + 1)
                A(fin_rows(2 * t + 1), fin_rows(2 * t), ACT.Square, accum_out=st[:, 66 + t:67 + t]).then_inc(fin_sq, 1)
            for t in range(TT):
                act.wait_ge(fin_sb, t + 1)
                act.dma_start(out_d[:, t, :], x1r[:, t, :]).then_inc(fin_out, 16)
            act.wait_ge(fin_out, 32)

        @block.gpsimd
        def _(pool):
            n_c = [0]

            def rms(src, dst, width):
                n = src.shape[1]
                nc.gpsimd.tensor_scalar(dst, src, 1.0 / width, EPS, ALU.mult, ALU.add).then_inc(pool_c, 1)
                n_c[0] += 1
                pool.wait_ge(pool_c, n_c[0])
                return nc.gpsimd.tensor_tensor(dst, dst, cst[:, C_NH:C_NH + n], ALU.pow)

            for dst, src in params:
                pool.dma_start(dst, src).then_inc(par_in, 16)
            pool.wait_ge(const_in, 32)
            for t in range(TT):
                pool.wait_ge(xsq, t + 1)
                rms(st[:, t:t + 1], st[:, 2 + t:3 + t], D).then_inc(xr, 1)
            pool.wait_ge(bias_in, 16)
            pool.memset(bias[0:CHUNK, :, S - CHUNK:S], NEG).then_inc(masked, 1)
            for item in SCHED:
                kind = item[0]
                if kind == "mod" and item[1] == 2:
                    pool.wait_ge(g_sb, 1)
                    pool.dma_start(gdram[0, :, :], mod[:, 2, :]).then_inc(g1_out, 16)
                elif kind == "mod" and item[1] == 5:
                    pool.wait_ge(g_sb, 2)
                    pool.dma_start(gdram[1, :, :], mod[:, 5, :]).then_inc(g2_out, 16)
                elif kind == "att" and item[1] % 4 == 1 and item[1] >= 5:
                    g = (item[1] - 5) // 4
                    pool.wait_ge(o_sq, g + 1)
                    if g:
                        pool.wait_ge(o_sb, g)
                    rms(st[:, 16:20], st[:, 20:24], A_DV).then_inc(o_rs, 1)
                elif kind == "glanorm":
                    t = item[1]
                    pool.wait_ge(gla_sq, t + 1)
                    rms(st[:, 24:28], st[:, 28:32], B_DV).then_inc(gla_rs, 1)
            pool.wait_ge(oT_sb, 4)
            pool.memset(ye, 0.0).then_inc(ye_sb, 1)
            pool.wait_ge(ye_sb, 1)
            pool.dma_start(ys[NE * ROWS:MAX_TILES * ROWS, :].rearrange("(p r) (g n) -> p (r g) n", p=P, g=4),
                           ye.unsqueeze(1).to_broadcast((P, 4 * (MAX_TILES - NE) * ROWS // P, 512))).then_inc(ys_zero, 16)
            pool.wait_ge(y_tot, 1)
            rms(st[:, 56:58], st[:, 58:60], D).then_inc(y_rs, 1)
            for t in range(TT):
                pool.wait_ge(x1_sq, t + 1)
                rms(st[:, 60 + t:61 + t], st[:, 62 + t:63 + t], D).then_inc(x1_rs, 1)
            pool.wait_ge(route_sb, 1)
            pool.wait_ge(ys_zero, 16)
            total = pool.value_load(cums[0:1, NE:NE + 1], min_val=NE, max_val=MAX_TILES)
            pool.wait_ge(ye_out, 64 * total)
            pool.nop(nofuse=True)
            for j in range(2 * TT):
                pool.indirect_dma_start(fin_rows(j), None, ys[:, :], bass.IndirectOffsetOnAxis(ap=slots[:, j:j + 1], axis=0)).then_inc(fin_rows_in[j // 2], 16)
            for t in range(TT):
                pool.wait_ge(fin_sq, t + 1)
                rms(st[:, 66 + t:67 + t], st[:, 70 + t:71 + t], D).then_inc(fin_rs, 1)


NAMES = ["x", "c", "rel_bias", "w_ada", "b_ada", "g_pre_mix", "g_post_mix", "w_in", "w_alpha", "b_alpha", "lam_q1", "lam_k1",
         "lam_q2", "lam_k2", "g_sub_a", "g_norm_b", "w_out", "g_pre_ffn", "g_post_ffn", "w_router_g", "b_router_g",
         "w_router_e", "b_router_e", "w1", "w3", "w2"]


def kernel(**inputs):
    import concourse.bacc as bacc
    from concourse.bass_utils import run_bass_kernel_spmd

    nc = bacc.Bacc("TRN2", target_bir_lowering=False, num_devices=1)
    arrays = {f"in_{n}": np.ascontiguousarray(inputs[n]) for n in NAMES}
    arrays["in_cst"] = shape_constants()
    aps = {n[3:]: nc.dram_tensor(n, v.shape, mybir.dt.from_np(v.dtype), kind="ExternalInput").ap() for n, v in arrays.items()}
    out = nc.dram_tensor("out", (1, S, D), mybir.dt.float32, kind="ExternalOutput").ap()
    build(nc, aps, out)
    return run_bass_kernel_spmd(nc, [arrays], core_ids=[0]).results[0]["out"]
```

```python
import math
from contextlib import ExitStack

import numpy as np
import concourse.bass as bass
from concourse import mybir

D = 2048
S = 256
P = 128
TT = S // P
KD = D // P
CHUNK = 64
A_HEADS, A_DK, A_DV = 8, 64, 128
B_HEADS, B_DK, B_DV = 4, 128, 256
GATE_RANK, GATE_TAU = 16, 16.0
N_BUCKETS, MAX_DISTANCE = 32, 256
N_GROUPS, PER_GROUP = 4, 8
NE = N_GROUPS * PER_GROUP
F = D // 4
D_IN = 3 * 1024 + 2 * 512 + 2 * 1024 + GATE_RANK
EPS = 1e-6
LAM_INIT = 0.8 - 0.6 * math.exp(-0.3 * 0)
NEG = -1e30
ROWS = 32
MAX_TILES = NE + (2 * S - NE) // ROWS + 1
UNIT = 8192
REL = 2 * S - 1
SKEW = 384

C_ID, C_LT, C_SUF, C_ONE, C_IOTA, C_THR, C_TOK, C_NH, C_HALF, C_BKT = 0, 128, 256, 384, 512, 544, 552, 554, 558, 560
C_KEEP = C_BKT
C_ALL = C_BKT + 512

ORDER = [0, 2, 4, 1, 3, 5, 7, 6, 8, 9, 10, 11]
TRANSPOSED = {0, 1, 2, 3, 6}
ATT = 2 * A_HEADS
HEADS_READY = [6, 12]
X1T_BANK = [[2, 3, 4, 5], [6, 7, 0, 1]]
ATT_FROM = 4


def head_block(i):
    g = i // 4
    return 4 * (g // 2) + i % 4, g % 2


def t5_bucket(rel):
    nb = N_BUCKETS // 2
    exact = nb // 2
    n = np.abs(rel)
    nf = np.maximum(n, 1).astype(np.float32)
    large = exact + (np.log(nf / exact) / math.log(MAX_DISTANCE / exact) * (nb - exact)).astype(np.int32)
    return np.where(rel > 0, nb, 0) + np.where(n < exact, n, np.minimum(large, nb - 1))


def shape_constants():
    c = np.zeros((P, C_ALL), np.float32)
    p = np.arange(P)
    c[:, C_ID:C_ID + P] = np.eye(P)
    c[:, C_LT:C_LT + P] = p[:, None] < p[None, :]
    c[:, C_SUF:C_SUF + P] = (p[:, None] > p[None, :]) & (p[:, None] // CHUNK == p[None, :] // CHUNK)
    c[:, C_ONE:C_ONE + P] = 1.0
    c[:, C_IOTA:C_IOTA + NE] = np.arange(NE)
    c[:, C_THR:C_THR + 8] = ROWS * np.arange(8)
    c[:, C_TOK:C_TOK + TT] = p[:, None] + P * np.arange(TT)
    c[:, C_NH:C_NH + 4] = -0.5
    c[:, C_HALF] = p < CHUNK
    c[:, C_HALF + 1] = p >= CHUNK
    rel = np.arange(REL) - (S - 1)
    c[0:N_BUCKETS, C_BKT:C_BKT + REL] = t5_bucket(rel)[None, :] == np.arange(N_BUCKETS)[:, None]
    return c


def schedule():
    out = []
    for m in (0, 1):
        for q in range(4):
            if (m, q) == (0, 3):
                out.append(("prepare",))
            out += [("ada", m, q, k) for k in range(4)]
        out.append(("mod", m))
    out.append(("modulate",))
    beside = [[] for _ in range(12 * 4)]
    beside[0].append(("alpha", 0))
    beside[1].append(("alpha", 1))
    beside[3].append(("alpha", 2))
    n = 0
    for i in range(12):
        for q in range(2 if i in (3, 9) else 1):
            m = 2 + n // 4
            for k in range(4):
                beside[4 * i + (2 * q + k // 2 if i in (3, 9) else k)].append(("ada", m, n % 4, k))
            if n % 4 == 3:
                beside[min(4 * i + 2 * q + 3, 4 * i + 3)].append(("mod", m))
            n += 1
    for j in range(ATT + 3):
        beside[4 * ATT_FROM + j].append(("att", j))
    beside[28].append(("kdec",))
    for j in range(5):
        if j:
            beside[40 + j].append(("glao", j - 1))
        if j < 4:
            beside[40 + j].append(("kv", j))
    beside[46] += [("silu", 0)]
    beside[47] += [("glanorm", 0)]
    for j in range(48):
        out.append(("proj", j // 4, j // 2 % 2, j % 2))
        out += beside[j]
    for u in range(4):
        if u == 0:
            out += [("silu", 1), ("wout", 0, 0), ("glanorm", 1), ("wout", 0, 1)]
        else:
            out += [("wout", u, 0), ("wout", u, 1)]
        if u < 2:
            out += [("ada", 5, 2 + u, k) for k in range(4)]
        if u == 1:
            out.append(("mod", 5))
    return out


def build(nc, a, out):
    f32, i32, u32 = mybir.dt.float32, mybir.dt.int32, mybir.dt.uint32
    ALU, ACT, AX = mybir.AluOpType, mybir.ActivationFunctionType, mybir.AxisListType
    SCHED = schedule()
    STREAM = []
    for s in SCHED:
        unit = ("ada", 4 * s[1] + s[2]) if s[0] == "ada" else s[:2]
        if s[0] in ("ada", "proj", "wout") and unit not in STREAM:
            STREAM.append(unit)
    SLOT = {s: (n % 3, n // 3) for n, s in enumerate(STREAM)}

    ctx = ExitStack()
    with ctx:
        def sb(name, shape, dt=f32):
            return ctx.enter_context(nc.sbuf_tensor(name, shape, dt))

        def sem(name):
            return ctx.enter_context(nc.semaphore(name))

        def dram(name, shape, dt=f32):
            return nc.dram_tensor(name, shape, dt, kind="Internal")

        stream = sb("stream", [P, 5, UNIT])
        resid = sb("resid", [P, TT, D])
        acc = sb("acc", [P, D])
        wk = sb("wk", [P, 4096])
        cst = sb("cst", [P, C_KEEP])
        wr = sb("wr", [P, KD, N_GROUPS + NE])
        br = sb("br", [P, N_GROUPS + NE])
        cc = sb("cc", [P, 3, KD])
        gains = sb("gains", [P, 4, KD])
        bada = sb("bada", [P, 6, KD])
        mod = sb("mod", [P, 6, KD])
        gsub = sb("gsub", [P, 1])
        gnb = sb("gnb", [P, 2])
        lamv = sb("lamv", [P, 8])
        st = sb("st", [P, 96])
        cums = sb("cums", [1, NE + 1], i32)
        rel = sb("rel", [P, TT, 2])
        gates = sb("gates", [P, TT, 2])
        slots = sb("slots", [P, 2 * TT], u32)

        ident = cst[:, C_ID:C_ID + P]
        ones = cst[:, C_ONE:C_ONE + P]

        def view(t, lo, n, c):
            return t[:, lo:lo + n * c].rearrange("p (n c) -> p n c", n=n)
        s3, s4 = stream[:, 3, :], stream[:, 4, :]
        va, vb, rb = view(s3, 0, TT, 1024), view(s3, 2048, TT, 1024), view(s3, 4096, TT, 1024)
        kb, qbT = view(s3, 6144, TT, 512), view(s3, 7168, B_HEADS, S)
        y, x1T = view(s3, 0, TT, D), view(s3, 4096, KD, S)
        hT, qaT, kaT = view(s4, 0, KD, S), view(s4, 4096, A_HEADS, S), view(s4, 6144, A_HEADS, S)
        oTa, oTb = qaT, view(s4, 0, 8, S)
        junk1 = s4[:, 4096:4096 + D]
        gl = resid[:, :, :].rearrange("p t d -> p (t d)")
        kdec, state = view(gl, 0, TT, 512), view(gl, 1024, B_HEADS, B_DV)
        la, tmp = view(gl, 2048, TT, 512), gl[:, 3072:4096]
        bias = view(wk, 0, A_HEADS, S)
        sc, pr = view(wk, 2048, 2, S), view(wk, 2560, 2, S)
        pd, pdT, on = wk[:, 3072:3328], wk[:, 3328:3584], view(wk, 3584, 4, A_DV)
        walpha, balpha, bkt = wk[0:GATE_RANK, 2048:2560], wk[:, 2560:3072], wk[0:N_BUCKETS, 3072:3584]
        zbT = wk[0:GATE_RANK, 3072:3328]
        wzb = view(s3, 7168, KD, GATE_RANK)
        relb, relrow, lamw = wk[0:N_BUCKETS, 3584:3592], wk[0:A_HEADS, 3600:3984], wk[:, 0:256]
        g1b = wk[:, 0:D]
        xe = view(wk, 2048, KD, ROWS)
        ab, eh, hid, ye = wk[:, 2560:2816], view(wk, 2816, 2, 64), view(wk, 2944, 2, 64), wk[:, 3072:3584]
        yo = wk[:, 0:512]
        xp = wk[:, 3584:4096]
        wrf = wr[:, :, :].rearrange("p k n -> p (k n)")
        hit, pick = view(wrf, 0, 2 * TT, ROWS), view(wrf, 256, TT, ROWS)
        g2b = acc[:, :]
        rows = resid[:, :, :].rearrange("p t (q k) -> p t k q", k=KD)
        shw, shs = view(wk, D, KD, 36), wk[:, D + KD * 36:D + (KD + 1) * 36]
        RSHAPES = dict(L=(TT, 36), g8=(TT, 8), gm=(TT, 8), gi=(TT, 8), ng=(TT, 1), gf=(TT, 1), sel=(TT, 4), eg=(TT, 4, 8), es=(TT, 8),
                       em=(TT, 8), ei=(TT, 8), d2=(TT, 1), ef=(TT, 2), ex=(TT, 2), oh=(TT, 2, NE), M=(TT, NE), w=(TT, 2), e2=(TT, 1),
                       gs=(TT, 1), ge=(TT, 4), cnt=(NE,), cmp=(NE, 8), nt=(NE,), zero=(NE,), cum=(NE,), base=(NE,), pos=(TT, NE))

        def R(name):
            lo = sum(int(np.prod(v)) for k, v in RSHAPES.items() if list(RSHAPES).index(k) < list(RSHAPES).index(name))
            shape = RSHAPES[name]
            v = wk[:, D + lo:D + lo + int(np.prod(shape))]
            if name in ("gi", "ei"):
                v = v.bitcast(u32)
            if len(shape) == 2:
                v = v.rearrange("p (a b) -> p a b", a=shape[0])
            if len(shape) == 3:
                v = v.rearrange("p (a b c) -> p a b c", a=shape[0], b=shape[1])
            return v

        def acc_of(m):
            return wk[:, 0:D] if m == 1 else acc[:, :]

        def fin_rows(j):
            return stream[:, 0, D * j:D * j + D]

        ps = ctx.enter_context(nc.psum_tensor("ps", [P, 8, 512], f32))

        def bank(b, *dims):
            if not dims:
                return ps[:, b, :]
            return ps[:, b, 0:dims[0] * dims[1]].rearrange("p (n c) -> p n c", n=dims[0])

        skew = dram("skew", [A_HEADS, P, SKEW])
        gdram = dram("gdram", [2, P, KD])
        ys = dram("ys", [MAX_TILES * ROWS, D])

        c_in, const_in, x_in, par_in, late_in = sem("c_in"), sem("const_in"), sem("x_in"), sem("par_in"), sem("late_in")
        bias_in, skew_out = sem("bias_in"), sem("skew_out")
        unit_in = [sem(f"unit_in{i}") for i in range(3)]
        piece_in = [sem(f"piece_in{i}") for i in range(3)]
        ada_done = sem("ada_done")
        act_c, dve_c, pool_c = sem("act_chain"), sem("dve_chain"), sem("pool_chain")
        relrow_ps, relrow_sb, masked = sem("relrow_ps"), sem("relrow_sb"), sem("masked")
        c_exp, scale_sb = sem("c_exp"), sem("scale_sb")
        xsq, xr, xn = sem("xsq"), sem("xr"), sem("xn")
        xT_ps, xT_sb = sem("xT_ps"), sem("xT_sb")
        mod_ps, mod_sb = sem("mod_ps"), sem("mod_sb")
        hT_dve, hT_act = sem("hT_dve"), sem("hT_act")
        zb_ps, zb_sb, z_ps, z_abs, z_ln, la_sb = sem("zb_ps"), sem("zb_sb"), sem("z_ps"), sem("z_abs"), sem("z_ln"), sem("la_sb")
        suf_ps, suf_exp, kdec_sb = sem("suf_ps"), sem("suf_exp"), sem("kdec_sb")
        proj_ps, proj_sb = sem("proj_ps"), sem("proj_sb")
        s_ps, s_sb, p_max, p_exp, pd_sb = sem("s_ps"), sem("s_sb"), sem("p_max"), sem("p_exp"), sem("pd_sb")
        pdT_ps, pdT_sb, o_ps, o_sq, o_rs, o_sb = sem("pdT_ps"), sem("pdT_sb"), sem("o_ps"), sem("o_sq"), sem("o_rs"), sem("o_sb")
        oT_ps, oT_sb = sem("oT_ps"), sem("oT_sb")
        lam_sum, lam_exp = sem("lam_sum"), sem("lam_exp")
        kv_ps, state_sb, gla_ps = sem("kv_ps"), sem("state_sb"), sem("gla_ps")
        rb_exp, rb_sb, gla_sq, gla_rs, gla_sb = sem("rb_exp"), sem("rb_sb"), sem("gla_sq"), sem("gla_rs"), sem("gla_sb")
        glaT_ps, glaT_sb = sem("glaT_ps"), sem("glaT_sb")
        g_sb, g1_out, g2_out, g1_in, g2_in, xre_in = sem("g_sb"), sem("g1_out"), sem("g2_out"), sem("g1_in"), sem("g2_in"), sem("xre_in")
        y_tot, y_sum, y_rs, x1_sb, x1_sq, x1_rs = sem("y_tot"), sem("y_sum"), sem("y_rs"), sem("x1_sb"), sem("x1_sq"), sem("x1_rs")
        x1T_ps, x1T_dve, x1T_act, shs_sb, shs_ps, wr_sb = sem("x1T_ps"), sem("x1T_dve"), sem("x1T_act"), sem("shs_sb"), sem("shs_ps"), sem("wr_sb")
        pick_sb, pick_c, rows_ps, rows_sb, ys_zero, ye_out, yo_sb = (
            sem("pick_sb"), sem("pick_c"), sem("rows_ps"), sem("rows_sb"), sem("ys_zero"), sem("ye_out"), sem("yo_sb"))
        log_ps, g_max, r_exp1, e_max, r_exp2, m_sb, rank_ps, route_sb = (
            sem("log_ps"), sem("g_max"), sem("r_exp1"), sem("e_max"), sem("r_exp2"), sem("m_sb"), sem("rank_ps"),
            sem("route_sb"))
        w1_in, w3_in, w2_in = [sem("w1_in0"), sem("w1_in1")], [[sem(f"w3_in{b}_half{j}") for j in range(2)] for b in range(2)], [sem("w2_in_half0"), sem("w2_in_half1")]
        xe_ps, xe_t, xe_sb, ab_ps, ab_sb, h_ps, h_exp, h_t, hid_sb, ye_ps, ye_sb = (
            sem("xe_ps"), sem("xe_t"), sem("xe_sb"), sem("ab_ps"), sem("ab_sb"), sem("h_ps"), sem("h_exp"), sem("h_t"),
            sem("hid_sb"), sem("ye_ps"), sem("ye_sb"))
        fin_rows_in, fin_sum, fin_sq, fin_rs, fin_sb, fin_out = (
            [sem("fin_rows_in0"), sem("fin_rows_in1")], sem("fin_sum"), sem("fin_sq"), sem("fin_rs"), sem("fin_sb"), sem("fin_out"))

        w_ada = a["w_ada"].rearrange("l (p k) (m n) -> (l p) k m n", p=P, m=6)
        w_in = a["w_in"].rearrange("l (p k) n -> (l p) k n", p=P)
        w_out = a["w_out"].rearrange("l (k p) n -> (l p) k n", p=P)
        w1 = a["w1"].rearrange("l e (p k) f -> (l e) p (k f)", p=P)
        w3 = a["w3"].rearrange("l e (p k) f -> (l e) p (k f)", p=P)
        w2 = a["w2"].rearrange("l e (k p) n -> (l e) p k n", p=P)
        x_d = a["x"].rearrange("b (t p) d -> (b p) t d", p=P)
        out_d = out.rearrange("b (t p) d -> (b p) t d", p=P)

        def row_bcast(ap, n):
            return bass.AP(tensor=ap.tensor, offset=ap.offset, ap=[[0, P], [1, n]])

        def DECAY(n, h):
            return 32 + 8 * (n // 2) + 2 * h + n % 2

        def vec(ap):
            return ap.rearrange("l (p k) -> (l p) k", p=P)

        params = [
            (relb, a["rel_bias"][:, :]),
            (lamw[:, 0:64], row_bcast(a["lam_q1"], 64)), (lamw[:, 64:128], row_bcast(a["lam_k1"], 64)),
            (lamw[:, 128:192], row_bcast(a["lam_q2"], 64)), (lamw[:, 192:256], row_bcast(a["lam_k2"], 64)),
            (gsub[:, :], a["g_sub_a"].rearrange("l (p o) -> (l p) o", o=1)),
            (bada[:, :, :], a["b_ada"].rearrange("l (m p k) -> (l p) m k", m=6, p=P)),
            (gains[:, 0, :], vec(a["g_pre_mix"])), (gains[:, 1, :], vec(a["g_post_mix"])),
            (gains[:, 2, :], vec(a["g_pre_ffn"])), (gains[:, 3, :], vec(a["g_post_ffn"])),
            (wzb[:, :, :], w_in[:, :, D_IN - GATE_RANK:D_IN]),
            (gnb[:, 0:1], a["g_norm_b"][:, 0:P].rearrange("l (p o) -> (l p) o", o=1)),
            (gnb[:, 1:2], a["g_norm_b"][:, P:2 * P].rearrange("l (p o) -> (l p) o", o=1)),
            (wr[:, :, 0:N_GROUPS], a["w_router_g"].rearrange("l (p k) n -> (l p) k n", p=P)),
            (wr[:, :, N_GROUPS:N_GROUPS + NE], a["w_router_e"].rearrange("l (p k) n -> (l p) k n", p=P)),
            (br[:, 0:N_GROUPS], row_bcast(a["b_router_g"], N_GROUPS)), (br[:, N_GROUPS:N_GROUPS + NE], row_bcast(a["b_router_e"], NE)),
        ]

        W1 = [stream[:, 0, :], stream[:, 1, :]]
        W3 = [stream[:, 2, :], stream[:, 3, :]]
        W2v = stream[:, 4, :].rearrange("p (k n) -> p k n", k=4)

        def half(w, j):
            return w[:, UNIT // 2 * j:UNIT // 2 * (j + 1)]

        def w_unit(e, t):
            return t[bass.ds(e, 1)].rearrange("e p n -> (e p) n")

        block = ctx.enter_context(nc.Block())

        @block.sync
        def _(sp):
            def wait_used(item):
                if item[0] == "ada":
                    sp.wait_ge(ada_done, item[1] + 1)
                elif item[0] == "proj":
                    sp.wait_ge(proj_ps, 2 * item[1] + 2)
                else:
                    sp.wait_ge(proj_ps, 24 + 2 * item[1] + 2)

            for n, item in enumerate(STREAM):
                s = n % 3
                if n >= 3:
                    wait_used(STREAM[n - 3])
                dst = stream[:, s, :]
                if item[0] == "ada":
                    m, q = item[1] // 4, item[1] % 4
                    if (m, q) == (1, 3):
                        for k in range(4):
                            sp.dma_start(dst.rearrange("p (k n) -> p k n", k=4)[:, k, :], w_ada[:, 4 * q + k, m, :]).then_inc(piece_in[k] if k < 3 else unit_in[s], 16)
                        continue
                    sp.dma_start(dst.rearrange("p (k n) -> p k n", k=4), w_ada[:, 4 * q:4 * q + 4, m, :]).then_inc(unit_in[s], 16)
                elif item[0] == "proj":
                    c = ORDER[item[1]]
                    sp.dma_start(dst.rearrange("p (k n) -> p k n", k=KD), w_in[:, :, 512 * c:512 * c + 512]).then_inc(unit_in[s], 16)
                else:
                    u = item[1]
                    sp.dma_start(dst.rearrange("p (k n) -> p k n", k=KD), w_out[:, :, 512 * u:512 * u + 512]).then_inc(unit_in[s], 16)
            for n in range(len(STREAM) - 3, len(STREAM)):
                wait_used(STREAM[n])
                if n % 3 == 0:
                    sp.dma_start(W1[0], w1[0]).then_inc(w1_in[0], 16)
                elif n % 3 == 1:
                    sp.dma_start(W1[1], w1[1]).then_inc(w1_in[1], 16)
                else:
                    for j in range(2):
                        sp.dma_start(half(W3[0], j), half(w3[0], j)).then_inc(w3_in[0][j], 16)
            sp.wait_ge(proj_ps, 24 + 8)
            sp.wait_ge(x1_sq, 1)
            for j in range(2):
                sp.dma_start(W2v[:, 2 * j:2 * j + 2, :], w2[0][:, 2 * j:2 * j + 2, :]).then_inc(w2_in[j], 16)
            sp.wait_ge(log_ps, 1)
            for j in range(2):
                sp.dma_start(half(W3[1], j), half(w3[1], j)).then_inc(w3_in[1][j], 16)
            sp.wait_ge(route_sb, 1)

            def load_w1(e, b):
                done = sp.value_load(cums[0:1, bass.ds(e - 1, 1)], min_val=1, max_val=MAX_TILES)
                sp.wait_ge(ab_ps, done)
                sp.dma_start(W1[b], w_unit(e, w1)).then_inc(w1_in[b], 16)

            def load_w3(e, b):
                for j in range(2):
                    sp.dma_start(half(W3[b], j), half(w_unit(e, w3), j)).then_inc(w3_in[b][j], 16)

            def load_w2(e):
                done = sp.value_load(cums[0:1, bass.ds(e, 1)], min_val=1, max_val=MAX_TILES)
                sp.wait_ge(ye_ps, done)
                src = w2[bass.ds(e, 1)].rearrange("e p k n -> (e p) k n")
                for j in range(2):
                    sp.dma_start(W2v[:, 2 * j:2 * j + 2, :], src[:, 2 * j:2 * j + 2, :]).then_inc(w2_in[j], 16)

            load_w1(2, 0)
            load_w2(1)
            load_w3(2, 0)
            load_w2(2)
            load_w1(3, 1)
            load_w3(3, 1)
            load_w2(3)
            sp.wait_ge(g2_out, 16)
            sp.wait_ge(x1_sq, TT)
            sp.dma_start(g2b, row_bcast(gdram[1, :, :], D)).then_inc(g2_in, 16)
            with sp.Fori(2, NE // 2) as i:
                for b in range(2):
                    load_w1(2 * i + b, b)
                    load_w3(2 * i + b, b)
                    load_w2(2 * i + b)

        @block.tensor
        def _(pe):
            pe.wait_ge(const_in, 32)
            pe.wait_ge(par_in, 16 * len(params))
            nc.tensor.matmul(bank(4)[0:A_HEADS, 0:384], relb, bkt[:, 0:384], start=True, stop=True).then_inc(relrow_ps, 1)
            fill = 0
            for item in SCHED:
                kind = item[0]
                if kind == "mod":
                    m = item[1]
                    pe.wait_ge(ada_done, 4 * (m + 1))
                    for k in range(KD):
                        last = nc.tensor.matmul(bank(6)[:, 16 * m + k:16 * m + k + 1], acc_of(m)[:, k::KD], ones[:, 0:1], start=True, stop=True)
                    last.then_inc(mod_ps, 1)
                elif kind == "prepare":
                    for t in range(TT):
                        pe.wait_ge(xn, t + 1)
                        for j in range(4):
                            if t:
                                pe.wait_ge(xT_sb, j + 1)
                            for k in range(4):
                                last = nc.tensor.transpose(bank(j, 4, P)[:, k, :], resid[:, t, 4 * j + k::KD], ident)
                            last.then_inc(xT_ps, 1)
                elif kind == "alpha":
                    if item[1] == 0:
                        for k in range(KD):
                            last = nc.tensor.matmul(bank(5)[0:GATE_RANK, 0:S], wzb[:, k, :], hT[:, k, :], start=(k == 0), stop=(k == KD - 1))
                        last.then_inc(zb_ps, 1)
                    elif item[1] == 1:
                        pe.wait_ge(late_in, 32)
                        pe.wait_ge(zb_sb, 1)
                        for t in range(TT):
                            nc.tensor.matmul(bank(2 + t), zbT[:, P * t:P * t + P], walpha, start=True, stop=True).then_inc(z_ps, 1)
                    else:
                        for t in range(TT):
                            pe.wait_ge(la_sb, t + 1)
                            nc.tensor.matmul(bank(4 + t), cst[:, C_SUF:C_SUF + P], la[:, t, :], start=True, stop=True).then_inc(suf_ps, 1)
                        for t in range(TT):
                            for h in range(B_HEADS):
                                last = nc.tensor.matmul(bank(7)[:, 8 * t + 2 * h:8 * t + 2 * h + 2], la[:, t, P * h:P * h + P],
                                                        cst[:, C_HALF:C_HALF + 2], start=True, stop=True)
                        last.then_inc(suf_ps, 1)
                elif kind == "proj":
                    _, i, half, part = item
                    c = ORDER[i]
                    s, n = SLOT[("proj", i)]
                    w = stream[:, s, :].rearrange("p (k n) -> p k n", k=KD)
                    if part == 0:
                        if half == 0:
                            pe.wait_ge(unit_in[s], 16 * (n + 1))
                        if fill >= 2:
                            pe.wait_ge(proj_sb, fill - 1)
                    if c in TRANSPOSED:
                        lo = 256 * half + P * part
                        for k in range(KD):
                            if fill == 0 and part == 0:
                                pe.wait_ge(hT_act if k % 2 else hT_dve, k // 2 + 1)
                            last = nc.tensor.matmul(bank(fill % 2, 2, S)[:, part, :], w[:, k, lo:lo + P], hT[:, k, :], start=(k == 0), stop=(k == KD - 1))
                    else:
                        for k in range(8 * part, 8 * part + 8):
                            last = nc.tensor.matmul(bank(fill % 2), hT[:, k, P * half:P * half + P], w[:, k, :], start=(k == 0), stop=(k == KD - 1))
                    if part == 1:
                        last.then_inc(proj_ps, 1)
                        fill += 1
                elif kind == "att":
                    i = item[1]
                    if i < ATT:
                        h, b = head_block(i)
                        nk = P * (b + 1)
                        if i == 0:
                            pe.wait_ge(suf_exp, 3)
                        else:
                            pe.wait_ge(s_sb, i)
                        pe.wait_ge(proj_sb, HEADS_READY[h // 4])
                        for m in range(2):
                            r = slice(A_DK * m, A_DK * m + A_DK)
                            last = nc.tensor.matmul(ps[:, 2 + m, 0:nk], qaT[r, h, P * b:P * b + P], kaT[r, h, 0:nk], start=True, stop=True)
                        last.then_inc(s_ps, 1)
                    if 2 <= i < ATT + 2:
                        j = i - 2
                        h, b = head_block(j)
                        pe.wait_ge(pdT_sb, j + 1)
                        if j >= 4 and j % 4 == 0:
                            pe.wait_ge(o_sb, j // 4)
                        for kt in range(b + 1):
                            last = nc.tensor.matmul(bank(4, 4, A_DV)[:, j % 4, :], pdT[:, P * kt:P * kt + P], va[:, kt, A_DV * h:A_DV * h + A_DV],
                                                    start=(kt == 0), stop=(kt == b))
                        last.then_inc(o_ps, 1)
                    if 1 <= i < ATT + 1:
                        j = i - 1
                        _, b = head_block(j)
                        pe.wait_ge(pd_sb, j + 1)
                        for kt in range(b + 1):
                            last = nc.tensor.transpose(bank(7)[:, P * kt:P * kt + P], pd[:, P * kt:P * kt + P], ident)
                        last.then_inc(pdT_ps, 1)
                    if i % 4 == 2 and i >= 6:
                        g = (i - 6) // 4
                        pe.wait_ge(o_sb, g + 1)
                        for j in range(4):
                            last = nc.tensor.transpose(bank(5, 4, P)[:, j, :], on[:, j, :], ident)
                        last.then_inc(oT_ps, 1)
                elif kind == "kv":
                    n = item[1]
                    t, lo = n // 2, CHUNK * (n % 2)
                    if n == 0:
                        pe.wait_ge(kdec_sb, 1)
                        pe.wait_ge(mod_sb, 5)
                        pe.wait_ge(oT_sb, 4)
                        pe.wait_ge(proj_sb, 20)
                    for h in range(B_HEADS):
                        last = nc.tensor.matmul(bank(6 + h // 2, 2, B_DV)[:, h % 2, :], kdec[lo:lo + CHUNK, t, P * h:P * h + P],
                                                vb[lo:lo + CHUNK, t, B_DV * h:B_DV * h + B_DV], start=True, stop=True)
                    last.then_inc(kv_ps, 1)
                elif kind == "glao":
                    n = item[1]
                    t, lo = n // 2, CHUNK * (n % 2)
                    pe.wait_ge(state_sb, n + 1)
                    for h in range(B_HEADS):
                        last = nc.tensor.matmul(bank(2 + 2 * t + h // 2, 2, B_DV)[lo:lo + CHUNK, h % 2, :], qbT[:, h, CHUNK * n:CHUNK * n + CHUNK],
                                                state[:, h, :], start=True, stop=True)
                    last.then_inc(gla_ps, 1)
                elif kind == "glanorm":
                    t = item[1]
                    pe.wait_ge(gla_sb, t + 1)
                    for j in range(2):
                        if t:
                            pe.wait_ge(glaT_sb, j + 1)
                        for k in range(4):
                            last = nc.tensor.transpose(bank(6 + j, 4, P)[:, k, :], rb[:, t, P * (4 * j + k):P * (4 * j + k) + P], ident)
                        last.then_inc(glaT_ps, 1)
                elif kind == "wout":
                    _, u, t = item
                    s, n = SLOT[("wout", u)]
                    w = stream[:, s, :].rearrange("p (k n) -> p k n", k=KD)
                    if t == 0:
                        pe.wait_ge(unit_in[s], 16 * (n + 1))
                    if u == 0:
                        pe.wait_ge(glaT_sb, 2 * t + 2)
                    if (u, t) == (2, 0):
                        pe.wait_ge(shs_sb, 1)
                        nc.tensor.matmul(bank(5)[:, 0:36], ones, shs, start=True, stop=True).then_inc(shs_ps, 1)
                    pe.wait_ge(proj_sb, fill - 1)
                    for k in range(KD):
                        lhs = (oTa if k < 8 else oTb)[:, k % 8, P * t:P * t + P]
                        last = nc.tensor.matmul(bank(fill % 2), lhs, w[:, k, :], start=(k == 0), stop=(k == KD - 1))
                    last.then_inc(proj_ps, 1)
                    fill += 1

            for t in range(TT):
                pe.wait_ge(x1_sb, t + 1)
                if t:
                    pe.wait_ge(proj_sb, 24 + 8)
                for j in range(4):
                    for k in range(4):
                        last = nc.tensor.transpose(bank(X1T_BANK[t][j], 4, P)[:, k, :], rows[:, t, 4 * j + k, :], ident)
                    last.then_inc(x1T_ps, 1)
                pe.wait_ge(wr_sb, 1)
                pe.wait_ge(x1T_act, 4 if t == 0 else 6)
                if t:
                    pe.wait_ge(x1T_dve, 2)
                for k in range(KD):
                    last = nc.tensor.matmul(bank(2, TT, 36)[:, t, :], x1T[:, k, P * t:P * t + P], wr[:, k, :], start=(k == 0), stop=(k == KD - 1))
            last.then_inc(log_ps, 1)
            pe.wait_ge(m_sb, 1)
            rk = bank(1, 4, NE)
            lt = cst[:, C_LT:C_LT + P]
            nc.tensor.matmul(rk[:, 0, :], lt, R("M")[:, 0, :], start=True, stop=True)
            nc.tensor.matmul(rk[:, 1, :], ones, R("M")[:, 0, :], start=True, stop=False)
            nc.tensor.matmul(rk[:, 1, :], lt, R("M")[:, 1, :], start=False, stop=True)
            nc.tensor.matmul(rk[:, 2, :], ones, R("M")[:, 0, :], start=True, stop=False)
            nc.tensor.matmul(rk[:, 2, :], ones, R("M")[:, 1, :], start=False, stop=True).then_inc(rank_ps, 1)

            def pick_rows():
                for t2 in range(TT):
                    for g in range(4):
                        last = nc.tensor.matmul(bank(0)[32 * g:32 * g + 32, :], pick[:, t2, :], rows[:, t2, 4 * g:4 * g + 4, :], start=(t2 == 0), stop=(t2 == TT - 1))
                last.then_inc(rows_ps, 1)

            def turn_rows():
                for j in range(4):
                    last = nc.tensor.transpose(bank(4, 4, P)[:, j, :], xp[:, P * j:P * j + P], ident)
                last.then_inc(xe_ps, 1)

            pe.wait_ge(pick_sb, 1)
            pick_rows()
            pe.wait_ge(rows_sb, 1)
            turn_rows()
            pe.wait_ge(route_sb, 1)
            with pe.Fori(0, NE // 2) as i:
                for b in range(2):
                    lo = pe.value_load(cums[0:1, bass.ds(2 * i + b, 1)], min_val=0, max_val=MAX_TILES)
                    hi = pe.value_load(cums[0:1, bass.ds(2 * i + b + 1, 1)], min_val=1, max_val=MAX_TILES)
                    pe.wait_ge(w1_in[b], 16 * i + 16)
                    pe.wait_ge(w3_in[b][0], 16 * i + 16)
                    pe.nop(nofuse=True)
                    a13 = [W1[b].rearrange("p (k f) -> p k f", k=KD), W3[b].rearrange("p (k f) -> p k f", k=KD)]
                    with pe.Fori(lo, hi) as t:
                        pe.wait_ge(xe_sb, t + 1)
                        for k in range(KD):
                            if k == KD // 2:
                                pe.wait_ge(w3_in[b][1], 16 * i + 16)
                            for g in range(4):
                                last = nc.tensor.matmul(bank(1)[32 * g:32 * g + 32, 0:256], xe[:, k, :], a13[g // 2][:, k, 256 * (g % 2):256 * (g % 2) + 256],
                                                        start=(k == 0), stop=(k == KD - 1))
                        last.then_inc(ab_ps, 1)
                        pe.wait_ge(pick_sb, t + 2)
                        pick_rows()
                        pe.wait_ge(ab_sb, t + 1)
                        for c in range(2):
                            last = nc.tensor.transpose(bank(2, 2, P)[:, c, :], ab[:, P * c:P * c + P], ident)
                        last.then_inc(h_ps, 1)
                        pe.wait_ge(rows_sb, t + 2)
                        turn_rows()
                        pe.wait_ge(ye_sb, t + 1)
                        pe.wait_ge(hid_sb, t + 1)
                        for k in range(4):
                            if k % 2 == 0:
                                pe.wait_ge(w2_in[k // 2], 32 * i + 16 * b + 16)
                            for g in range(4):
                                last = nc.tensor.matmul(bank(3)[32 * g:32 * g + 32, :], hid[:, k % 2, 32 * (k // 2):32 * (k // 2) + 32], W2v[:, k, 512 * g:512 * g + 512],
                                                        start=(k == 0), stop=(k == 3))
                        last.then_inc(ye_ps, 1)

        @block.vector
        def _(dve):
            n_c = [0]

            def step(ins):
                ins.then_inc(dve_c, 1)
                n_c[0] += 1

            def settle():
                dve.wait_ge(dve_c, n_c[0])

            def link(ins):
                step(ins)
                settle()

            V = nc.vector
            dve.wait_ge(c_exp, 1)
            link(V.tensor_scalar_add(cc[:, 2, :], cc[:, 1, :], 1.0))
            link(V.reciprocal(cc[:, 2, :], cc[:, 2, :]))
            link(V.tensor_tensor(cc[:, 2, :], cc[:, 2, :], cc[:, 0, :], ALU.mult))

            def prepare():
                dve.wait_ge(par_in, 16 * len(params))
                lw = lamw.rearrange("p (n c) -> p n c", n=4)
                link(V.tensor_tensor(lw[:, 0:4:2, :], lw[:, 0:4:2, :], lw[:, 1:4:2, :], ALU.mult))
                V.tensor_reduce(lamv[:, 0:2], lw[:, 0:4:2, :], axis=AX.X, op=ALU.add).then_inc(lam_sum, 1)
                dve.wait_ge(lam_exp, 1)
                link(V.tensor_tensor(lamv[:, 4:5], lamv[:, 3:4], lamv[:, 2:3], ALU.subtract))
                link(V.tensor_scalar_add(lamv[:, 5:6], lamv[:, 4:5], -LAM_INIT))
                link(V.tensor_scalar(gsub[:, :], gsub[:, :], 1.0 - LAM_INIT, None, ALU.mult))
                dve.wait_ge(relrow_ps, 1)
                V.tensor_copy(relrow, bank(4)[0:A_HEADS, 0:384]).then_inc(relrow_sb, 1)
                for t in range(TT):
                    dve.wait_ge(xr, t + 1)
                    V.tensor_scalar(resid[:, t, :], resid[:, t, :], st[:, 2 + t:3 + t], None, ALU.mult).then_inc(xn, 1)

            def accumulate(m, q, k):
                s, n = SLOT[("ada", 4 * m + q)]
                w = stream[:, s, :].rearrange("p (k n) -> p k n", k=4)
                if (m, q) == (1, 3) and k < 3:
                    dve.wait_ge(piece_in[k], 16)
                elif k == (3 if (m, q) == (1, 3) else 0):
                    dve.wait_ge(unit_in[s], 16 * (n + 1))
                if q == 0 and k == 0 and m > 1:
                    dve.wait_ge(mod_ps, m)
                acc_m = acc_of(m)
                col = cc[:, 2, 4 * q + k:4 * q + k + 1]
                if 4 * q + k == 0:
                    ins = V.tensor_scalar(acc_m, w[:, k, :], col, None, ALU.mult)
                else:
                    ins = V.scalar_tensor_tensor(out=acc_m, in0=w[:, k, :], scalar=col, in1=acc_m, op0=ALU.mult, op1=ALU.add)
                if k < 3:
                    link(ins)
                else:
                    ins.then_inc(ada_done, 1)
                    dve.wait_ge(ada_done, 4 * m + q + 1)

            def gain_y(u, t):
                dve.wait_ge(proj_sb, 24 + 2 * u + t + 1)
                dve.wait_ge(g1_in, 16)
                c = slice(512 * u, 512 * u + 512)
                link(V.tensor_tensor(y[:, t, c], y[:, t, c], g1b[:, c], ALU.mult))

            def total_of(t):
                dve.wait_ge(y_sum, 7 + t)
                V.tensor_reduce(st[:, 56 + t:57 + t], st[:, 48 + 4 * t:52 + 4 * t], axis=AX.X, op=ALU.add).then_inc(y_tot, 1)

            for item in SCHED:
                kind = item[0]
                if kind == "ada":
                    accumulate(*item[1:])
                elif kind == "wout":
                    _, u, t = item
                    if t:
                        continue
                    if u == 0:
                        link(V.tensor_tensor(shw, wr[:, :, :], mod[:, 3, :].unsqueeze(2).to_broadcast((P, KD, 36)), ALU.mult))
                        V.tensor_reduce(shs, shw.rearrange("p k n -> p n k"), axis=AX.X, op=ALU.add).then_inc(shs_sb, 1)
                        V.tensor_tensor(wr[:, :, :], wr[:, :, :], mod[:, 4, :].unsqueeze(2).to_broadcast((P, KD, 36)), ALU.mult).then_inc(wr_sb, 1)
                    else:
                        for j in range(TT):
                            gain_y(u - 1, j)
                    if u == 3:
                        dve.wait_ge(shs_ps, 1)
                        link(V.tensor_tensor(br[:, :], br[:, :], bank(5)[:, 0:36], ALU.add))
                elif kind == "prepare":
                    prepare()
                elif kind == "mod":
                    m = item[1]
                    j = m
                    dve.wait_ge(mod_ps, j + 1)
                    V.tensor_tensor(mod[:, m, :], bank(6)[:, 16 * m:16 * m + 16], bada[:, m, :], ALU.add).then_inc(mod_sb, 1)
                    dve.wait_ge(mod_sb, j + 1)
                    if m == 1 or m == 4:
                        V.scalar_tensor_tensor(out=mod[:, m, :], in0=mod[:, m, :], scalar=1.0, in1=gains[:, 0 if m == 1 else 2, :], op0=ALU.add, op1=ALU.mult).then_inc(scale_sb, 1)
                        dve.wait_ge(scale_sb, 1 if m == 1 else 2)
                    if m == 2 or m == 5:
                        V.tensor_tensor(mod[:, m, :], mod[:, m, :], gains[:, 1 if m == 2 else 3, :], ALU.mult).then_inc(g_sb, 1)
                elif kind == "modulate":
                    dve.wait_ge(xT_sb, 8)
                    for k in range(0, KD, 2):
                        V.tensor_scalar(hT[:, k, :], hT[:, k, :], mod[:, 1, k:k + 1], mod[:, 0, k:k + 1], ALU.mult, ALU.add).then_inc(hT_dve, 1)
                elif kind == "alpha" and item[1] == 1:
                    dve.wait_ge(late_in, 32)
                    for t in range(TT):
                        dve.wait_ge(z_ps, t + 1)
                        link(V.tensor_tensor(la[:, t, :], bank(2 + t), balpha, ALU.add))
                        V.scalar_tensor_tensor(out=tmp[:, 512 * t:512 * t + 512], in0=la[:, t, :], scalar=-1.0, in1=la[:, t, :],
                                               op0=ALU.mult, op1=ALU.max).then_inc(z_abs, 1)
                    for t in range(TT):
                        dve.wait_ge(z_ln, t + 1)
                        V.scalar_tensor_tensor(out=la[:, t, :], in0=la[:, t, :], scalar=0.0, in1=tmp[:, 512 * t:512 * t + 512],
                                               op0=ALU.min, op1=ALU.subtract).then_inc(la_sb, 1)
                elif kind == "kdec":
                    dve.wait_ge(suf_exp, 3)
                    dve.wait_ge(proj_sb, 14)
                    for t in range(TT):
                        ins = V.tensor_tensor(kdec[:, t, :], kdec[:, t, :], kb[:, t, :], ALU.mult)
                    ins.then_inc(kdec_sb, 1)
                elif kind == "att":
                    i = item[1]
                    if i < ATT:
                        h, b = head_block(i)
                        nk = P * (b + 1)
                        if i == 0:
                            dve.wait_ge(masked, 1)
                        dve.wait_ge(s_ps, i + 1)
                        V.scalar_tensor_tensor(out=sc[:, :, 0:nk], in0=ps[:, 2:4, 0:nk], scalar=A_DK ** -0.5,
                                               in1=bias[:, h:h + 1, S - nk:S].to_broadcast((P, 2, nk)), op0=ALU.mult, op1=ALU.add).then_inc(s_sb, 1)
                        dve.wait_ge(s_sb, i + 1)
                        V.tensor_reduce(st[:, 8:10], sc[:, :, 0:nk], axis=AX.X, op=ALU.max, negate=True).then_inc(p_max, 1)
                        dve.wait_ge(p_exp, i + 1)
                        if i:
                            dve.wait_ge(pdT_ps, i)
                        link(V.reciprocal(st[:, 12:14], st[:, 10:12]))
                        link(V.tensor_tensor(st[:, 14:15], st[:, 13:14], lamv[:, 5:6], ALU.mult))
                        link(V.tensor_scalar(pr[:, 0, 0:nk], pr[:, 0, 0:nk], st[:, 12:13], None, ALU.mult))
                        V.scalar_tensor_tensor(out=pd[:, 0:nk], in0=pr[:, 1, 0:nk], scalar=st[:, 14:15], in1=pr[:, 0, 0:nk],
                                               op0=ALU.mult, op1=ALU.add).then_inc(pd_sb, 1)
                    if i % 4 == 1 and i >= 5:
                        g = (i - 5) // 4
                        dve.wait_ge(o_rs, g + 1)
                        if g:
                            dve.wait_ge(oT_ps, g)
                        V.tensor_tensor(on, bank(4, 4, A_DV), st[:, 20:24].unsqueeze(2).to_broadcast((P, 4, A_DV)), ALU.mult).then_inc(o_sb, 1)
                    if i % 4 == 2 and i >= 6:
                        g = (i - 6) // 4
                        dve.wait_ge(oT_ps, g + 1)
                        V.tensor_scalar(oTa[:, 4 * (g // 2):4 * (g // 2) + 4, P * (g % 2):P * (g % 2) + P], bank(5, 4, P), gsub[:, 0:1], None,
                                        ALU.mult).then_inc(oT_sb, 1)
                elif kind == "silu":
                    t = item[1]
                    dve.wait_ge(rb_exp, t + 1)
                    link(V.tensor_scalar_add(tmp, tmp, 1.0))
                    link(V.reciprocal(tmp, tmp))
                    V.tensor_tensor(rb[:, t, :], rb[:, t, :], tmp, ALU.mult).then_inc(rb_sb, 1)
                elif kind == "kv":
                    n = item[1]
                    dve.wait_ge(kv_ps, n + 1)
                    for h in range(B_HEADS):
                        kv = bank(6 + h // 2, 2, B_DV)[:, h % 2, :]
                        if n == 0:
                            ins = V.tensor_copy(state[:, h, :], kv)
                        else:
                            ins = V.scalar_tensor_tensor(out=state[:, h, :], in0=state[:, h, :], scalar=st[:, DECAY(n, h):DECAY(n, h) + 1], in1=kv,
                                                         op0=ALU.mult, op1=ALU.add)
                    ins.then_inc(state_sb, 1)
                    dve.wait_ge(state_sb, n + 1)
                elif kind == "glanorm":
                    t = item[1]
                    dve.wait_ge(gla_rs, t + 1)
                    dve.wait_ge(rb_sb, t + 1)
                    for h in range(B_HEADS):
                        r = rb[:, t, B_DV * h:B_DV * h + B_DV]
                        ins = V.scalar_tensor_tensor(out=r, in0=bank(2 + 2 * t + h // 2, 2, B_DV)[:, h % 2, :], scalar=st[:, 28 + h:29 + h], in1=r,
                                                     op0=ALU.mult, op1=ALU.mult)
                    ins.then_inc(gla_sb, 1)

            gain_y(3, 0)
            for t in range(TT):
                total_of(t)
                if t:
                    gain_y(3, 1)
                dve.wait_ge(y_rs, t + 1)
                dve.wait_ge(xre_in, 16)
                V.scalar_tensor_tensor(out=resid[:, t, :], in0=y[:, t, :], scalar=st[:, 58 + t:59 + t], in1=resid[:, t, :], op0=ALU.mult, op1=ALU.add).then_inc(x1_sb, 1)
            for j in (0, 2):
                dve.wait_ge(x1T_ps, 4 + j + 1)
                V.tensor_copy(x1T[:, 4 * j:4 * j + 4, P:2 * P], bank(X1T_BANK[1][j], 4, P)).then_inc(x1T_dve, 1)

            dve.wait_ge(log_ps, 1)
            dve.wait_ge(x1_rs, TT)
            L, g8 = R("L"), R("g8")
            link(V.memset(g8, -3.0e38))
            for t in range(TT):
                link(V.scalar_tensor_tensor(out=L[:, t, :], in0=bank(2, TT, 36)[:, t, :], scalar=st[:, 62 + t:63 + t], in1=br[:, :], op0=ALU.mult, op1=ALU.add))
            link(V.tensor_copy(g8[:, :, 0:4], L[:, :, 0:4]))
            for t in range(TT):
                link(V.max(R("gm")[:, t, :], g8[:, t, :]))
                link(V.max_index(R("gi")[:, t, :], R("gm")[:, t, :], g8[:, t, :]))
            V.tensor_scalar(R("ng"), R("gm")[:, :, 0:1], -1.0, None, ALU.mult).then_inc(g_max, 1)
            link(V.tensor_copy(R("gf"), R("gi")[:, :, 0:1]))
            link(V.tensor_tensor(R("sel"), cst[:, C_IOTA:C_IOTA + 4].unsqueeze(1).to_broadcast((P, TT, 4)), R("gf").to_broadcast((P, TT, 4)), ALU.is_equal))
            link(V.tensor_tensor(R("eg"), L[:, :, 4:36].rearrange("p t (g e) -> p t g e", g=4), R("sel").unsqueeze(3).to_broadcast((P, TT, 4, 8)), ALU.mult))
            link(V.tensor_reduce(R("es"), R("eg").rearrange("p t g e -> p t e g"), axis=AX.X, op=ALU.add))
            for t in range(TT):
                link(V.max(R("em")[:, t, :], R("es")[:, t, :]))
                link(V.max_index(R("ei")[:, t, :], R("em")[:, t, :], R("es")[:, t, :]))
            V.tensor_tensor(R("d2"), R("em")[:, :, 1:2], R("em")[:, :, 0:1], ALU.subtract).then_inc(e_max, 1)
            link(V.tensor_copy(R("ef"), R("ei")[:, :, 0:2]))
            link(V.scalar_tensor_tensor(out=R("ex"), in0=R("gf").to_broadcast((P, TT, 2)), scalar=float(PER_GROUP), in1=R("ef"), op0=ALU.mult, op1=ALU.add))
            link(V.tensor_tensor(R("oh"), cst[:, C_IOTA:C_IOTA + NE].unsqueeze(1).unsqueeze(1).to_broadcast((P, TT, 2, NE)),
                                 R("ex").unsqueeze(3).to_broadcast((P, TT, 2, NE)), ALU.is_equal))
            V.tensor_tensor(R("M"), R("oh")[:, :, 0, :], R("oh")[:, :, 1, :], ALU.add).then_inc(m_sb, 1)
            dve.wait_ge(r_exp2, 1)
            link(V.tensor_scalar_add(R("w")[:, :, 0:1], R("e2"), 1.0))
            link(V.tensor_tensor(R("w")[:, :, 0:1], R("w")[:, :, 0:1], R("gs"), ALU.mult))
            link(V.reciprocal(R("w")[:, :, 0:1], R("w")[:, :, 0:1]))
            link(V.tensor_tensor(R("w")[:, :, 1:2], R("w")[:, :, 0:1], R("e2"), ALU.mult))
            dve.wait_ge(rank_ps, 1)
            rk = bank(1, 4, NE)
            link(V.tensor_copy(R("cnt"), rk[:, 2, :]))
            link(V.tensor_tensor(R("cmp"), R("cnt").unsqueeze(2).to_broadcast((P, NE, 8)),
                                 cst[:, C_THR:C_THR + 8].unsqueeze(1).to_broadcast((P, NE, 8)), ALU.is_gt))
            link(V.tensor_reduce(R("nt"), R("cmp"), axis=AX.X, op=ALU.add))
            link(V.tensor_scalar(R("nt"), R("nt"), 1.0, None, ALU.max))
            link(V.memset(R("zero"), 0.0))
            link(V.tensor_tensor_scan(R("cum"), R("nt"), R("zero"), 0.0, ALU.add, ALU.add))
            link(V.memset(cums[0:1, 0:1], 0))
            link(V.tensor_copy(cums[0:1, 1:NE + 1], R("cum")[0:1, :]))
            link(V.tensor_tensor(R("base"), R("cum"), R("nt"), ALU.subtract))
            link(V.scalar_tensor_tensor(out=R("pos"), in0=R("base").unsqueeze(1).to_broadcast((P, TT, NE)), scalar=float(ROWS), in1=rk[:, 0:TT, :],
                                        op0=ALU.mult, op1=ALU.add))
            link(V.tensor_tensor(R("oh"), R("oh"), R("pos").unsqueeze(2).to_broadcast((P, TT, 2, NE)), ALU.mult))
            link(V.tensor_reduce(rel[:, :, :], R("oh"), axis=AX.X, op=ALU.add))
            link(V.tensor_copy(slots[:, :], rel[:, :, :].rearrange("p t j -> p (t j)")))
            V.tensor_copy(gates[:, :, :], R("w")).then_inc(route_sb, 1)
            dve.wait_ge(route_sb, 1)

            total = dve.value_load(cums[0:1, NE:NE + 1], min_val=NE, max_val=MAX_TILES)
            iota = cst[:, C_IOTA:C_IOTA + ROWS].unsqueeze(1).to_broadcast((P, 2 * TT, ROWS))
            rel4 = rel[:, :, :].rearrange("p t j -> p (t j)").unsqueeze(2).to_broadcast((P, 2 * TT, ROWS))

            def picks():
                return V.tensor_tensor(hit, iota, rel4, ALU.is_equal)

            def both():
                return V.tensor_tensor(pick, hit[:, 0::2, :], hit[:, 1::2, :], ALU.add)

            def normed():
                return V.tensor_tensor(pick, pick, st[:, 62:64].unsqueeze(2).to_broadcast((P, TT, ROWS)), ALU.mult)

            def by_column(m):
                return mod[:, m, :].rearrange("p (g j) -> p j g", g=4).unsqueeze(3).to_broadcast((P, 4, 4, ROWS))

            xe4 = xe.rearrange("p (g j) r -> p j g r", g=4)
            xe_ps4 = bank(4, 4, P).rearrange("p j (g r) -> p j g r", g=4)

            link(picks())
            link(both())
            normed().then_inc(pick_sb, 1)
            dve.wait_ge(rows_ps, 1)
            V.tensor_copy(xp, bank(0)).then_inc(rows_sb, 1)
            dve.wait_ge(xe_ps, 1)
            V.tensor_tensor(xe4, xe_ps4, by_column(4), ALU.mult).then_inc(xe_t, 1)
            dve.wait_ge(xe_t, 1)
            V.tensor_tensor(xe4, xe4, by_column(3), ALU.add).then_inc(xe_sb, 1)
            with dve.Fori(0, total) as t:
                V.tensor_scalar_add(rel[:, :, :], rel[:, :, :], -float(ROWS)).then_inc(pick_c, 1)
                dve.wait_ge(pick_c, 3 * t + 1)
                picks().then_inc(pick_c, 1)
                dve.wait_ge(pick_c, 3 * t + 2)
                both().then_inc(pick_c, 1)
                dve.wait_ge(pick_c, 3 * t + 3)
                normed().then_inc(pick_sb, 1)
                dve.wait_ge(rows_ps, t + 2)
                V.tensor_copy(xp, bank(0)).then_inc(rows_sb, 1)
                dve.wait_ge(h_exp, t + 1)
                hp = bank(2, 2, P)
                V.tensor_scalar_add(eh, eh, 1.0).then_inc(h_t, 1)
                dve.wait_ge(h_t, 3 * t + 1)
                V.reciprocal(eh, eh).then_inc(h_t, 1)
                dve.wait_ge(h_t, 3 * t + 2)
                V.tensor_tensor(eh, hp[:, :, 0:64], eh, ALU.mult).then_inc(h_t, 1)
                dve.wait_ge(h_t, 3 * t + 3)
                V.tensor_tensor(hid, hp[:, :, 64:128], eh, ALU.mult).then_inc(hid_sb, 1)
                dve.wait_ge(xe_ps, t + 2)
                V.tensor_tensor(xe4, xe_ps4, by_column(4), ALU.mult).then_inc(xe_t, 1)
                dve.wait_ge(xe_t, t + 2)
                V.tensor_tensor(xe4, xe4, by_column(3), ALU.add).then_inc(xe_sb, 1)

            for t in range(TT):
                dve.wait_ge(fin_rows_in[t], 32)
                ga, gb = fin_rows(2 * t), fin_rows(2 * t + 1)
                link(V.tensor_scalar(ga, ga, gates[:, t, 0:1], None, ALU.mult))
                V.scalar_tensor_tensor(out=ga, in0=gb, scalar=gates[:, t, 1:2], in1=ga, op0=ALU.mult, op1=ALU.add).then_inc(fin_sum, 1)
                dve.wait_ge(fin_sq, t + 1)
                dve.wait_ge(g2_in, 16)
                link(V.tensor_tensor(ga, ga, g2b, ALU.mult))
            for t in range(TT):
                dve.wait_ge(fin_rs, t + 1)
                V.scalar_tensor_tensor(out=resid[:, t, :], in0=fin_rows(2 * t), scalar=st[:, 70 + t:71 + t], in1=resid[:, t, :], op0=ALU.mult, op1=ALU.add).then_inc(fin_sb, 1)

        @block.scalar
        def _(act):
            n_c = [0]

            def link(ins):
                ins.then_inc(act_c, 1)
                n_c[0] += 1
                act.wait_ge(act_c, n_c[0])

            A = nc.scalar.activation
            act.dma_start(cc[:, 0, :], vec(a["c"])).then_inc(c_in, 16)
            act.dma_start(cst[:, :], a["cst"][:, 0:C_KEEP]).then_inc(const_in, 16)
            act.dma_start(bkt, a["cst"][0:N_BUCKETS, C_BKT:C_ALL]).then_inc(const_in, 16)
            for t in range(TT):
                act.dma_start(resid[:, t, :], x_d[:, t, :]).then_inc(x_in, 16)
            act.wait_ge(c_in, 16)
            A(cc[:, 1, :], cc[:, 0, :], ACT.Exp, scale=-1.0).then_inc(c_exp, 1)
            act.wait_ge(x_in, 32)
            for t in range(TT):
                A(junk1, resid[:, t, :], ACT.Square, accum_out=st[:, t:t + 1]).then_inc(xsq, 1)
                act.wait_ge(xsq, t + 1)
            act.wait_ge(lam_sum, 1)
            A(lamv[:, 2:4], lamv[:, 0:2], ACT.Exp).then_inc(lam_exp, 1)
            for t in range(TT):
                for j in range(4):
                    act.wait_ge(xT_ps, 4 * t + j + 1)
                    A(hT[:, 4 * j:4 * j + 4, P * t:P * t + P], bank(j, 4, P), ACT.Copy).then_inc(xT_sb, 1)
            act.dma_start(walpha, a["w_alpha"][0]).then_inc(late_in, 16)
            act.dma_start(balpha, row_bcast(a["b_alpha"], 512)).then_inc(late_in, 16)

            def squares(t):
                act.wait_ge(x1_sb, t + 1)
                if t:
                    act.wait_ge(mod_ps, 6)
                A(acc[:, :] if t else s4[:, D:2 * D], resid[:, t, :], ACT.Square, accum_out=st[:, 60 + t:61 + t]).then_inc(x1_sq, 1)
                act.wait_ge(x1_sq, t + 1)

            fill = 0
            for item in SCHED:
                kind = item[0]
                if kind == "alpha":
                    if item[1] == 0:
                        act.wait_ge(zb_ps, 1)
                        A(zbT[:, :], bank(5)[0:GATE_RANK, 0:S], ACT.Copy).then_inc(zb_sb, 1)
                    elif item[1] == 1:
                        for t in range(TT):
                            act.wait_ge(z_abs, t + 1)
                            link(A(tmp[:, 512 * t:512 * t + 512], tmp[:, 512 * t:512 * t + 512], ACT.Exp, scale=-1.0))
                            A(tmp[:, 512 * t:512 * t + 512], tmp[:, 512 * t:512 * t + 512], ACT.Ln, bias=ones[:, 0:1]).then_inc(z_ln, 1)
                    else:
                        for t in range(TT):
                            act.wait_ge(suf_ps, t + 1)
                            A(kdec[:, t, :], bank(4 + t), ACT.Exp, scale=1.0 / GATE_TAU).then_inc(suf_exp, 1)
                        act.wait_ge(suf_ps, 3)
                        A(st[:, 32:48], bank(7)[:, 0:16], ACT.Exp, scale=1.0 / GATE_TAU).then_inc(suf_exp, 1)
                elif kind == "modulate":
                    act.wait_ge(scale_sb, 1)
                    act.wait_ge(xT_sb, 8)
                    for k in range(1, KD, 2):
                        A(hT[:, k, :], hT[:, k, :], ACT.Identity, scale=mod[:, 1, k:k + 1], bias=mod[:, 0, k:k + 1]).then_inc(hT_act, 1)
                    act.wait_ge(relrow_sb, 1)
                    rr = bass.AP(tensor=relrow.tensor, offset=relrow.offset, ap=[relrow.ap[0], [0, P], [1, SKEW]])
                    act.dma_start(skew[:, :, :], rr).then_inc(skew_out, 16)
                    act.wait_ge(skew_out, 16)
                    act.dma_start(bias, bass.AP(tensor=skew[:, :, :].tensor, offset=P - 1, ap=[[SKEW - 1, P], [P * SKEW, A_HEADS], [1, S]])).then_inc(bias_in, 16)
                elif kind == "proj":
                    _, i, half, part = item
                    if part == 0:
                        continue
                    c = ORDER[i]
                    act.wait_ge(proj_ps, fill + 1)
                    src = bank(fill % 2)
                    if c in TRANSPOSED:
                        dst = {0: (qaT, 0), 1: (qaT, 4), 2: (kaT, 0), 3: (kaT, 4), 6: (qbT, 0)}[c]
                        dst = dst[0][:, dst[1] + 2 * half:dst[1] + 2 * half + 2, :]
                        src = bank(fill % 2, 2, S)
                        scale = B_DK ** -0.5 if c == 6 else 1.0
                    else:
                        dst = {4: (va, 0), 5: (va, 512), 7: (kb, 0), 8: (vb, 0), 9: (vb, 512), 10: (rb, 0), 11: (rb, 512)}[c]
                        dst = dst[0][:, half, dst[1]:dst[1] + 512]
                        scale = 1.0
                    A(dst, src, ACT.Copy, scale=scale).then_inc(proj_sb, 1)
                    fill += 1
                elif kind == "att":
                    i = item[1]
                    if 1 <= i < ATT + 1:
                        j = i - 1
                        _, b = head_block(j)
                        act.wait_ge(pdT_ps, j + 1)
                        A(pdT[:, 0:P * (b + 1)], bank(7)[:, 0:P * (b + 1)], ACT.Copy).then_inc(pdT_sb, 1)
                    if i < ATT:
                        _, b = head_block(i)
                        nk = P * (b + 1)
                        act.wait_ge(p_max, i + 1)
                        if i:
                            act.wait_ge(pd_sb, i)
                        for m in range(2):
                            ins = A(pr[:, m, 0:nk], sc[:, m, 0:nk], ACT.Exp, bias=st[:, 8 + m:9 + m], accum_out=st[:, 10 + m:11 + m])
                        ins.then_inc(p_exp, 1)
                    if i % 4 == 1 and i >= 5:
                        g = (i - 5) // 4
                        act.wait_ge(o_ps, 4 * g + 4)
                        for j in range(4):
                            ins = A(tmp[:, 0:A_DV], bank(4, 4, A_DV)[:, j, :], ACT.Square, accum_out=st[:, 16 + j:17 + j])
                            if j < 3:
                                link(ins)
                        ins.then_inc(o_sq, 1)
                        act.wait_ge(o_sq, g + 1)
                elif kind == "kv" and item[1] == 0:
                    act.wait_ge(g1_out, 16)
                    act.wait_ge(pd_sb, ATT)
                    act.dma_start(g1b, row_bcast(gdram[0, :, :], D)).then_inc(g1_in, 16)
                elif kind == "silu":
                    t = item[1]
                    act.wait_ge(proj_sb, 22 + t + 1)
                    if t == 0:
                        act.wait_ge(z_ln, 2)
                        act.wait_ge(la_sb, 2)
                    else:
                        act.wait_ge(rb_sb, 1)
                    A(tmp, rb[:, t, :], ACT.Exp, scale=-1.0).then_inc(rb_exp, 1)
                elif kind == "glanorm":
                    t = item[1]
                    act.wait_ge(gla_ps, 2 * t + 2)
                    act.wait_ge(rb_sb, t + 1)
                    if t:
                        act.wait_ge(gla_sb, t)
                    for h in range(B_HEADS):
                        ins = A(tmp[:, 0:B_DV], bank(2 + 2 * t + h // 2, 2, B_DV)[:, h % 2, :], ACT.Square, accum_out=st[:, 24 + h:25 + h])
                        if h < B_HEADS - 1:
                            link(ins)
                    ins.then_inc(gla_sq, 1)
                    act.wait_ge(gla_sq, t + 1)
                    for j in range(2):
                        act.wait_ge(glaT_ps, 2 * t + j + 1)
                        for r in range(2):
                            ins = A(oTb[:, 4 * j + r:4 * j + 4:2, P * t:P * t + P], bank(6 + j, 4, P)[:, r::2, :], ACT.Copy, scale=gnb[:, r:r + 1])
                        ins.then_inc(glaT_sb, 1)
                elif kind == "wout":
                    _, u, t = item
                    if (u, t) == (3, 1):
                        squares(0)
                    act.wait_ge(proj_ps, fill + 1)
                    A(y[:, t, 512 * u:512 * u + 512], bank(fill % 2), ACT.Square, accum_out=st[:, 48 + 4 * t + u:49 + 4 * t + u]).then_inc(y_sum, 1)
                    act.wait_ge(y_sum, 2 * u + t + 1)
                    A(y[:, t, 512 * u:512 * u + 512], bank(fill % 2), ACT.Copy).then_inc(proj_sb, 1)
                    fill += 1
                    if (u, t) == (0, 1):
                        act.dma_start(resid[:, :, :], x_d).then_inc(xre_in, 16)

            for t in range(TT):
                for j in (range(4) if t == 0 else (1, 3)):
                    act.wait_ge(x1T_ps, 4 * t + j + 1)
                    A(x1T[:, 4 * j:4 * j + 4, P * t:P * t + P], bank(X1T_BANK[t][j], 4, P), ACT.Copy).then_inc(x1T_act, 1)
                if t == 0:
                    squares(1)
            act.wait_ge(g_max, 1)
            for t in range(TT):
                link(A(R("ge")[:, t, :], R("L")[:, t, 0:4], ACT.Exp, bias=R("ng")[:, t, :], accum_out=R("gs")[:, t, :]))
            act.wait_ge(e_max, 1)
            A(R("e2"), R("d2"), ACT.Exp).then_inc(r_exp2, 1)

            act.wait_ge(route_sb, 1)
            total = act.value_load(cums[0:1, NE:NE + 1], min_val=NE, max_val=MAX_TILES)

            act.wait_ge(ys_zero, 16)
            with act.Fori(0, total) as t:
                act.wait_ge(ab_ps, t + 1)
                A(ab, bank(1)[:, 0:256], ACT.Copy).then_inc(ab_sb, 1)
                act.wait_ge(h_ps, t + 1)
                A(eh, bank(2, 2, P)[:, :, 0:64], ACT.Exp, scale=-1.0).then_inc(h_exp, 1)
                act.wait_ge(ye_ps, t + 1)
                act.wait_ge(yo_sb, t + 1)
                A(ye, bank(3), ACT.Copy).then_inc(ye_sb, 1)
            for t in range(TT):
                act.wait_ge(fin_sum, t + 1)
                A(fin_rows(2 * t + 1), fin_rows(2 * t), ACT.Square, accum_out=st[:, 66 + t:67 + t]).then_inc(fin_sq, 1)
            for t in range(TT):
                act.wait_ge(fin_sb, t + 1)
                act.dma_start(out_d[:, t, :], resid[:, t, :]).then_inc(fin_out, 16)
            act.wait_ge(fin_out, 32)

        @block.gpsimd
        def _(pool):
            n_c = [0]

            def rms(src, dst, width):
                n = src.shape[1]
                nc.gpsimd.tensor_scalar(dst, src, 1.0 / width, EPS, ALU.mult, ALU.add).then_inc(pool_c, 1)
                n_c[0] += 1
                pool.wait_ge(pool_c, n_c[0])
                return nc.gpsimd.tensor_tensor(dst, dst, cst[:, C_NH:C_NH + n], ALU.pow)

            for dst, src in params:
                pool.dma_start(dst, src).then_inc(par_in, 16)
            pool.wait_ge(const_in, 32)
            for t in range(TT):
                pool.wait_ge(xsq, t + 1)
                rms(st[:, t:t + 1], st[:, 2 + t:3 + t], D).then_inc(xr, 1)
            pool.wait_ge(bias_in, 16)
            pool.memset(bias[0:CHUNK, :, S - CHUNK:S], NEG).then_inc(masked, 1)
            for item in SCHED:
                kind = item[0]
                if kind == "mod" and item[1] == 2:
                    pool.wait_ge(g_sb, 1)
                    pool.dma_start(gdram[0, :, :], mod[:, 2, :]).then_inc(g1_out, 16)
                elif kind == "mod" and item[1] == 5:
                    pool.wait_ge(g_sb, 2)
                    pool.dma_start(gdram[1, :, :], mod[:, 5, :]).then_inc(g2_out, 16)
                elif kind == "att" and item[1] % 4 == 1 and item[1] >= 5:
                    g = (item[1] - 5) // 4
                    pool.wait_ge(o_sq, g + 1)
                    if g:
                        pool.wait_ge(o_sb, g)
                    rms(st[:, 16:20], st[:, 20:24], A_DV).then_inc(o_rs, 1)
                elif kind == "glanorm":
                    t = item[1]
                    pool.wait_ge(gla_sq, t + 1)
                    rms(st[:, 24:28], st[:, 28:32], B_DV).then_inc(gla_rs, 1)
            pool.wait_ge(oT_sb, 4)
            pool.memset(ye, 0.0).then_inc(ye_sb, 1)
            pool.wait_ge(ye_sb, 1)
            pool.dma_start(ys[NE * ROWS:MAX_TILES * ROWS, :].rearrange("(p r) (g n) -> p (r g) n", p=P, g=4),
                           ye.unsqueeze(1).to_broadcast((P, 4 * (MAX_TILES - NE) * ROWS // P, 512))).then_inc(ys_zero, 16)
            for t in range(TT):
                pool.wait_ge(y_tot, t + 1)
                rms(st[:, 56 + t:57 + t], st[:, 58 + t:59 + t], D).then_inc(y_rs, 1)
                pool.wait_ge(x1_sq, t + 1)
                rms(st[:, 60 + t:61 + t], st[:, 62 + t:63 + t], D).then_inc(x1_rs, 1)
            pool.wait_ge(route_sb, 1)
            pool.wait_ge(ys_zero, 16)
            total = pool.value_load(cums[0:1, NE:NE + 1], min_val=NE, max_val=MAX_TILES)

            def outputs(t, first):
                pool.wait_ge(ye_sb, t + 2)
                if not first:
                    pool.wait_ge(ye_out, 64 * t)
                pool.nop(nofuse=True)
                nc.gpsimd.tensor_copy(yo, ye).then_inc(yo_sb, 1)
                pool.wait_ge(yo_sb, t + 2)
                pool.nop(nofuse=True)
                for g in range(4):
                    pool.dma_start(ys[bass.ds(t * ROWS, ROWS), 512 * g:512 * g + 512], yo[32 * g:32 * g + 32, :]).then_inc(ye_out, 16)

            pool.wait_ge(x1_sb, TT)
            nc.gpsimd.memset(yo, 0.0).then_inc(yo_sb, 1)
            pool.wait_ge(yo_sb, 1)
            outputs(0, True)
            with pool.Fori(1, total) as t:
                outputs(t, False)
            pool.wait_ge(ye_out, 64 * total)
            pool.nop(nofuse=True)
            for j in range(2 * TT):
                pool.indirect_dma_start(fin_rows(j), None, ys[:, :], bass.IndirectOffsetOnAxis(ap=slots[:, j:j + 1], axis=0)).then_inc(fin_rows_in[j // 2], 16)
            for t in range(TT):
                pool.wait_ge(fin_sq, t + 1)
                rms(st[:, 66 + t:67 + t], st[:, 70 + t:71 + t], D).then_inc(fin_rs, 1)


NAMES = ["x", "c", "rel_bias", "w_ada", "b_ada", "g_pre_mix", "g_post_mix", "w_in", "w_alpha", "b_alpha", "lam_q1", "lam_k1",
         "lam_q2", "lam_k2", "g_sub_a", "g_norm_b", "w_out", "g_pre_ffn", "g_post_ffn", "w_router_g", "b_router_g",
         "w_router_e", "b_router_e", "w1", "w3", "w2"]


def kernel(**inputs):
    import concourse.bacc as bacc
    from concourse.bass_utils import run_bass_kernel_spmd

    nc = bacc.Bacc("TRN2", target_bir_lowering=False, num_devices=1)
    arrays = {f"in_{n}": np.ascontiguousarray(inputs[n]) for n in NAMES}
    arrays["in_cst"] = shape_constants()
    aps = {n[3:]: nc.dram_tensor(n, v.shape, mybir.dt.from_np(v.dtype), kind="ExternalInput").ap() for n, v in arrays.items()}
    out = nc.dram_tensor("out", (1, S, D), mybir.dt.float32, kind="ExternalOutput").ap()
    build(nc, aps, out)
    return run_bass_kernel_spmd(nc, [arrays], core_ids=[0]).results[0]["out"]
```

```python
import math
from contextlib import ExitStack

import numpy as np
import concourse.bass as bass
from concourse import mybir

D = 2048
S = 256
P = 128
TT = S // P
KD = D // P
CHUNK = 64
A_HEADS, A_DK, A_DV = 8, 64, 128
B_HEADS, B_DK, B_DV = 4, 128, 256
GATE_RANK, GATE_TAU = 16, 16.0
N_BUCKETS, MAX_DISTANCE = 32, 256
N_GROUPS, PER_GROUP = 4, 8
NE = N_GROUPS * PER_GROUP
F = D // 4
D_IN = 3 * 1024 + 2 * 512 + 2 * 1024 + GATE_RANK
EPS = 1e-6
LAM_INIT = 0.8 - 0.6 * math.exp(-0.3 * 0)
NEG = -1e30
ROWS = 32
MAX_TILES = NE + (2 * S - NE) // ROWS + 1
UNIT = 8192
REL = 2 * S - 1
SKEW = 384

C_ID, C_LT, C_SUF, C_ONE, C_IOTA, C_THR, C_NH, C_HALF, C_BKT = 0, 128, 256, 384, 512, 544, 554, 558, 560
C_KEEP = C_BKT
C_ALL = C_BKT + 512

ORDER = [0, 2, 4, 1, 3, 5, 7, 6, 8, 9, 10, 11]
TRANSPOSED = {0, 1, 2, 3, 6}
ATT = 2 * A_HEADS
HEADS_READY = [6, 12]
X1T_BANK = [[2, 3, 4, 5], [6, 7, 0, 1]]
PIECES = [(1, 1), (1, 2), (1, 3)]
ATT_FROM = 4


def head_block(i):
    g = i // 4
    return 4 * (g // 2) + i % 4, g % 2


def t5_bucket(rel):
    nb = N_BUCKETS // 2
    exact = nb // 2
    n = np.abs(rel)
    nf = np.maximum(n, 1).astype(np.float32)
    large = exact + (np.log(nf / exact) / math.log(MAX_DISTANCE / exact) * (nb - exact)).astype(np.int32)
    return np.where(rel > 0, nb, 0) + np.where(n < exact, n, np.minimum(large, nb - 1))


def shape_constants():
    c = np.zeros((P, C_ALL), np.float32)
    p = np.arange(P)
    c[:, C_ID:C_ID + P] = np.eye(P)
    c[:, C_LT:C_LT + P] = p[:, None] < p[None, :]
    c[:, C_SUF:C_SUF + P] = (p[:, None] > p[None, :]) & (p[:, None] // CHUNK == p[None, :] // CHUNK)
    c[:, C_ONE:C_ONE + P] = 1.0
    c[:, C_IOTA:C_IOTA + NE] = np.arange(NE)
    c[:, C_THR:C_THR + 8] = ROWS * np.arange(8)
    c[:, C_NH:C_NH + 4] = -0.5
    c[:, C_HALF] = p < CHUNK
    c[:, C_HALF + 1] = p >= CHUNK
    rel = np.arange(REL) - (S - 1)
    c[0:N_BUCKETS, C_BKT:C_BKT + REL] = t5_bucket(rel)[None, :] == np.arange(N_BUCKETS)[:, None]
    return c


def schedule():
    out = []
    for m in (0, 1):
        for q in range(4):
            if (m, q) == (0, 3):
                out.append(("prepare",))
            out += [("ada", m, q, k) for k in range(4)]
            if (m, q) == (1, 0):
                out.append(("mod", 0))
    out.append(("mod", 1))
    out.append(("modulate",))
    beside = [[] for _ in range(12 * 4)]
    beside[0].append(("alpha", 0))
    beside[2].append(("alpha", 1))
    beside[5].append(("alpha", 2))
    beside[17].append(("mod", 2))
    beside[33].append(("mod", 3))
    for j in range(48):
        beside[j].append(("ada", 2 + j // 16, j // 4 % 4, j % 4))
    for j in range(ATT + 3):
        beside[4 * ATT_FROM + j].append(("att", j))
    beside[28].append(("kdec",))
    for j in range(5):
        if j:
            beside[41 + j].append(("glao", j - 1))
        if j < 4:
            beside[41 + j].append(("kv", j))
    beside[42] += [("silu", 0, 0)]
    beside[44] += [("gsq", 0), ("silu", 1, 0)]
    beside[45] += [("gmul", 0, 0)]
    beside[46] += [("gsq", 1), ("silu", 0, 1), ("gmul", 0, 1)]
    beside[47] += [("gmul", 1, 0), ("glaT", 0)]
    for j in range(48):
        out.append(("proj", j // 4, j // 2 % 2, j % 2))
        out += beside[j]
    for u in range(4):
        if u == 0:
            out += [("silu", 1, 1), ("gmul", 1, 1), ("wout", 0, 0), ("glaT", 1), ("mod", 4)]
        else:
            out.append(("wout", u, 0))
        out += [("ada", 5, u, k) for k in range(4)]
        out.append(("wout", u, 1))
    return out


def build(nc, a, out):
    f32, i32, u32 = mybir.dt.float32, mybir.dt.int32, mybir.dt.uint32
    ALU, ACT, AX = mybir.AluOpType, mybir.ActivationFunctionType, mybir.AxisListType
    SCHED = schedule()
    STREAM = []
    for s in SCHED:
        unit = ("ada", 4 * s[1] + s[2]) if s[0] == "ada" else s[:2]
        if s[0] in ("ada", "proj", "wout") and unit not in STREAM:
            STREAM.append(unit)
    SLOT = {s: (n % 3, n // 3) for n, s in enumerate(STREAM)}

    ctx = ExitStack()
    with ctx:
        def sb(name, shape, dt=f32):
            return ctx.enter_context(nc.sbuf_tensor(name, shape, dt))

        def sem(name):
            return ctx.enter_context(nc.semaphore(name))

        def dram(name, shape, dt=f32):
            return nc.dram_tensor(name, shape, dt, kind="Internal")

        stream = sb("stream", [P, 5, UNIT])
        resid = sb("resid", [P, TT, D])
        acc = sb("acc", [P, D])
        wk = sb("wk", [P, 4096])
        cst = sb("cst", [P, C_KEEP])
        wr = sb("wr", [P, KD, N_GROUPS + NE])
        br = sb("br", [P, N_GROUPS + NE])
        cc = sb("cc", [P, 3, KD])
        gains = sb("gains", [P, 4, KD])
        bada = sb("bada", [P, 6, KD])
        mod = sb("mod", [P, 6, KD])
        gsub = sb("gsub", [P, 1])
        gnb = sb("gnb", [P, 2])
        lamv = sb("lamv", [P, 8])
        st = sb("st", [P, 96])
        cums = sb("cums", [1, NE + 1], i32)
        rel = sb("rel", [P, TT, 2])
        gates = sb("gates", [P, TT, 2])
        slots = sb("slots", [P, 2 * TT], u32)

        ident = cst[:, C_ID:C_ID + P]
        ones = cst[:, C_ONE:C_ONE + P]

        def view(t, lo, n, c):
            return t[:, lo:lo + n * c].rearrange("p (n c) -> p n c", n=n)
        s3, s4 = stream[:, 3, :], stream[:, 4, :]
        va, vb, rb = view(s3, 0, TT, 1024), view(s3, 2048, TT, 1024), view(s3, 4096, TT, 1024)
        kb, qbT = view(s3, 6144, TT, 512), view(s3, 7168, B_HEADS, S)
        y, x1T = view(s3, 0, TT, D), view(s3, 4096, KD, S)
        hT, qaT, kaT = view(s4, 0, KD, S), view(s4, 4096, A_HEADS, S), view(s4, 6144, A_HEADS, S)
        oTa, oTb = qaT, view(s4, 0, 8, S)
        junk1 = s4[:, 4096:4096 + D]
        gl = resid[:, :, :].rearrange("p t d -> p (t d)")
        kdec, state = view(gl, 0, TT, 512), view(gl, 1024, B_HEADS, B_DV)
        la, tmp = view(gl, 2048, TT, 512), gl[:, 3072:4096]
        bias = view(wk, 0, A_HEADS, S)
        sc, pr = view(wk, 2048, 2, S), view(wk, 2560, 2, S)
        pd, pdT, on = wk[:, 3072:3328], wk[:, 3328:3584], view(wk, 3584, 4, A_DV)
        walpha, balpha, bkt = wk[0:GATE_RANK, 2048:2560], wk[:, 2560:3072], wk[0:N_BUCKETS, 3072:3584]
        zbT = wk[0:GATE_RANK, 3072:3328]
        wzb = view(s3, 7168, KD, GATE_RANK)
        relb, relrow, lamw = wk[0:N_BUCKETS, 3584:3592], wk[0:A_HEADS, 3600:3984], wk[:, 0:256]
        g1b = acc[:, :]
        xe = view(wk, 2048, KD, ROWS)
        ab, eh, hid, ye = wk[:, 2560:2816], view(wk, 2816, 2, 64), view(wk, 2944, 2, 64), wk[:, 3072:3584]
        logT = wk[0:36, 3584:3584 + S]
        yo = wk[:, 0:512]
        xp = wk[:, 3584:4096]
        wrf = wr[:, :, :].rearrange("p k n -> p (k n)")
        hit, pick = view(wrf, 0, 2 * TT, ROWS), view(wrf, 256, TT, ROWS)
        g2b = acc[:, :]
        rows = resid[:, :, :].rearrange("p t (q k) -> p t k q", k=KD)
        shw, shs = view(wk, D, KD, 36), wk[:, D + KD * 36:D + (KD + 1) * 36]
        RSHAPES = dict(L=(TT, 36), g8=(TT, 8), gm=(TT, 8), gi=(TT, 8), ng=(TT, 1), gf=(TT, 1), sel=(TT, 4), eg=(TT, 4, 8), es=(TT, 8),
                       em=(TT, 8), ei=(TT, 8), d2=(TT, 1), ef=(TT, 2), ex=(TT, 2), oh=(TT, 2, NE), M=(TT, NE), w=(TT, 2), e2=(TT, 1),
                       gs=(TT, 1), ge=(TT, 4), cnt=(NE,), cmp=(NE, 8), nt=(NE,), zero=(NE,), cum=(NE,), base=(NE,), pos=(TT, NE))

        def R(name):
            lo = sum(int(np.prod(v)) for k, v in RSHAPES.items() if list(RSHAPES).index(k) < list(RSHAPES).index(name))
            shape = RSHAPES[name]
            v = wk[:, D + lo:D + lo + int(np.prod(shape))]
            if name in ("gi", "ei"):
                v = v.bitcast(u32)
            if len(shape) == 2:
                v = v.rearrange("p (a b) -> p a b", a=shape[0])
            if len(shape) == 3:
                v = v.rearrange("p (a b c) -> p a b c", a=shape[0], b=shape[1])
            return v

        def mod_bank(m):
            return bank(3 if m == 4 else 6)

        def acc_of(m):
            return {1: wk[:, 0:D], 3: s3[:, 4096:4096 + D], 5: wk[:, 0:D]}.get(m, acc[:, :])

        def fin_rows(j):
            return stream[:, 0, D * j:D * j + D]

        ps = ctx.enter_context(nc.psum_tensor("ps", [P, 8, 512], f32))

        def bank(b, *dims):
            if not dims:
                return ps[:, b, :]
            return ps[:, b, 0:dims[0] * dims[1]].rearrange("p (n c) -> p n c", n=dims[0])

        skew = dram("skew", [A_HEADS, P, SKEW])
        gdram = dram("gdram", [2, P, KD])
        ys = dram("ys", [MAX_TILES * ROWS, D])

        c_in, const_in, x_in, par_in, late_in = sem("c_in"), sem("const_in"), sem("x_in"), sem("par_in"), sem("late_in")
        bias_in, skew_out = sem("bias_in"), sem("skew_out")
        unit_in = [sem(f"unit_in{i}") for i in range(3)]
        piece_in = [[sem(f"piece_in{m}_{q}_{k}") for k in range(3)] for m, q in PIECES]
        ada_done = sem("ada_done")
        act_c, dve_c, pool_c = sem("act_chain"), sem("dve_chain"), sem("pool_chain")
        relrow_ps, relrow_sb, masked = sem("relrow_ps"), sem("relrow_sb"), sem("masked")
        c_exp, scale_sb, last_out, fin_gate = sem("c_exp"), sem("scale_sb"), sem("last_out"), sem("fin_gate")
        xsq, xr, xn = sem("xsq"), sem("xr"), sem("xn")
        xT_ps, xT_sb = sem("xT_ps"), sem("xT_sb")
        mod_ps, mod_sb = sem("mod_ps"), sem("mod_sb")
        hT_dve, hT_act = sem("hT_dve"), sem("hT_act")
        zb_ps, zb_sb, z_ps, z_abs, z_ln, la_sb = sem("zb_ps"), sem("zb_sb"), sem("z_ps"), sem("z_abs"), sem("z_ln"), sem("la_sb")
        suf_ps, suf_exp, kdec_sb = sem("suf_ps"), sem("suf_exp"), sem("kdec_sb")
        proj_ps, proj_sb = sem("proj_ps"), sem("proj_sb")
        s_ps, s_sb, p_max, p_exp, pd_sb = sem("s_ps"), sem("s_sb"), sem("p_max"), sem("p_exp"), sem("pd_sb")
        pdT_ps, pdT_sb, o_ps, o_sq, o_rs, o_sb = sem("pdT_ps"), sem("pdT_sb"), sem("o_ps"), sem("o_sq"), sem("o_rs"), sem("o_sb")
        oT_ps, oT_sb = sem("oT_ps"), sem("oT_sb")
        lam_sum, lam_exp = sem("lam_sum"), sem("lam_exp")
        kv_ps, state_sb, gla_ps = sem("kv_ps"), sem("state_sb"), sem("gla_ps")
        rb_exp, rb_sb, gla_sq, gla_rs, gla_sb = sem("rb_exp"), sem("rb_sb"), sem("gla_sq"), sem("gla_rs"), sem("gla_sb")
        glaT_ps, glaT_sb = sem("glaT_ps"), sem("glaT_sb")
        g_sb, g1_out, g2_out, g1_in, g2_in, xre_in = sem("g_sb"), sem("g1_out"), sem("g2_out"), sem("g1_in"), sem("g2_in"), sem("xre_in")
        y_tot, y_sum, y_rs, x1_sb, x1_sq, x1_rs = sem("y_tot"), sem("y_sum"), sem("y_rs"), sem("x1_sb"), sem("x1_sq"), sem("x1_rs")
        x1T_ps, x1T_dve, x1T_act, logT_ps, logT_sb, shs_sb, shs_ps, wr_sb = sem("x1T_ps"), sem("x1T_dve"), sem("x1T_act"), sem("logT_ps"), sem("logT_sb"), sem("shs_sb"), sem("shs_ps"), sem("wr_sb")
        pick_sb, pick_c, rows_ps, rows_sb, ye_out, yo_sb = (
            sem("pick_sb"), sem("pick_c"), sem("rows_ps"), sem("rows_sb"), sem("ye_out"), sem("yo_sb"))
        log_ps, g_max, e_max, r_exp2, m_sb, rank_ps, route_sb = (
            sem("log_ps"), sem("g_max"), sem("e_max"), sem("r_exp2"), sem("m_sb"), sem("rank_ps"),
            sem("route_sb"))
        w1_in, w3_in, w2_in = [sem("w1_in0"), sem("w1_in1")], [[sem(f"w3_in{b}_half{j}") for j in range(2)] for b in range(2)], [sem("w2_in_half0"), sem("w2_in_half1")]
        xe_ps, xe_t, xe_sb, ab_ps, ab_sb, h_ps, h_exp, h_t, hid_sb, ye_ps, ye_sb = (
            sem("xe_ps"), sem("xe_t"), sem("xe_sb"), sem("ab_ps"), sem("ab_sb"), sem("h_ps"), sem("h_exp"), sem("h_t"),
            sem("hid_sb"), sem("ye_ps"), sem("ye_sb"))
        fin_rows_in, fin_sum, fin_sq, fin_rs, fin_sb, fin_out = (
            [sem(f"fin_rows_in{j}") for j in range(2 * TT)], sem("fin_sum"), sem("fin_sq"), sem("fin_rs"), sem("fin_sb"), sem("fin_out"))

        w_ada = a["w_ada"].rearrange("l (p k) (m n) -> (l p) k m n", p=P, m=6)
        w_in = a["w_in"].rearrange("l (p k) n -> (l p) k n", p=P)
        w_out = a["w_out"].rearrange("l (k p) n -> (l p) k n", p=P)
        w1 = a["w1"].rearrange("l e (p k) f -> (l e) p (k f)", p=P)
        w3 = a["w3"].rearrange("l e (p k) f -> (l e) p (k f)", p=P)
        w2 = a["w2"].rearrange("l e (k p) n -> (l e) p k n", p=P)
        x_d = a["x"].rearrange("b (t p) d -> (b p) t d", p=P)
        out_d = out.rearrange("b (t p) d -> (b p) t d", p=P)

        def row_bcast(ap, n):
            return bass.AP(tensor=ap.tensor, offset=ap.offset, ap=[[0, P], [1, n]])

        GSQ = (24, 72)

        def DECAY(n, h):
            return 32 + 8 * (n // 2) + 2 * h + n % 2

        def vec(ap):
            return ap.rearrange("l (p k) -> (l p) k", p=P)

        params = [
            (relb, a["rel_bias"][:, :]),
            (lamw[:, 0:64], row_bcast(a["lam_q1"], 64)), (lamw[:, 64:128], row_bcast(a["lam_k1"], 64)),
            (lamw[:, 128:192], row_bcast(a["lam_q2"], 64)), (lamw[:, 192:256], row_bcast(a["lam_k2"], 64)),
            (gsub[:, :], a["g_sub_a"].rearrange("l (p o) -> (l p) o", o=1)),
            (bada[:, :, :], a["b_ada"].rearrange("l (m p k) -> (l p) m k", m=6, p=P)),
            (gains[:, 0, :], vec(a["g_pre_mix"])), (gains[:, 1, :], vec(a["g_post_mix"])),
            (gains[:, 2, :], vec(a["g_pre_ffn"])), (gains[:, 3, :], vec(a["g_post_ffn"])),
            (wzb[:, :, :], w_in[:, :, D_IN - GATE_RANK:D_IN]),
            (gnb[:, 0:1], a["g_norm_b"][:, 0:P].rearrange("l (p o) -> (l p) o", o=1)),
            (gnb[:, 1:2], a["g_norm_b"][:, P:2 * P].rearrange("l (p o) -> (l p) o", o=1)),
            (wr[:, :, 0:N_GROUPS], a["w_router_g"].rearrange("l (p k) n -> (l p) k n", p=P)),
            (wr[:, :, N_GROUPS:N_GROUPS + NE], a["w_router_e"].rearrange("l (p k) n -> (l p) k n", p=P)),
            (br[:, 0:N_GROUPS], row_bcast(a["b_router_g"], N_GROUPS)), (br[:, N_GROUPS:N_GROUPS + NE], row_bcast(a["b_router_e"], NE)),
        ]

        W1 = [stream[:, 0, :], stream[:, 1, :]]
        W3 = [stream[:, 2, :], stream[:, 3, :]]
        W2v = stream[:, 4, :].rearrange("p (k n) -> p k n", k=4)

        def half(w, j):
            return w[:, UNIT // 2 * j:UNIT // 2 * (j + 1)]

        def w_unit(e, t):
            return t[bass.ds(e, 1)].rearrange("e p n -> (e p) n")

        block = ctx.enter_context(nc.Block())

        @block.sync
        def _(sp):
            def wait_used(item):
                if item[0] == "ada":
                    sp.wait_ge(ada_done, item[1] + 1)
                elif item[0] == "proj":
                    sp.wait_ge(proj_ps, 2 * item[1] + 2)
                else:
                    sp.wait_ge(proj_ps, 24 + 2 * item[1] + 2)

            for n, item in enumerate(STREAM):
                s = n % 3
                if n >= 3:
                    wait_used(STREAM[n - 3])
                dst = stream[:, s, :]
                if item[0] == "ada":
                    m, q = item[1] // 4, item[1] % 4
                    if (m, q) in PIECES:
                        for k in range(4):
                            sp.dma_start(dst.rearrange("p (k n) -> p k n", k=4)[:, k, :], w_ada[:, 4 * q + k, m, :]).then_inc(piece_in[PIECES.index((m, q))][k] if k < 3 else unit_in[s], 16)
                        continue
                    sp.dma_start(dst.rearrange("p (k n) -> p k n", k=4), w_ada[:, 4 * q:4 * q + 4, m, :]).then_inc(unit_in[s], 16)
                elif item[0] == "proj":
                    c = ORDER[item[1]]
                    sp.dma_start(dst.rearrange("p (k n) -> p k n", k=KD), w_in[:, :, 512 * c:512 * c + 512]).then_inc(unit_in[s], 16)
                else:
                    u = item[1]
                    sp.dma_start(dst.rearrange("p (k n) -> p k n", k=KD), w_out[:, :, 512 * u:512 * u + 512]).then_inc(unit_in[s], 16)
            for n in range(len(STREAM) - 3, len(STREAM)):
                wait_used(STREAM[n])
                if n % 3 == 0:
                    sp.dma_start(W1[0], w1[0]).then_inc(w1_in[0], 16)
                elif n % 3 == 1:
                    sp.dma_start(W1[1], w1[1]).then_inc(w1_in[1], 16)
                else:
                    for j in range(2):
                        sp.dma_start(half(W3[0], j), half(w3[0], j)).then_inc(w3_in[0][j], 16)
            sp.wait_ge(proj_ps, 24 + 8)
            sp.wait_ge(x1_sq, 1)
            for j in range(2):
                sp.dma_start(W2v[:, 2 * j:2 * j + 2, :], w2[0][:, 2 * j:2 * j + 2, :]).then_inc(w2_in[j], 16)
            sp.wait_ge(log_ps, 1)
            for j in range(2):
                sp.dma_start(half(W3[1], j), half(w3[1], j)).then_inc(w3_in[1][j], 16)
            sp.wait_ge(route_sb, 1)

            def load_w1(e, b):
                done = sp.value_load(cums[0:1, bass.ds(e - 1, 1)], min_val=1, max_val=MAX_TILES)
                sp.wait_ge(ab_ps, done)
                sp.dma_start(W1[b], w_unit(e, w1)).then_inc(w1_in[b], 16)

            def load_w3(e, b):
                for j in range(2):
                    sp.dma_start(half(W3[b], j), half(w_unit(e, w3), j)).then_inc(w3_in[b][j], 16)

            def load_w2(e):
                done = sp.value_load(cums[0:1, bass.ds(e, 1)], min_val=1, max_val=MAX_TILES)
                sp.wait_ge(ye_ps, done)
                src = w2[bass.ds(e, 1)].rearrange("e p k n -> (e p) k n")
                for j in range(2):
                    sp.dma_start(W2v[:, 2 * j:2 * j + 2, :], src[:, 2 * j:2 * j + 2, :]).then_inc(w2_in[j], 16)

            load_w1(2, 0)
            load_w2(1)
            load_w3(2, 0)
            load_w2(2)
            load_w1(3, 1)
            load_w3(3, 1)
            load_w2(3)
            sp.wait_ge(g2_out, 16)
            sp.wait_ge(x1_sq, TT)
            sp.dma_start(g2b, row_bcast(gdram[1, :, :], D)).then_inc(g2_in, 16)
            with sp.Fori(2, NE // 2) as i:
                for b in range(2):
                    load_w1(2 * i + b, b)
                    load_w3(2 * i + b, b)
                    load_w2(2 * i + b)

        @block.tensor
        def _(pe):
            pe.wait_ge(const_in, 32)
            pe.wait_ge(par_in, 16 * len(params))
            nc.tensor.matmul(bank(4)[0:A_HEADS, 0:384], relb, bkt[:, 0:384], start=True, stop=True).then_inc(relrow_ps, 1)
            def mod_sums(m, ks):
                for k in ks:
                    last = nc.tensor.matmul(mod_bank(m)[:, 16 * m + k:16 * m + k + 1], acc_of(m)[:, k::KD], ones[:, 0:1], start=True, stop=True)
                return last

            fill = 0
            for item in SCHED:
                kind = item[0]
                if kind == "mod":
                    pe.wait_ge(ada_done, 4 * item[1] + 4)
                    if item[1] == 4:
                        pe.wait_ge(gla_sb, 2)
                    mod_sums(item[1], range(KD)).then_inc(mod_ps, 1)
                elif kind == "prepare":
                    for t in range(TT):
                        pe.wait_ge(xn, t + 1)
                        for j in range(4):
                            if t:
                                pe.wait_ge(xT_sb, j + 1)
                            for k in range(4):
                                last = nc.tensor.transpose(bank(j, 4, P)[:, k, :], resid[:, t, 4 * j + k::KD], ident)
                            last.then_inc(xT_ps, 1)
                elif kind == "alpha":
                    if item[1] == 0:
                        for k in range(KD):
                            last = nc.tensor.matmul(bank(5)[0:GATE_RANK, 0:S], wzb[:, k, :], hT[:, k, :], start=(k == 0), stop=(k == KD - 1))
                        last.then_inc(zb_ps, 1)
                    elif item[1] == 1:
                        pe.wait_ge(late_in, 32)
                        pe.wait_ge(zb_sb, 1)
                        for t in range(TT):
                            nc.tensor.matmul(bank(2 + t), zbT[:, P * t:P * t + P], walpha, start=True, stop=True).then_inc(z_ps, 1)
                    else:
                        for t in range(TT):
                            pe.wait_ge(la_sb, t + 1)
                            nc.tensor.matmul(bank(4 + t), cst[:, C_SUF:C_SUF + P], la[:, t, :], start=True, stop=True).then_inc(suf_ps, 1)
                        for t in range(TT):
                            for h in range(B_HEADS):
                                last = nc.tensor.matmul(bank(7)[:, 8 * t + 2 * h:8 * t + 2 * h + 2], la[:, t, P * h:P * h + P],
                                                        cst[:, C_HALF:C_HALF + 2], start=True, stop=True)
                        last.then_inc(suf_ps, 1)
                elif kind == "proj":
                    _, i, half, part = item
                    c = ORDER[i]
                    s, n = SLOT[("proj", i)]
                    w = stream[:, s, :].rearrange("p (k n) -> p k n", k=KD)
                    if part == 0:
                        if half == 0:
                            pe.wait_ge(unit_in[s], 16 * (n + 1))
                        if fill >= 2:
                            pe.wait_ge(proj_sb, fill - 1)
                    if c in TRANSPOSED:
                        lo = 256 * half + P * part
                        for k in range(KD):
                            if fill == 0 and part == 0:
                                pe.wait_ge(hT_act if k % 2 else hT_dve, k // 2 + 1)
                            last = nc.tensor.matmul(bank(fill % 2, 2, S)[:, part, :], w[:, k, lo:lo + P], hT[:, k, :], start=(k == 0), stop=(k == KD - 1))
                    else:
                        for k in range(8 * part, 8 * part + 8):
                            last = nc.tensor.matmul(bank(fill % 2), hT[:, k, P * half:P * half + P], w[:, k, :], start=(k == 0), stop=(k == KD - 1))
                    if part == 1:
                        last.then_inc(proj_ps, 1)
                        fill += 1
                elif kind == "att":
                    i = item[1]
                    if i < ATT:
                        h, b = head_block(i)
                        nk = P * (b + 1)
                        if i == 0:
                            pe.wait_ge(suf_exp, 3)
                        else:
                            pe.wait_ge(s_sb, i)
                        pe.wait_ge(proj_sb, HEADS_READY[h // 4])
                        for m in range(2):
                            r = slice(A_DK * m, A_DK * m + A_DK)
                            last = nc.tensor.matmul(ps[:, 2 + m, 0:nk], qaT[r, h, P * b:P * b + P], kaT[r, h, 0:nk], start=True, stop=True)
                        last.then_inc(s_ps, 1)
                    if 2 <= i < ATT + 2:
                        j = i - 2
                        h, b = head_block(j)
                        pe.wait_ge(pdT_sb, j + 1)
                        if j >= 4 and j % 4 == 0:
                            pe.wait_ge(o_sb, j // 4)
                        for kt in range(b + 1):
                            last = nc.tensor.matmul(bank(4, 4, A_DV)[:, j % 4, :], pdT[:, P * kt:P * kt + P], va[:, kt, A_DV * h:A_DV * h + A_DV],
                                                    start=(kt == 0), stop=(kt == b))
                        last.then_inc(o_ps, 1)
                    if 1 <= i < ATT + 1:
                        j = i - 1
                        _, b = head_block(j)
                        pe.wait_ge(pd_sb, j + 1)
                        for kt in range(b + 1):
                            last = nc.tensor.transpose(bank(7)[:, P * kt:P * kt + P], pd[:, P * kt:P * kt + P], ident)
                        last.then_inc(pdT_ps, 1)
                    if i % 4 == 2 and i >= 6:
                        g = (i - 6) // 4
                        pe.wait_ge(o_sb, g + 1)
                        for j in range(4):
                            last = nc.tensor.transpose(bank(5, 4, P)[:, j, :], on[:, j, :], ident)
                        last.then_inc(oT_ps, 1)
                elif kind == "kv":
                    n = item[1]
                    t, lo = n // 2, CHUNK * (n % 2)
                    if n == 0:
                        pe.wait_ge(kdec_sb, 1)
                        pe.wait_ge(mod_sb, 4)
                        pe.wait_ge(oT_sb, 4)
                        pe.wait_ge(proj_sb, 20)
                    for h in range(B_HEADS):
                        last = nc.tensor.matmul(bank(6 + h // 2, 2, B_DV)[:, h % 2, :], kdec[lo:lo + CHUNK, t, P * h:P * h + P],
                                                vb[lo:lo + CHUNK, t, B_DV * h:B_DV * h + B_DV], start=True, stop=True)
                    last.then_inc(kv_ps, 1)
                elif kind == "glao":
                    n = item[1]
                    t, lo = n // 2, CHUNK * (n % 2)
                    pe.wait_ge(state_sb, n + 1)
                    for h in range(B_HEADS):
                        last = nc.tensor.matmul(bank(2 + 2 * t + h // 2, 2, B_DV)[lo:lo + CHUNK, h % 2, :], qbT[:, h, CHUNK * n:CHUNK * n + CHUNK],
                                                state[:, h, :], start=True, stop=True)
                    last.then_inc(gla_ps, 1)
                elif kind == "glaT":
                    t = item[1]
                    pe.wait_ge(gla_sb, 2 * t + 2)
                    for j in range(2):
                        if t:
                            pe.wait_ge(glaT_sb, j + 1)
                        for k in range(4):
                            last = nc.tensor.transpose(bank(6 + j, 4, P)[:, k, :], rb[:, t, P * (4 * j + k):P * (4 * j + k) + P], ident)
                        last.then_inc(glaT_ps, 1)
                elif kind == "wout":
                    _, u, t = item
                    s, n = SLOT[("wout", u)]
                    w = stream[:, s, :].rearrange("p (k n) -> p k n", k=KD)
                    if t == 0:
                        pe.wait_ge(unit_in[s], 16 * (n + 1))
                    if u == 0:
                        pe.wait_ge(glaT_sb, 2 * t + 2)
                    if (u, t) == (2, 0):
                        pe.wait_ge(shs_sb, 1)
                        nc.tensor.matmul(bank(5)[:, 0:36], ones, shs, start=True, stop=True).then_inc(shs_ps, 1)
                    pe.wait_ge(proj_sb, fill - 1)
                    for k in range(KD):
                        lhs = (oTa if k < 8 else oTb)[:, k % 8, P * t:P * t + P]
                        last = nc.tensor.matmul(bank(fill % 2), lhs, w[:, k, :], start=(k == 0), stop=(k == KD - 1))
                    last.then_inc(proj_ps, 1)
                    fill += 1

            pe.wait_ge(mod_sb, 5)
            for t in range(TT):
                pe.wait_ge(x1_sb, t + 1)
                if t:
                    pe.wait_ge(proj_sb, 24 + 8)
                for j in range(4):
                    for k in range(4):
                        last = nc.tensor.transpose(bank(X1T_BANK[t][j], 4, P)[:, k, :], rows[:, t, 4 * j + k, :], ident)
                    last.then_inc(x1T_ps, 1)
                pe.wait_ge(wr_sb, 1)
                pe.wait_ge(x1T_act, 4 if t == 0 else 6)
                if t:
                    pe.wait_ge(x1T_dve, 2)
                for k in range(KD):
                    last = nc.tensor.matmul(bank(2)[0:36, P * t:P * t + P], wr[:, k, :], x1T[:, k, P * t:P * t + P], start=(k == 0), stop=(k == KD - 1))
            last.then_inc(logT_ps, 1)
            pe.wait_ge(logT_sb, 1)
            for t in range(TT):
                last = nc.tensor.transpose(bank(3, TT, 36)[:, t, :], logT[:, P * t:P * t + P], ident[0:36, 0:36])
            last.then_inc(log_ps, 1)
            pe.wait_ge(ada_done, 24)
            mod_sums(5, range(0, 8))
            pe.wait_ge(m_sb, 1)
            rk = bank(1, 4, NE)
            lt = cst[:, C_LT:C_LT + P]
            nc.tensor.matmul(rk[:, 0, :], lt, R("M")[:, 0, :], start=True, stop=True)
            nc.tensor.matmul(rk[:, 1, :], ones, R("M")[:, 0, :], start=True, stop=False)
            nc.tensor.matmul(rk[:, 1, :], lt, R("M")[:, 1, :], start=False, stop=True)
            nc.tensor.matmul(rk[:, 2, :], ones, R("M")[:, 0, :], start=True, stop=False)
            nc.tensor.matmul(rk[:, 2, :], ones, R("M")[:, 1, :], start=False, stop=True).then_inc(rank_ps, 1)
            mod_sums(5, range(8, KD)).then_inc(mod_ps, 1)

            def pick_rows():
                for t2 in range(TT):
                    for g in range(4):
                        last = nc.tensor.matmul(bank(0)[32 * g:32 * g + 32, :], pick[:, t2, :], rows[:, t2, 4 * g:4 * g + 4, :], start=(t2 == 0), stop=(t2 == TT - 1))
                last.then_inc(rows_ps, 1)

            def turn_rows():
                for j in range(4):
                    last = nc.tensor.transpose(bank(4, 4, P)[:, j, :], xp[:, P * j:P * j + P], ident)
                last.then_inc(xe_ps, 1)

            pe.wait_ge(pick_sb, 1)
            pick_rows()
            pe.wait_ge(rows_sb, 1)
            turn_rows()
            pe.wait_ge(route_sb, 1)
            with pe.Fori(0, NE // 2) as i:
                for b in range(2):
                    lo = pe.value_load(cums[0:1, bass.ds(2 * i + b, 1)], min_val=0, max_val=MAX_TILES)
                    hi = pe.value_load(cums[0:1, bass.ds(2 * i + b + 1, 1)], min_val=1, max_val=MAX_TILES)
                    pe.wait_ge(w1_in[b], 16 * i + 16)
                    pe.wait_ge(w3_in[b][0], 16 * i + 16)
                    pe.nop(nofuse=True)
                    a13 = [W1[b].rearrange("p (k f) -> p k f", k=KD), W3[b].rearrange("p (k f) -> p k f", k=KD)]
                    with pe.Fori(lo, hi) as t:
                        pe.wait_ge(xe_sb, t + 1)
                        for k in range(KD):
                            if k == KD // 2:
                                pe.wait_ge(w3_in[b][1], 16 * i + 16)
                            for g in range(4):
                                last = nc.tensor.matmul(bank(1)[32 * g:32 * g + 32, 0:256], xe[:, k, :], a13[g // 2][:, k, 256 * (g % 2):256 * (g % 2) + 256],
                                                        start=(k == 0), stop=(k == KD - 1))
                        last.then_inc(ab_ps, 1)
                        pe.wait_ge(pick_sb, t + 2)
                        pick_rows()
                        pe.wait_ge(ab_sb, t + 1)
                        for c in range(2):
                            last = nc.tensor.transpose(bank(2, 2, P)[:, c, :], ab[:, P * c:P * c + P], ident)
                        last.then_inc(h_ps, 1)
                        pe.wait_ge(rows_sb, t + 2)
                        turn_rows()
                        pe.wait_ge(ye_sb, t + 1)
                        pe.wait_ge(hid_sb, t + 1)
                        for k in range(4):
                            if k % 2 == 0:
                                pe.wait_ge(w2_in[k // 2], 32 * i + 16 * b + 16)
                            for g in range(4):
                                last = nc.tensor.matmul(bank(3)[32 * g:32 * g + 32, :], hid[:, k % 2, 32 * (k // 2):32 * (k // 2) + 32], W2v[:, k, 512 * g:512 * g + 512],
                                                        start=(k == 0), stop=(k == 3))
                        last.then_inc(ye_ps, 1)

        @block.vector
        def _(dve):
            n_c = [0]

            def step(ins):
                ins.then_inc(dve_c, 1)
                n_c[0] += 1

            def settle():
                dve.wait_ge(dve_c, n_c[0])

            def link(ins):
                step(ins)
                settle()

            V = nc.vector
            dve.wait_ge(c_exp, 1)
            link(V.tensor_scalar_add(cc[:, 2, :], cc[:, 1, :], 1.0))
            link(V.reciprocal(cc[:, 2, :], cc[:, 2, :]))
            link(V.tensor_tensor(cc[:, 2, :], cc[:, 2, :], cc[:, 0, :], ALU.mult))

            def prepare():
                dve.wait_ge(par_in, 16 * len(params))
                lw = lamw.rearrange("p (n c) -> p n c", n=4)
                link(V.tensor_tensor(lw[:, 0:4:2, :], lw[:, 0:4:2, :], lw[:, 1:4:2, :], ALU.mult))
                V.tensor_reduce(lamv[:, 0:2], lw[:, 0:4:2, :], axis=AX.X, op=ALU.add).then_inc(lam_sum, 1)
                dve.wait_ge(lam_exp, 1)
                link(V.tensor_tensor(lamv[:, 4:5], lamv[:, 3:4], lamv[:, 2:3], ALU.subtract))
                link(V.tensor_scalar_add(lamv[:, 5:6], lamv[:, 4:5], -LAM_INIT))
                link(V.tensor_scalar(gsub[:, :], gsub[:, :], 1.0 - LAM_INIT, None, ALU.mult))
                dve.wait_ge(relrow_ps, 1)
                V.tensor_copy(relrow, bank(4)[0:A_HEADS, 0:384]).then_inc(relrow_sb, 1)
                for t in range(TT):
                    dve.wait_ge(xr, t + 1)
                    V.tensor_scalar(resid[:, t, :], resid[:, t, :], st[:, 2 + t:3 + t], None, ALU.mult).then_inc(xn, 1)

            def accumulate(m, q, k):
                s, n = SLOT[("ada", 4 * m + q)]
                w = stream[:, s, :].rearrange("p (k n) -> p k n", k=4)
                if (m, q) in PIECES and k < 3:
                    dve.wait_ge(piece_in[PIECES.index((m, q))][k], 16)
                elif k == (3 if (m, q) in PIECES else 0):
                    dve.wait_ge(unit_in[s], 16 * (n + 1))
                if q == 0 and k == 0 and m in (2, 4):
                    dve.wait_ge(mod_ps, m - 1)
                acc_m = acc_of(m)
                col = cc[:, 2, 4 * q + k:4 * q + k + 1]
                if 4 * q + k == 0:
                    ins = V.tensor_scalar(acc_m, w[:, k, :], col, None, ALU.mult)
                else:
                    ins = V.scalar_tensor_tensor(out=acc_m, in0=w[:, k, :], scalar=col, in1=acc_m, op0=ALU.mult, op1=ALU.add)
                if k < 3:
                    link(ins)
                else:
                    ins.then_inc(ada_done, 1)
                    dve.wait_ge(ada_done, 4 * m + q + 1)

            def take_mod(m):
                dve.wait_ge(mod_ps, m + 1)
                V.tensor_tensor(mod[:, m, :], mod_bank(m)[:, 16 * m:16 * m + 16], bada[:, m, :], ALU.add).then_inc(mod_sb, 1)
                dve.wait_ge(mod_sb, m + 1)
                if m in (1, 4):
                    V.scalar_tensor_tensor(out=mod[:, m, :], in0=mod[:, m, :], scalar=1.0, in1=gains[:, 0 if m == 1 else 2, :], op0=ALU.add, op1=ALU.mult).then_inc(scale_sb, 1)
                    dve.wait_ge(scale_sb, 1 if m == 1 else 2)
                if m in (2, 5):
                    V.tensor_tensor(mod[:, m, :], mod[:, m, :], gains[:, 1 if m == 2 else 3, :], ALU.mult).then_inc(g_sb, 1)

            def gain_y(u, t):
                dve.wait_ge(proj_sb, 24 + 2 * u + t + 1)
                dve.wait_ge(g1_in, 16)
                c = slice(512 * u, 512 * u + 512)
                link(V.tensor_tensor(y[:, t, c], y[:, t, c], g1b[:, c], ALU.mult))

            def total_of(t):
                dve.wait_ge(y_sum, 7 + t)
                V.tensor_reduce(st[:, 56 + t:57 + t], st[:, 48 + 4 * t:52 + 4 * t], axis=AX.X, op=ALU.add).then_inc(y_tot, 1)

            for item in SCHED:
                kind = item[0]
                if kind == "ada":
                    accumulate(*item[1:])
                elif kind == "wout":
                    _, u, t = item
                    if t:
                        continue
                    if u == 1:
                        link(V.tensor_tensor(shw, wr[:, :, :], mod[:, 3, :].unsqueeze(2).to_broadcast((P, KD, 36)), ALU.mult))
                        V.tensor_reduce(shs, shw.rearrange("p k n -> p n k"), axis=AX.X, op=ALU.add).then_inc(shs_sb, 1)
                        V.tensor_tensor(wr[:, :, :], wr[:, :, :], mod[:, 4, :].unsqueeze(2).to_broadcast((P, KD, 36)), ALU.mult).then_inc(wr_sb, 1)
                    if u:
                        for j in range(TT):
                            gain_y(u - 1, j)
                    if u == 3:
                        dve.wait_ge(shs_ps, 1)
                        link(V.tensor_tensor(br[:, :], br[:, :], bank(5)[:, 0:36], ALU.add))
                elif kind == "prepare":
                    prepare()
                elif kind == "mod":
                    take_mod(item[1])
                elif kind == "modulate":
                    dve.wait_ge(xT_sb, 8)
                    for k in range(0, KD, 2):
                        V.tensor_scalar(hT[:, k, :], hT[:, k, :], mod[:, 1, k:k + 1], mod[:, 0, k:k + 1], ALU.mult, ALU.add).then_inc(hT_dve, 1)
                elif kind == "alpha" and item[1] == 1:
                    dve.wait_ge(late_in, 32)
                    for t in range(TT):
                        dve.wait_ge(z_ps, t + 1)
                        link(V.tensor_tensor(la[:, t, :], bank(2 + t), balpha, ALU.add))
                        V.scalar_tensor_tensor(out=tmp[:, 512 * t:512 * t + 512], in0=la[:, t, :], scalar=-1.0, in1=la[:, t, :],
                                               op0=ALU.mult, op1=ALU.max).then_inc(z_abs, 1)
                    for t in range(TT):
                        dve.wait_ge(z_ln, t + 1)
                        V.scalar_tensor_tensor(out=la[:, t, :], in0=la[:, t, :], scalar=0.0, in1=tmp[:, 512 * t:512 * t + 512],
                                               op0=ALU.min, op1=ALU.subtract).then_inc(la_sb, 1)
                elif kind == "kdec":
                    dve.wait_ge(suf_exp, 3)
                    dve.wait_ge(proj_sb, 14)
                    for t in range(TT):
                        ins = V.tensor_tensor(kdec[:, t, :], kdec[:, t, :], kb[:, t, :], ALU.mult)
                    ins.then_inc(kdec_sb, 1)
                elif kind == "att":
                    i = item[1]
                    if i < ATT:
                        h, b = head_block(i)
                        nk = P * (b + 1)
                        if i == 0:
                            dve.wait_ge(masked, 1)
                        dve.wait_ge(s_ps, i + 1)
                        V.scalar_tensor_tensor(out=sc[:, :, 0:nk], in0=ps[:, 2:4, 0:nk], scalar=A_DK ** -0.5,
                                               in1=bias[:, h:h + 1, S - nk:S].to_broadcast((P, 2, nk)), op0=ALU.mult, op1=ALU.add).then_inc(s_sb, 1)
                        dve.wait_ge(s_sb, i + 1)
                        V.tensor_reduce(st[:, 8:10], sc[:, :, 0:nk], axis=AX.X, op=ALU.max, negate=True).then_inc(p_max, 1)
                        dve.wait_ge(p_exp, i + 1)
                        if i:
                            dve.wait_ge(pdT_ps, i)
                        link(V.reciprocal(st[:, 12:14], st[:, 10:12]))
                        link(V.tensor_tensor(st[:, 14:15], st[:, 13:14], lamv[:, 5:6], ALU.mult))
                        link(V.tensor_scalar(pr[:, 0, 0:nk], pr[:, 0, 0:nk], st[:, 12:13], None, ALU.mult))
                        V.scalar_tensor_tensor(out=pd[:, 0:nk], in0=pr[:, 1, 0:nk], scalar=st[:, 14:15], in1=pr[:, 0, 0:nk],
                                               op0=ALU.mult, op1=ALU.add).then_inc(pd_sb, 1)
                    if i % 4 == 1 and i >= 5:
                        g = (i - 5) // 4
                        dve.wait_ge(o_rs, g + 1)
                        if g:
                            dve.wait_ge(oT_ps, g)
                        V.tensor_tensor(on, bank(4, 4, A_DV), st[:, 20:24].unsqueeze(2).to_broadcast((P, 4, A_DV)), ALU.mult).then_inc(o_sb, 1)
                    if i % 4 == 2 and i >= 6:
                        g = (i - 6) // 4
                        dve.wait_ge(oT_ps, g + 1)
                        V.tensor_scalar(oTa[:, 4 * (g // 2):4 * (g // 2) + 4, P * (g % 2):P * (g % 2) + P], bank(5, 4, P), gsub[:, 0:1], None,
                                        ALU.mult).then_inc(oT_sb, 1)
                elif kind == "silu":
                    _, t, c = item
                    r, e = rb[:, t, 512 * c:512 * c + 512], tmp[:, 512 * t:512 * t + 512]
                    dve.wait_ge(rb_exp, 2 * c + t + 1)
                    link(V.tensor_scalar_add(e, e, 1.0))
                    link(V.reciprocal(e, e))
                    V.tensor_tensor(r, r, e, ALU.mult).then_inc(rb_sb, 1)
                elif kind == "kv":
                    n = item[1]
                    dve.wait_ge(kv_ps, n + 1)
                    for h in range(B_HEADS):
                        kv = bank(6 + h // 2, 2, B_DV)[:, h % 2, :]
                        if n == 0:
                            ins = V.tensor_copy(state[:, h, :], kv)
                        else:
                            ins = V.scalar_tensor_tensor(out=state[:, h, :], in0=state[:, h, :], scalar=st[:, DECAY(n, h):DECAY(n, h) + 1], in1=kv,
                                                         op0=ALU.mult, op1=ALU.add)
                    ins.then_inc(state_sb, 1)
                    dve.wait_ge(state_sb, n + 1)
                elif kind == "gmul":
                    _, t, c = item
                    dve.wait_ge(gla_rs, t + 1)
                    dve.wait_ge(rb_sb, 2 * c + t + 1)
                    for h in (2 * c, 2 * c + 1):
                        r = rb[:, t, B_DV * h:B_DV * h + B_DV]
                        ins = V.scalar_tensor_tensor(out=r, in0=bank(2 + 2 * t + c, 2, B_DV)[:, h % 2, :], scalar=st[:, GSQ[t] + 4 + h:GSQ[t] + 5 + h], in1=r,
                                                     op0=ALU.mult, op1=ALU.mult)
                    ins.then_inc(gla_sb, 1)

            gain_y(3, 0)
            for t in range(TT):
                total_of(t)
                if t:
                    gain_y(3, 1)
                dve.wait_ge(y_rs, t + 1)
                dve.wait_ge(xre_in, 16)
                V.scalar_tensor_tensor(out=resid[:, t, :], in0=y[:, t, :], scalar=st[:, 58 + t:59 + t], in1=resid[:, t, :], op0=ALU.mult, op1=ALU.add).then_inc(x1_sb, 1)
            for j in (0, 2):
                dve.wait_ge(x1T_ps, 4 + j + 1)
                V.tensor_copy(x1T[:, 4 * j:4 * j + 4, P:2 * P], bank(X1T_BANK[1][j], 4, P)).then_inc(x1T_dve, 1)

            dve.wait_ge(logT_ps, 1)
            V.tensor_copy(logT, bank(2)[0:36, 0:S]).then_inc(logT_sb, 1)
            dve.wait_ge(log_ps, 1)
            dve.wait_ge(x1_rs, TT)
            L, g8 = R("L"), R("g8")
            link(V.memset(g8, -3.0e38))
            for t in range(TT):
                link(V.scalar_tensor_tensor(out=L[:, t, :], in0=bank(3, TT, 36)[:, t, :], scalar=st[:, 62 + t:63 + t], in1=br[:, :], op0=ALU.mult, op1=ALU.add))
            link(V.tensor_copy(g8[:, :, 0:4], L[:, :, 0:4]))
            for t in range(TT):
                link(V.max(R("gm")[:, t, :], g8[:, t, :]))
                link(V.max_index(R("gi")[:, t, :], R("gm")[:, t, :], g8[:, t, :]))
            V.tensor_scalar(R("ng"), R("gm")[:, :, 0:1], -1.0, None, ALU.mult).then_inc(g_max, 1)
            link(V.tensor_copy(R("gf"), R("gi")[:, :, 0:1]))
            link(V.tensor_tensor(R("sel"), cst[:, C_IOTA:C_IOTA + 4].unsqueeze(1).to_broadcast((P, TT, 4)), R("gf").to_broadcast((P, TT, 4)), ALU.is_equal))
            link(V.tensor_tensor(R("eg"), L[:, :, 4:36].rearrange("p t (g e) -> p t g e", g=4), R("sel").unsqueeze(3).to_broadcast((P, TT, 4, 8)), ALU.mult))
            link(V.tensor_reduce(R("es"), R("eg").rearrange("p t g e -> p t e g"), axis=AX.X, op=ALU.add))
            for t in range(TT):
                link(V.max(R("em")[:, t, :], R("es")[:, t, :]))
                link(V.max_index(R("ei")[:, t, :], R("em")[:, t, :], R("es")[:, t, :]))
            V.tensor_tensor(R("d2"), R("em")[:, :, 1:2], R("em")[:, :, 0:1], ALU.subtract).then_inc(e_max, 1)
            link(V.tensor_copy(R("ef"), R("ei")[:, :, 0:2]))
            link(V.scalar_tensor_tensor(out=R("ex"), in0=R("gf").to_broadcast((P, TT, 2)), scalar=float(PER_GROUP), in1=R("ef"), op0=ALU.mult, op1=ALU.add))
            link(V.tensor_tensor(R("oh"), cst[:, C_IOTA:C_IOTA + NE].unsqueeze(1).unsqueeze(1).to_broadcast((P, TT, 2, NE)),
                                 R("ex").unsqueeze(3).to_broadcast((P, TT, 2, NE)), ALU.is_equal))
            V.tensor_tensor(R("M"), R("oh")[:, :, 0, :], R("oh")[:, :, 1, :], ALU.add).then_inc(m_sb, 1)
            dve.wait_ge(r_exp2, 1)
            link(V.tensor_scalar_add(R("w")[:, :, 0:1], R("e2"), 1.0))
            link(V.tensor_tensor(R("w")[:, :, 0:1], R("w")[:, :, 0:1], R("gs"), ALU.mult))
            link(V.reciprocal(R("w")[:, :, 0:1], R("w")[:, :, 0:1]))
            link(V.tensor_tensor(R("w")[:, :, 1:2], R("w")[:, :, 0:1], R("e2"), ALU.mult))
            dve.wait_ge(rank_ps, 1)
            rk = bank(1, 4, NE)
            link(V.tensor_copy(R("cnt"), rk[:, 2, :]))
            link(V.tensor_tensor(R("cmp"), R("cnt").unsqueeze(2).to_broadcast((P, NE, 8)),
                                 cst[:, C_THR:C_THR + 8].unsqueeze(1).to_broadcast((P, NE, 8)), ALU.is_gt))
            link(V.tensor_reduce(R("nt"), R("cmp"), axis=AX.X, op=ALU.add))
            link(V.tensor_scalar(R("nt"), R("nt"), 1.0, None, ALU.max))
            link(V.memset(R("zero"), 0.0))
            link(V.tensor_tensor_scan(R("cum"), R("nt"), R("zero"), 0.0, ALU.add, ALU.add))
            link(V.memset(cums[0:1, 0:1], 0))
            link(V.tensor_copy(cums[0:1, 1:NE + 1], R("cum")[0:1, :]))
            link(V.tensor_tensor(R("base"), R("cum"), R("nt"), ALU.subtract))
            link(V.scalar_tensor_tensor(out=R("pos"), in0=R("base").unsqueeze(1).to_broadcast((P, TT, NE)), scalar=float(ROWS), in1=rk[:, 0:TT, :],
                                        op0=ALU.mult, op1=ALU.add))
            link(V.tensor_tensor(R("oh"), R("oh"), R("pos").unsqueeze(2).to_broadcast((P, TT, 2, NE)), ALU.mult))
            link(V.tensor_reduce(rel[:, :, :], R("oh"), axis=AX.X, op=ALU.add))
            link(V.tensor_copy(slots[:, :], rel[:, :, :].rearrange("p t j -> p (t j)")))
            V.tensor_copy(gates[:, :, :], R("w")).then_inc(route_sb, 1)
            dve.wait_ge(route_sb, 1)

            total = dve.value_load(cums[0:1, NE:NE + 1], min_val=NE, max_val=MAX_TILES)
            iota = cst[:, C_IOTA:C_IOTA + ROWS].unsqueeze(1).to_broadcast((P, 2 * TT, ROWS))
            rel4 = rel[:, :, :].rearrange("p t j -> p (t j)").unsqueeze(2).to_broadcast((P, 2 * TT, ROWS))

            def picks():
                return V.tensor_tensor(hit, iota, rel4, ALU.is_equal)

            def both():
                return V.tensor_tensor(pick, hit[:, 0::2, :], hit[:, 1::2, :], ALU.add)

            def normed():
                return V.tensor_tensor(pick, pick, st[:, 62:64].unsqueeze(2).to_broadcast((P, TT, ROWS)), ALU.mult)

            def by_column(m):
                return mod[:, m, :].rearrange("p (g j) -> p j g", g=4).unsqueeze(3).to_broadcast((P, 4, 4, ROWS))

            xe4 = xe.rearrange("p (g j) r -> p j g r", g=4)
            xe_ps4 = bank(4, 4, P).rearrange("p j (g r) -> p j g r", g=4)

            link(picks())
            link(both())
            normed().then_inc(pick_sb, 1)
            take_mod(5)
            dve.wait_ge(rows_ps, 1)
            V.tensor_copy(xp, bank(0)).then_inc(rows_sb, 1)
            dve.wait_ge(xe_ps, 1)
            V.tensor_tensor(xe4, xe_ps4, by_column(4), ALU.mult).then_inc(xe_t, 1)
            dve.wait_ge(xe_t, 1)
            V.tensor_tensor(xe4, xe4, by_column(3), ALU.add).then_inc(xe_sb, 1)
            with dve.Fori(0, total) as t:
                V.tensor_scalar_add(rel[:, :, :], rel[:, :, :], -float(ROWS)).then_inc(pick_c, 1)
                dve.wait_ge(pick_c, 3 * t + 1)
                picks().then_inc(pick_c, 1)
                dve.wait_ge(pick_c, 3 * t + 2)
                both().then_inc(pick_c, 1)
                dve.wait_ge(pick_c, 3 * t + 3)
                normed().then_inc(pick_sb, 1)
                dve.wait_ge(rows_ps, t + 2)
                V.tensor_copy(xp, bank(0)).then_inc(rows_sb, 1)
                dve.wait_ge(h_exp, t + 1)
                hp = bank(2, 2, P)
                V.tensor_scalar_add(eh, eh, 1.0).then_inc(h_t, 1)
                dve.wait_ge(h_t, 3 * t + 1)
                V.reciprocal(eh, eh).then_inc(h_t, 1)
                dve.wait_ge(h_t, 3 * t + 2)
                V.tensor_tensor(eh, hp[:, :, 0:64], eh, ALU.mult).then_inc(h_t, 1)
                dve.wait_ge(h_t, 3 * t + 3)
                V.tensor_tensor(hid, hp[:, :, 64:128], eh, ALU.mult).then_inc(hid_sb, 1)
                dve.wait_ge(xe_ps, t + 2)
                V.tensor_tensor(xe4, xe_ps4, by_column(4), ALU.mult).then_inc(xe_t, 1)
                dve.wait_ge(xe_t, t + 2)
                V.tensor_tensor(xe4, xe4, by_column(3), ALU.add).then_inc(xe_sb, 1)

            def summed(t):
                ga, gb = fin_rows(2 * t), fin_rows(2 * t + 1)
                dve.wait_ge(fin_gate, t + 1)
                dve.wait_ge(fin_rows_in[2 * t + 1], 16)
                V.scalar_tensor_tensor(out=ga, in0=gb, scalar=gates[:, t, 1:2], in1=ga, op0=ALU.mult, op1=ALU.add).then_inc(fin_sum, 1)
                dve.wait_ge(fin_sum, t + 1)

            def gained(t):
                dve.wait_ge(g2_in, 16)
                link(V.tensor_tensor(fin_rows(2 * t + 1), fin_rows(2 * t), g2b, ALU.mult))

            def residual(t):
                dve.wait_ge(fin_rs, t + 1)
                V.scalar_tensor_tensor(out=resid[:, t, :], in0=fin_rows(2 * t + 1), scalar=st[:, 70 + t:71 + t], in1=resid[:, t, :], op0=ALU.mult, op1=ALU.add).then_inc(fin_sb, 1)

            summed(0)
            gained(0)
            summed(1)
            residual(0)
            gained(1)
            residual(1)

        @block.scalar
        def _(act):
            n_c = [0]

            def link(ins):
                ins.then_inc(act_c, 1)
                n_c[0] += 1
                act.wait_ge(act_c, n_c[0])

            A = nc.scalar.activation
            act.dma_start(cc[:, 0, :], vec(a["c"])).then_inc(c_in, 16)
            act.dma_start(cst[:, :], a["cst"][:, 0:C_KEEP]).then_inc(const_in, 16)
            act.dma_start(bkt, a["cst"][0:N_BUCKETS, C_BKT:C_ALL]).then_inc(const_in, 16)
            for t in range(TT):
                act.dma_start(resid[:, t, :], x_d[:, t, :]).then_inc(x_in, 16)
            act.wait_ge(c_in, 16)
            A(cc[:, 1, :], cc[:, 0, :], ACT.Exp, scale=-1.0).then_inc(c_exp, 1)
            act.wait_ge(x_in, 32)
            for t in range(TT):
                A(junk1, resid[:, t, :], ACT.Square, accum_out=st[:, t:t + 1]).then_inc(xsq, 1)
                act.wait_ge(xsq, t + 1)
            act.wait_ge(lam_sum, 1)
            A(lamv[:, 2:4], lamv[:, 0:2], ACT.Exp).then_inc(lam_exp, 1)
            for t in range(TT):
                for j in range(4):
                    act.wait_ge(xT_ps, 4 * t + j + 1)
                    A(hT[:, 4 * j:4 * j + 4, P * t:P * t + P], bank(j, 4, P), ACT.Copy).then_inc(xT_sb, 1)
            act.dma_start(walpha, a["w_alpha"][0]).then_inc(late_in, 16)
            act.dma_start(balpha, row_bcast(a["b_alpha"], 512)).then_inc(late_in, 16)

            def squares(t):
                act.wait_ge(x1_sb, t + 1)
                A(acc[:, :] if t else s4[:, D:2 * D], resid[:, t, :], ACT.Square, accum_out=st[:, 60 + t:61 + t]).then_inc(x1_sq, 1)
                act.wait_ge(x1_sq, t + 1)

            fill = 0
            for item in SCHED:
                kind = item[0]
                if kind == "alpha":
                    if item[1] == 0:
                        act.wait_ge(zb_ps, 1)
                        A(zbT[:, :], bank(5)[0:GATE_RANK, 0:S], ACT.Copy).then_inc(zb_sb, 1)
                    elif item[1] == 1:
                        for t in range(TT):
                            act.wait_ge(z_abs, t + 1)
                            link(A(tmp[:, 512 * t:512 * t + 512], tmp[:, 512 * t:512 * t + 512], ACT.Exp, scale=-1.0))
                            A(tmp[:, 512 * t:512 * t + 512], tmp[:, 512 * t:512 * t + 512], ACT.Ln, bias=ones[:, 0:1]).then_inc(z_ln, 1)
                    else:
                        for t in range(TT):
                            act.wait_ge(suf_ps, t + 1)
                            A(kdec[:, t, :], bank(4 + t), ACT.Exp, scale=1.0 / GATE_TAU).then_inc(suf_exp, 1)
                        act.wait_ge(suf_ps, 3)
                        A(st[:, 32:48], bank(7)[:, 0:16], ACT.Exp, scale=1.0 / GATE_TAU).then_inc(suf_exp, 1)
                elif kind == "modulate":
                    act.wait_ge(scale_sb, 1)
                    act.wait_ge(xT_sb, 8)
                    for k in range(1, KD, 2):
                        A(hT[:, k, :], hT[:, k, :], ACT.Identity, scale=mod[:, 1, k:k + 1], bias=mod[:, 0, k:k + 1]).then_inc(hT_act, 1)
                    act.wait_ge(relrow_sb, 1)
                    rr = bass.AP(tensor=relrow.tensor, offset=relrow.offset, ap=[relrow.ap[0], [0, P], [1, SKEW]])
                    act.dma_start(skew[:, :, :], rr).then_inc(skew_out, 16)
                    act.wait_ge(skew_out, 16)
                    act.dma_start(bias, bass.AP(tensor=skew[:, :, :].tensor, offset=P - 1, ap=[[SKEW - 1, P], [P * SKEW, A_HEADS], [1, S]])).then_inc(bias_in, 16)
                elif kind == "proj":
                    _, i, half, part = item
                    if part == 0:
                        continue
                    c = ORDER[i]
                    act.wait_ge(proj_ps, fill + 1)
                    src = bank(fill % 2)
                    if c in TRANSPOSED:
                        dst = {0: (qaT, 0), 1: (qaT, 4), 2: (kaT, 0), 3: (kaT, 4), 6: (qbT, 0)}[c]
                        dst = dst[0][:, dst[1] + 2 * half:dst[1] + 2 * half + 2, :]
                        src = bank(fill % 2, 2, S)
                        scale = B_DK ** -0.5 if c == 6 else 1.0
                    else:
                        dst = {4: (va, 0), 5: (va, 512), 7: (kb, 0), 8: (vb, 0), 9: (vb, 512), 10: (rb, 0), 11: (rb, 512)}[c]
                        dst = dst[0][:, half, dst[1]:dst[1] + 512]
                        scale = 1.0
                    A(dst, src, ACT.Copy, scale=scale).then_inc(proj_sb, 1)
                    fill += 1
                elif kind == "att":
                    i = item[1]
                    if 1 <= i < ATT + 1:
                        j = i - 1
                        _, b = head_block(j)
                        act.wait_ge(pdT_ps, j + 1)
                        A(pdT[:, 0:P * (b + 1)], bank(7)[:, 0:P * (b + 1)], ACT.Copy).then_inc(pdT_sb, 1)
                    if i < ATT:
                        _, b = head_block(i)
                        nk = P * (b + 1)
                        act.wait_ge(p_max, i + 1)
                        if i:
                            act.wait_ge(pd_sb, i)
                        for m in range(2):
                            ins = A(pr[:, m, 0:nk], sc[:, m, 0:nk], ACT.Exp, bias=st[:, 8 + m:9 + m], accum_out=st[:, 10 + m:11 + m])
                        ins.then_inc(p_exp, 1)
                    if i % 4 == 1 and i >= 5:
                        g = (i - 5) // 4
                        act.wait_ge(o_ps, 4 * g + 4)
                        for j in range(4):
                            ins = A(tmp[:, 0:A_DV], bank(4, 4, A_DV)[:, j, :], ACT.Square, accum_out=st[:, 16 + j:17 + j])
                            if j < 3:
                                link(ins)
                        ins.then_inc(o_sq, 1)
                        act.wait_ge(o_sq, g + 1)
                elif kind == "silu":
                    _, t, c = item
                    act.wait_ge(proj_sb, 20 + 2 * c + t + 1)
                    act.wait_ge(la_sb, 2)
                    if c:
                        act.wait_ge(rb_sb, t + 1)
                    A(tmp[:, 512 * t:512 * t + 512], rb[:, t, 512 * c:512 * c + 512], ACT.Exp, scale=-1.0).then_inc(rb_exp, 1)
                elif kind == "gsq":
                    t = item[1]
                    act.wait_ge(gla_ps, 2 * t + 2)
                    act.wait_ge(oT_sb, 4)
                    for h in range(B_HEADS):
                        ins = A(s4[:, 6144 + B_DV * (4 * t + h):6144 + B_DV * (4 * t + h + 1)], bank(2 + 2 * t + h // 2, 2, B_DV)[:, h % 2, :], ACT.Square,
                                accum_out=st[:, GSQ[t] + h:GSQ[t] + h + 1])
                    ins.then_inc(gla_sq, 1)
                elif kind == "glaT":
                    t = item[1]
                    for j in range(2):
                        act.wait_ge(glaT_ps, 2 * t + j + 1)
                        for r in range(2):
                            ins = A(oTb[:, 4 * j + r:4 * j + 4:2, P * t:P * t + P], bank(6 + j, 4, P)[:, r::2, :], ACT.Copy, scale=gnb[:, r:r + 1])
                        ins.then_inc(glaT_sb, 1)
                elif kind == "wout":
                    _, u, t = item
                    if (u, t) == (3, 1):
                        squares(0)
                    act.wait_ge(proj_ps, fill + 1)
                    A(y[:, t, 512 * u:512 * u + 512], bank(fill % 2), ACT.Square, accum_out=st[:, 48 + 4 * t + u:49 + 4 * t + u]).then_inc(y_sum, 1)
                    act.wait_ge(y_sum, 2 * u + t + 1)
                    A(y[:, t, 512 * u:512 * u + 512], bank(fill % 2), ACT.Copy).then_inc(proj_sb, 1)
                    fill += 1
                    if (u, t) == (0, 1):
                        act.dma_start(resid[:, :, :], x_d).then_inc(xre_in, 16)
                        act.wait_ge(g1_out, 16)
                        act.wait_ge(mod_sb, 5)
                        act.dma_start(g1b, row_bcast(gdram[0, :, :], D)).then_inc(g1_in, 16)

            for t in range(TT):
                for j in (range(4) if t == 0 else (1, 3)):
                    act.wait_ge(x1T_ps, 4 * t + j + 1)
                    A(x1T[:, 4 * j:4 * j + 4, P * t:P * t + P], bank(X1T_BANK[t][j], 4, P), ACT.Copy).then_inc(x1T_act, 1)
                if t == 0:
                    squares(1)
            act.wait_ge(g_max, 1)
            for t in range(TT):
                link(A(R("ge")[:, t, :], R("L")[:, t, 0:4], ACT.Exp, bias=R("ng")[:, t, :], accum_out=R("gs")[:, t, :]))
            act.wait_ge(e_max, 1)
            A(R("e2"), R("d2"), ACT.Exp).then_inc(r_exp2, 1)

            act.wait_ge(route_sb, 1)
            total = act.value_load(cums[0:1, NE:NE + 1], min_val=NE, max_val=MAX_TILES)

            act.wait_ge(ye_out, 64)
            def tile(t):
                act.wait_ge(ab_ps, t + 1)
                A(ab, bank(1)[:, 0:256], ACT.Copy).then_inc(ab_sb, 1)
                act.wait_ge(h_ps, t + 1)
                A(eh, bank(2, 2, P)[:, :, 0:64], ACT.Exp, scale=-1.0).then_inc(h_exp, 1)
                act.wait_ge(ye_ps, t + 1)
                act.wait_ge(yo_sb, t + 1)
                A(ye, bank(3), ACT.Copy).then_inc(ye_sb, 1)

            with act.Fori(0, total - 1) as t:
                tile(t)
            tile(total - 1)
            act.wait_ge(ye_sb, total + 1)
            act.nop(nofuse=True)
            for g in range(4):
                act.dma_start(ys[bass.ds((total - 1) * ROWS, ROWS), 512 * g:512 * g + 512], ye[32 * g:32 * g + 32, :]).then_inc(last_out, 16)

            def gate(t):
                act.wait_ge(fin_rows_in[2 * t], 16)
                A(fin_rows(2 * t), fin_rows(2 * t), ACT.Copy, scale=gates[:, t, 0:1]).then_inc(fin_gate, 1)

            gate(0)
            gate(1)
            for t in range(TT):
                act.wait_ge(fin_sum, t + 1)
                A(stream[:, 2, D * t:D * t + D], fin_rows(2 * t), ACT.Square, accum_out=st[:, 66 + t:67 + t]).then_inc(fin_sq, 1)
            for t in range(TT):
                act.wait_ge(fin_sb, t + 1)
                act.dma_start(out_d[:, t, :], resid[:, t, :]).then_inc(fin_out, 16)
            act.wait_ge(fin_out, 32)

        @block.gpsimd
        def _(pool):
            n_c = [0]

            def rms(src, dst, width):
                n = src.shape[1]
                nc.gpsimd.tensor_scalar(dst, src, 1.0 / width, EPS, ALU.mult, ALU.add).then_inc(pool_c, 1)
                n_c[0] += 1
                pool.wait_ge(pool_c, n_c[0])
                return nc.gpsimd.tensor_tensor(dst, dst, cst[:, C_NH:C_NH + n], ALU.pow)

            for dst, src in params:
                pool.dma_start(dst, src).then_inc(par_in, 16)
            pool.wait_ge(const_in, 32)
            for t in range(TT):
                pool.wait_ge(xsq, t + 1)
                rms(st[:, t:t + 1], st[:, 2 + t:3 + t], D).then_inc(xr, 1)
            pool.wait_ge(bias_in, 16)
            pool.memset(bias[0:CHUNK, :, S - CHUNK:S], NEG).then_inc(masked, 1)
            for item in SCHED:
                kind = item[0]
                if kind == "mod" and item[1] == 2:
                    pool.wait_ge(g_sb, 1)
                    pool.dma_start(gdram[0, :, :], mod[:, 2, :]).then_inc(g1_out, 16)
                elif kind == "att" and item[1] % 4 == 1 and item[1] >= 5:
                    g = (item[1] - 5) // 4
                    pool.wait_ge(o_sq, g + 1)
                    if g:
                        pool.wait_ge(o_sb, g)
                    rms(st[:, 16:20], st[:, 20:24], A_DV).then_inc(o_rs, 1)
                elif kind == "gsq":
                    t = item[1]
                    pool.wait_ge(gla_sq, t + 1)
                    rms(st[:, GSQ[t]:GSQ[t] + 4], st[:, GSQ[t] + 4:GSQ[t] + 8], B_DV).then_inc(gla_rs, 1)
            pool.wait_ge(oT_sb, 4)
            pool.memset(ye, 0.0).then_inc(ye_sb, 1)
            pool.wait_ge(ye_sb, 1)
            spare = ys[NE * ROWS:MAX_TILES * ROWS, :].rearrange("(p r) (g n) -> p (r g) n", p=P, g=4)
            part = spare.shape[1] // 4
            for j in range(4):
                pool.dma_start(spare[:, part * j:part * (j + 1), :], ye.unsqueeze(1).to_broadcast((P, part, 512))).then_inc(ye_out, 16)
            for t in range(TT):
                pool.wait_ge(y_tot, t + 1)
                rms(st[:, 56 + t:57 + t], st[:, 58 + t:59 + t], D).then_inc(y_rs, 1)
                pool.wait_ge(x1_sq, t + 1)
                rms(st[:, 60 + t:61 + t], st[:, 62 + t:63 + t], D).then_inc(x1_rs, 1)
            pool.wait_ge(g_sb, 2)
            pool.dma_start(gdram[1, :, :], mod[:, 5, :]).then_inc(g2_out, 16)
            pool.wait_ge(route_sb, 1)
            total = pool.value_load(cums[0:1, NE:NE + 1], min_val=NE, max_val=MAX_TILES)

            def outputs(t):
                pool.wait_ge(ye_sb, t + 2)
                pool.wait_ge(ye_out, 64 * (t + 1))
                pool.nop(nofuse=True)
                nc.gpsimd.tensor_copy(yo, ye).then_inc(yo_sb, 1)
                pool.wait_ge(yo_sb, t + 2)
                pool.nop(nofuse=True)
                for g in range(4):
                    pool.dma_start(ys[bass.ds(t * ROWS, ROWS), 512 * g:512 * g + 512], yo[32 * g:32 * g + 32, :]).then_inc(ye_out, 16)

            pool.wait_ge(mod_ps, 6)
            nc.gpsimd.memset(yo, 0.0).then_inc(yo_sb, 1)
            pool.wait_ge(yo_sb, 1)
            with pool.Fori(0, total - 1) as t:
                outputs(t)
            pool.wait_ge(ye_out, 64 * total)
            pool.wait_ge(last_out, 64)
            pool.nop(nofuse=True)
            for j in range(2 * TT):
                pool.indirect_dma_start(fin_rows(j), None, ys[:, :], bass.IndirectOffsetOnAxis(ap=slots[:, j:j + 1], axis=0)).then_inc(fin_rows_in[j], 16)
            for t in range(TT):
                pool.wait_ge(fin_sq, t + 1)
                rms(st[:, 66 + t:67 + t], st[:, 70 + t:71 + t], D).then_inc(fin_rs, 1)


NAMES = ["x", "c", "rel_bias", "w_ada", "b_ada", "g_pre_mix", "g_post_mix", "w_in", "w_alpha", "b_alpha", "lam_q1", "lam_k1",
         "lam_q2", "lam_k2", "g_sub_a", "g_norm_b", "w_out", "g_pre_ffn", "g_post_ffn", "w_router_g", "b_router_g",
         "w_router_e", "b_router_e", "w1", "w3", "w2"]


def kernel(**inputs):
    import concourse.bacc as bacc
    from concourse.bass_utils import run_bass_kernel_spmd

    nc = bacc.Bacc("TRN2", target_bir_lowering=False, num_devices=1)
    arrays = {f"in_{n}": np.ascontiguousarray(inputs[n]) for n in NAMES}
    arrays["in_cst"] = shape_constants()
    aps = {n[3:]: nc.dram_tensor(n, v.shape, mybir.dt.from_np(v.dtype), kind="ExternalInput").ap() for n, v in arrays.items()}
    out = nc.dram_tensor("out", (1, S, D), mybir.dt.float32, kind="ExternalOutput").ap()
    build(nc, aps, out)
    return run_bass_kernel_spmd(nc, [arrays], core_ids=[0]).results[0]["out"]
```
